# Optimizing a Trainium2 kernel written in Bass

```python
import math
import jax, jax.numpy as jnp
from jax import lax
import numpy as np

D_MODEL = 1024
BATCH = 1
SEQ = 512
DEPTH = 1

CHUNK = 64
Q_BLOCK = 128
PLE_DIM = 256
D_MIX = D_MODEL
D_ATTN = D_MIX // 2
D_CONV = D_MIX - D_ATTN
N_HEADS_A = 4
HEAD_DIM_V = D_ATTN // N_HEADS_A
HEAD_DIM_QK = HEAD_DIM_V // 2
CONV_WIDTH = 3
N_IN_PARTS = 8
D_IN = 4 * D_ATTN + 4 * D_CONV
EPS = 1e-6
SUBLN_EPS = 1e-5


def rms_norm(x, gain, eps=EPS):
    xf = x.astype(jnp.float32)
    y = xf * lax.rsqrt(jnp.mean(xf * xf, axis=-1, keepdims=True) + eps)
    return (y * gain.astype(jnp.float32)).astype(x.dtype)

def alibi_slopes(n_heads):
    return jnp.exp2(-8.0 * jnp.arange(1, n_heads + 1, dtype=jnp.float32) / n_heads)

def diff_attention(q, k, v, lam, slopes):
    seq = q.shape[1]
    scale = HEAD_DIM_QK ** -0.5
    outs = []
    for q0 in range(0, seq, Q_BLOCK):
        k_end = q0 + Q_BLOCK
        t = jnp.arange(q0, k_end)
        s = jnp.arange(k_end)
        scores = jnp.einsum('bqhmd,bkhmd->bhmqk', q[:, q0:k_end], k[:, :k_end]).astype(jnp.float32) * scale
        dist = jnp.abs(t[:, None] - s[None, :]).astype(jnp.float32)
        allowed = (s[None, :] // CHUNK) <= (t[:, None] // CHUNK)
        bias = jnp.where(allowed[None], -slopes[:, None, None] * dist[None], -jnp.inf)
        probs = jax.nn.softmax(scores + bias[None, :, None], axis=-1)
        weights = probs[:, :, 0] - lam * probs[:, :, 1]
        outs.append(jnp.einsum('bhqk,bkhd->bqhd', weights.astype(v.dtype), v[:, :k_end]))
    return jnp.concatenate(outs, axis=1)

def first_inputs(seed: int = 0) -> dict:
    key = jax.random.key(seed)
    ks = jax.random.split(key, 16)
    f32 = jnp.float32
    x = jax.random.normal(ks[0], (BATCH, SEQ, D_MODEL), f32)
    p = jax.random.normal(ks[1], (DEPTH, BATCH, SEQ, PLE_DIM), f32)
    pre_norm_gain = 1.0 + 0.02 * jax.random.normal(ks[2], (DEPTH, D_MODEL), f32)
    w_in = jax.random.normal(ks[3], (DEPTH, D_MODEL, D_IN), f32) * D_MODEL ** -0.5
    lambda_q1 = 0.1 * jax.random.normal(ks[4], (DEPTH, HEAD_DIM_QK), f32)
    lambda_k1 = 0.1 * jax.random.normal(ks[5], (DEPTH, HEAD_DIM_QK), f32)
    lambda_q2 = 0.1 * jax.random.normal(ks[6], (DEPTH, HEAD_DIM_QK), f32)
    lambda_k2 = 0.1 * jax.random.normal(ks[7], (DEPTH, HEAD_DIM_QK), f32)
    subln_gain = 1.0 + 0.02 * jax.random.normal(ks[8], (DEPTH, HEAD_DIM_V), f32)
    conv_w = jax.random.normal(ks[9], (DEPTH, CONV_WIDTH, D_CONV), f32) * CONV_WIDTH ** -0.5
    w_out = jax.random.normal(ks[10], (DEPTH, D_MIX, D_MODEL), f32) * D_MIX ** -0.5
    post_norm_gain = 1.0 + 0.02 * jax.random.normal(ks[11], (DEPTH, D_MODEL), f32)
    w_ple_proj = jax.random.normal(ks[12], (DEPTH, PLE_DIM, D_MODEL), f32) * PLE_DIM ** -0.5
    ple_norm_gain = 1.0 + 0.02 * jax.random.normal(ks[13], (DEPTH, D_MODEL), f32)
    w_ple_gate = jax.random.normal(ks[14], (DEPTH, D_MODEL, D_MODEL), f32) * D_MODEL ** -0.5
    return {"x": x, "p": p, "pre_norm_gain": pre_norm_gain, "w_in": w_in,
            "lambda_q1": lambda_q1, "lambda_k1": lambda_k1, "lambda_q2": lambda_q2,
            "lambda_k2": lambda_k2, "subln_gain": subln_gain, "conv_w": conv_w,
            "w_out": w_out, "post_norm_gain": post_norm_gain, "w_ple_proj": w_ple_proj,
            "ple_norm_gain": ple_norm_gain, "w_ple_gate": w_ple_gate}

def first_block(x, p, pre_norm_gain, w_in, lambda_q1, lambda_k1, lambda_q2, lambda_k2,
              subln_gain, conv_w, w_out, post_norm_gain, w_ple_proj, ple_norm_gain, w_ple_gate):
    bsz, seq, _ = x.shape
    slopes = alibi_slopes(N_HEADS_A)
    for i in range(DEPTH):
        lambda_init = 0.8 - 0.6 * math.exp(-0.3 * i)
        h = rms_norm(x, pre_norm_gain[i])
        proj = h @ w_in[i]
        q, k, v, z_a, b_gate, c_gate, u, z_c = jnp.split(proj, N_IN_PARTS, axis=-1)

        q = q.reshape(bsz, seq, N_HEADS_A, 2, HEAD_DIM_QK)
        k = k.reshape(bsz, seq, N_HEADS_A, 2, HEAD_DIM_QK)
        v = v.reshape(bsz, seq, N_HEADS_A, HEAD_DIM_V)
        lam = (jnp.exp(jnp.sum((lambda_q1[i] * lambda_k1[i]).astype(jnp.float32)))
               - jnp.exp(jnp.sum((lambda_q2[i] * lambda_k2[i]).astype(jnp.float32)))
               + lambda_init)
        attn = diff_attention(q, k, v, lam, slopes)
        attn = rms_norm(attn, subln_gain[i], SUBLN_EPS) * (1.0 - lambda_init)
        attn = attn.reshape(bsz, seq, D_ATTN) * jax.nn.silu(z_a)

        g = c_gate * u
        g_pad = jnp.pad(g, ((0, 0), (CONV_WIDTH - 1, 0), (0, 0)))
        conv = conv_w[i, 0] * g_pad[:, 0:seq]
        for j in range(1, CONV_WIDTH):
            conv = conv + conv_w[i, j] * g_pad[:, j:j + seq]
        conv_out = b_gate * conv * jax.nn.silu(z_c)

        mixed = jnp.concatenate([attn, conv_out], axis=-1) @ w_out[i]
        x = x + rms_norm(mixed, post_norm_gain[i])

        e = rms_norm(p[i] @ w_ple_proj[i], ple_norm_gain[i])
        x = x + jax.nn.sigmoid(x @ w_ple_gate[i]) * e
    return x


DEPTH_2 = 2

N_A_LAYERS = DEPTH_2 // 2
N_B_LAYERS = DEPTH_2 - N_A_LAYERS

CHUNK_2 = 128
A_WIDTH = 2 * D_MODEL
A_GROUPS = 8
A_GROUP_CH = A_WIDTH // A_GROUPS

HEAD_DIM = 64
N_Q_HEADS = D_MODEL // HEAD_DIM
N_KV_HEADS = 4
Q_PER_KV = N_Q_HEADS // N_KV_HEADS
B_WIDTH = N_Q_HEADS * HEAD_DIM
KV_WIDTH = N_KV_HEADS * HEAD_DIM
WINDOW = 128
BLOCK = 128


def rms_norm_2(x, g):
    xf = x.astype(jnp.float32)
    y = xf * lax.rsqrt(jnp.mean(xf * xf, axis=-1, keepdims=True) + EPS)
    return (y * g.astype(jnp.float32)).astype(x.dtype)

def layer_norm(x, g, b):
    xf = x.astype(jnp.float32)
    mu = jnp.mean(xf, axis=-1, keepdims=True)
    var = jnp.mean(jnp.square(xf - mu), axis=-1, keepdims=True)
    y = (xf - mu) * lax.rsqrt(var + EPS)
    return (y * g.astype(jnp.float32) + b.astype(jnp.float32)).astype(x.dtype)

def alibi_slopes_2(n_heads):
    return jnp.asarray(np.array([2.0 ** (-8.0 * (h + 1) / n_heads) for h in range(n_heads)], dtype=np.float32))

def gmlp_mixer(h, w_in, ln_g, ln_b, w_s, b_s, w_out):
    bsz, s_len, _ = h.shape
    u, v, z = jnp.split(h @ w_in, 3, axis=-1)
    u = jax.nn.gelu(u)
    v = layer_norm(jax.nn.gelu(v), ln_g, ln_b)
    n_chunks = s_len // CHUNK_2
    v = v.reshape(bsz, n_chunks, CHUNK_2, A_GROUPS, A_GROUP_CH)
    causal = jnp.tril(jnp.ones((CHUNK_2, CHUNK_2), dtype=bool))
    w_causal = jnp.where(causal[None], w_s, 0.0).astype(v.dtype)
    s = jnp.einsum('gts,bnsgc->bntgc', w_causal, v) + b_s.T[:, :, None].astype(v.dtype)
    s = s.reshape(bsz, s_len, A_WIDTH)
    y = u * s * jax.nn.silu(z)
    return y @ w_out

def swa_mixer(h, k, v, w_in, sinks, w_out):
    bsz, s_len, _ = h.shape
    q, z = jnp.split(h @ w_in, 2, axis=-1)
    q = q * (HEAD_DIM ** -0.5)
    n_blocks = s_len // BLOCK
    q_blocks = q.reshape(bsz, n_blocks, BLOCK, N_KV_HEADS, Q_PER_KV, HEAD_DIM).transpose(1, 0, 2, 3, 4, 5)
    pad = jnp.zeros((bsz, BLOCK, N_KV_HEADS, HEAD_DIM), k.dtype)
    k_pad = jnp.concatenate([pad, k], axis=1)
    v_pad = jnp.concatenate([pad, v], axis=1)

    r = jnp.arange(BLOCK)[:, None]
    c = jnp.arange(2 * BLOCK)[None, :]
    dist = BLOCK + r - c
    in_window = (dist >= 0) & (dist < WINDOW)
    slopes = alibi_slopes_2(N_Q_HEADS).reshape(N_KV_HEADS, Q_PER_KV)
    alibi = -slopes[:, :, None, None] * dist.astype(jnp.float32)
    sink = sinks.astype(jnp.float32).reshape(N_KV_HEADS, Q_PER_KV)[None, :, :, None]

    def block_fn(args):
        i, qb = args
        start = i * BLOCK
        kb = lax.dynamic_slice_in_dim(k_pad, start, 2 * BLOCK, axis=1)
        vb = lax.dynamic_slice_in_dim(v_pad, start, 2 * BLOCK, axis=1)
        logits = jnp.einsum('btkgd,bskd->bkgts', qb, kb).astype(jnp.float32) + alibi
        valid = in_window & ((start - BLOCK + c) >= 0)
        logits = jnp.where(valid, logits, -jnp.inf)
        m = jnp.maximum(jnp.max(logits, axis=-1), sink)
        p = jnp.exp(logits - m[..., None])
        denom = jnp.sum(p, axis=-1) + jnp.exp(sink - m)
        o = jnp.einsum('bkgts,bskd->btkgd', p.astype(vb.dtype), vb).astype(jnp.float32)
        o = o / denom.transpose(0, 3, 1, 2)[..., None]
        return o.astype(h.dtype)

    out = lax.map(block_fn, (jnp.arange(n_blocks), q_blocks))
    out = out.transpose(1, 0, 2, 3, 4, 5).reshape(bsz, s_len, B_WIDTH)
    y = out * jax.nn.silu(z)
    return y @ w_out

def second_inputs(seed: int = 0) -> dict:
    key = jax.random.key(seed)
    ks = jax.random.split(key, 20)
    f32 = jnp.float32
    nrm = lambda k, shape, scale: jax.random.normal(k, shape, f32) * scale
    x = jax.random.normal(ks[0], (BATCH, SEQ, D_MODEL), f32)
    a_w_in = nrm(ks[1], (N_A_LAYERS, D_MODEL, 3 * A_WIDTH), D_MODEL ** -0.5)
    a_ln_g = 1.0 + nrm(ks[2], (N_A_LAYERS, A_WIDTH), 0.05)
    a_ln_b = nrm(ks[3], (N_A_LAYERS, A_WIDTH), 0.02)
    a_w_s = nrm(ks[4], (N_A_LAYERS, A_GROUPS, CHUNK_2, CHUNK_2), CHUNK_2 ** -0.5)
    a_b_s = 1.0 + nrm(ks[5], (N_A_LAYERS, A_GROUPS, CHUNK_2), 0.1)
    a_w_out = nrm(ks[6], (N_A_LAYERS, A_WIDTH, D_MODEL), A_WIDTH ** -0.5)
    a_pre_g = 1.0 + nrm(ks[7], (N_A_LAYERS, D_MODEL), 0.05)
    a_post_g = 1.0 + nrm(ks[8], (N_A_LAYERS, D_MODEL), 0.05)
    kv_norm_g = 1.0 + nrm(ks[9], (D_MODEL,), 0.05)
    w_k = nrm(ks[10], (D_MODEL, KV_WIDTH), D_MODEL ** -0.5)
    w_v = nrm(ks[11], (D_MODEL, KV_WIDTH), D_MODEL ** -0.5)
    b_w_in = nrm(ks[12], (N_B_LAYERS, D_MODEL, 2 * B_WIDTH), D_MODEL ** -0.5)
    b_sinks = nrm(ks[13], (N_B_LAYERS, N_Q_HEADS), 0.5)
    b_w_out = nrm(ks[14], (N_B_LAYERS, B_WIDTH, D_MODEL), B_WIDTH ** -0.5)
    b_pre_g = 1.0 + nrm(ks[15], (N_B_LAYERS, D_MODEL), 0.05)
    b_post_g = 1.0 + nrm(ks[16], (N_B_LAYERS, D_MODEL), 0.05)
    return {"x": x, "a_w_in": a_w_in, "a_ln_g": a_ln_g, "a_ln_b": a_ln_b, "a_w_s": a_w_s,
            "a_b_s": a_b_s, "a_w_out": a_w_out, "a_pre_g": a_pre_g, "a_post_g": a_post_g,
            "kv_norm_g": kv_norm_g, "w_k": w_k, "w_v": w_v, "b_w_in": b_w_in, "b_sinks": b_sinks,
            "b_w_out": b_w_out, "b_pre_g": b_pre_g, "b_post_g": b_post_g}

def second_block(x, a_w_in, a_ln_g, a_ln_b, a_w_s, a_b_s, a_w_out, a_pre_g, a_post_g,
              kv_norm_g, w_k, w_v, b_w_in, b_sinks, b_w_out, b_pre_g, b_post_g):
    bsz, s_len, _ = x.shape
    h = x
    k_shared = None
    v_shared = None
    for layer in range(DEPTH_2):
        if layer < N_A_LAYERS:
            i = layer
            y = gmlp_mixer(rms_norm_2(h, a_pre_g[i]), a_w_in[i], a_ln_g[i], a_ln_b[i],
                           a_w_s[i], a_b_s[i], a_w_out[i])
            h = h + rms_norm_2(y, a_post_g[i])
            if layer == N_A_LAYERS - 1:
                kv_in = rms_norm_2(h, kv_norm_g)
                k_shared = (kv_in @ w_k).reshape(bsz, s_len, N_KV_HEADS, HEAD_DIM)
                v_shared = (kv_in @ w_v).reshape(bsz, s_len, N_KV_HEADS, HEAD_DIM)
        else:
            j = layer - N_A_LAYERS
            y = swa_mixer(rms_norm_2(h, b_pre_g[j]), k_shared, v_shared,
                          b_w_in[j], b_sinks[j], b_w_out[j])
            h = h + rms_norm_2(y, b_post_g[j])
    return h


def setup_inputs(seed=0):
    out = dict(first_inputs(seed))
    for name, value in second_inputs(seed + 1).items():
        if name != "x":
            out[name + "_2"] = value
    return out


def reference(
    x, p, pre_norm_gain, w_in, lambda_q1, lambda_k1, lambda_q2, lambda_k2, subln_gain, conv_w,
    w_out, post_norm_gain, w_ple_proj, ple_norm_gain, w_ple_gate, a_w_in_2, a_ln_g_2, a_ln_b_2,
    a_w_s_2, a_b_s_2, a_w_out_2, a_pre_g_2, a_post_g_2, kv_norm_g_2, w_k_2, w_v_2, b_w_in_2,
    b_sinks_2, b_w_out_2, b_pre_g_2, b_post_g_2,
):
    x = first_block(
        x, p, pre_norm_gain, w_in, lambda_q1, lambda_k1, lambda_q2, lambda_k2, subln_gain,
        conv_w, w_out, post_norm_gain, w_ple_proj, ple_norm_gain, w_ple_gate,
    )
    return second_block(
        x, a_w_in_2, a_ln_g_2, a_ln_b_2, a_w_s_2, a_b_s_2, a_w_out_2, a_pre_g_2, a_post_g_2,
        kv_norm_g_2, w_k_2, w_v_2, b_w_in_2, b_sinks_2, b_w_out_2, b_pre_g_2, b_post_g_2,
    )


_drawn_inputs = setup_inputs


def setup_inputs(seed=0):
    import zlib

    import numpy as np

    out = dict(_drawn_inputs(seed))
    spreads = {}
    factors = {'lambda_k1': 2.773,
     'lambda_q2': 2.922,
     'subln_gain': 13.305,
     'post_norm_gain': 8.912,
     'ple_norm_gain': 17.183,
     'a_ln_g_2': 17.826,
     'a_ln_b_2': 42.163,
     'a_b_s_2': 4.994,
     'a_pre_g_2': 2.682,
     'a_post_g_2': 4.545,
     'kv_norm_g_2': 3.906,
     'b_sinks_2': 30.096,
     'b_pre_g_2': 4.098,
     'b_post_g_2': 17.644}
    for name, (base, spread) in spreads.items():
        noise = np.random.default_rng([zlib.crc32(name.encode()), seed]).standard_normal(out[name].shape)
        drawn = base * np.exp(spread * noise) if base else spread * noise
        out[name] = __import__('jax').numpy.asarray(drawn.astype(out[name].dtype))
    for name, factor in factors.items():
        out[name] = (out[name] * factor).astype(out[name].dtype)
    return out
```

```python
import math
from contextlib import ExitStack

import concourse.bass as bass
from concourse import mybir

P = 128
S = 512
T = S // P
D = 1024
KD = D // P
HALF = 512
NH1, DV1, DQK1 = 4, 128, 64
LAM_INIT = 0.8 - 0.6 * math.exp(0.0)
AW = 2048
KA = AW // P
NG = 8
NQ, NKV, DH = 16, 4, 64
PLE = 256
EPS, SUBLN_EPS = 1e-6, 1e-5
MASKED = 1e30
SLOPE1 = [2.0 ** (-8.0 * (h + 1) / NH1) for h in range(NH1)]
SLOPE2 = [2.0 ** (-8.0 * (h + 1) / NQ) for h in range(NQ)]
UNIT = 2048
RAW = UNIT // 2


def weight_units():
    u = []
    part = lambda n: n * 512
    for stage, n in (("q", 0), ("k", 1)):
        u += [(stage, j, "F", "w_in", 0, part(n) + 256 * j) for j in range(2)]
    u += [("v", kh, "T", "w_in", 4 * kh, part(2)) for kh in range(2)]
    u += [("za", j, "F", "w_in", 0, part(3) + 256 * j) for j in range(2)]
    for j in range(2):
        for stage, n in (("c", 5), ("u", 6), ("b", 4), ("zc", 7)):
            u += [(stage, j, "F", "w_in", 0, part(n) + 256 * j)]
    u += [("wo", 2 * c + kh, "T", "w_out", 4 * kh, 512 * c) for c in range(2) for kh in range(2)]
    u += [("ple", 0, "P", "w_ple_proj", 0, 0)]
    u += [("gate", 2 * c + kh, "T", "w_ple_gate", 4 * kh, 512 * c) for c in range(2) for kh in range(2)]
    u += [("v4", 2 * c + kh, "T", "a_w_in_2", 4 * kh, AW + 512 * c) for c in range(4) for kh in range(2)]
    for half in range(2):
        for j in range(4 * half, 4 * half + 4):
            u += [("z4", j, "F", "a_w_in_2", 0, 2 * AW + 256 * j), ("u4", j, "F", "a_w_in_2", 0, 256 * j)]
        u += [(f"a{half}", 2 * c + kh, "T", "a_w_out_2", 8 * half + 4 * kh, 512 * c)
              for c in range(2) for kh in range(2)]
    u += [("v5", 0, "F", "w_v_2", 0, 0), ("k5", 0, "F", "w_k_2", 0, 0)]
    u += [("q5", j, "F", "b_w_in_2", 0, 256 * j) for j in range(4)]
    u += [("z5", j, "F", "b_w_in_2", 0, 1024 + 256 * j) for j in range(4)]
    u += [("f", 2 * c + kh, "T", "b_w_out_2", 4 * kh, 512 * c) for c in range(2) for kh in range(2)]
    return u


UNITS = weight_units()
UNIT_NO = {(s, j): n for n, (s, j, *_) in enumerate(UNITS)}

STEPS1 = [(h, qt) for h in range(NH1) for qt in range(T)]
JOBS1 = [("za", f) for f in range(4)]
for _j in range(2):
    for _s in ("c", "u", "b", "zc"):
        JOBS1 += [(_s, 2 * _j), (_s, 2 * _j + 1)]
SLOTS1 = len(JOBS1)
STEPS2 = [(g, b) for g in range(NKV) for b in range(T)]
JOBS2 = {n: ("q5", 2 + n) for n in range(6)}
JOBS2 |= dict(zip((6, 7, 10, 11, 14, 15, 17, 18), [("z5", f) for f in range(8)]))
SLOTS2 = 19


def tensor_order():
    o = [("tr", "x", t, j) for t in range(T) for j in range(2)]
    o += [("F", "q", f) for f in range(4)] + [("F", "k", f) for f in range(4)]
    o += [("T", "v", 0, kh, t) for kh in range(2) for t in range(T)]
    for i in range(SLOTS1):
        if 2 <= i < 18:
            o += [("pv", i - 2)]
        if 1 <= i < 17:
            o += [("tw", i - 1)]
        if i < 16:
            o += [("sc", i, m) for m in range(2)]
        if i == 18:
            o += [("ss", h) for h in range(NH1)]
        o += [("F", *JOBS1[i])]
    o += [("T", "wo", 0, 0, t) for t in range(T)] + [("tr", "p", 0, k) for k in range(2)]
    o += [("T", "wo", 0, 1, t) for t in range(T)]
    o += [("T", "wo", 1, kh, t) for kh in range(2) for t in range(T)]
    for t in range(T):
        o += [("ple", t, c) for c in range(2)]
        if t:
            o += [("tr", "x1", t - 1, j) for j in range(2)]
    o += [("T", "gate", 0, 0, 0)] + [("tr", "x1", 3, j) for j in range(2)]
    o += [("T", "gate", 0, 0, t) for t in range(1, T)] + [("wt", j) for j in range(2)]
    o += [("T", "gate", 0, 1, t) for t in range(2)] + [("rw", j) for j in range(2)]
    o += [("T", "gate", 0, 1, t) for t in range(2, T)]
    o += [("T", "gate", 1, kh, t) for kh in range(2) for t in range(T)]
    for t in range(T):
        o += [("tr", "h", t, j) for j in range(2)] + [("T", "v4", 0, 0, t)]
    o += [("T", "v4", 0, 1, t) for t in range(T)]
    o += [("T", "v4", c, kh, t) for c in range(1, 4) for kh in range(2) for t in range(T)]
    for half in range(2):
        for j in range(4 * half, 4 * half + 4):
            o += [("F", s, 2 * j + f) for s in ("z4", "u4") for f in range(2)]
            o += [("s4", 2 * j + f) for f in range(2)]
        o += [("T", f"a{half}", c, kh, t) for c in range(2) for kh in range(2) for t in range(T)]
    for t in range(T):
        o += [("tr", "n", t, j) for j in range(2)] + [("v5", t)]
    o += [("F", "k5", j) for j in range(2)] + [("F", "q5", f) for f in range(2)]
    for i in range(SLOTS2):
        if 2 <= i < 18:
            o += [("o5", i - 2)]
        if 1 <= i < 17:
            o += [("t5", i - 1, kt) for kt in ((0, 1) if STEPS2[i - 1][1] else (1,))]
        if i < 16:
            o += [("s5", i, m) for m in range(2)]
        if i in JOBS2:
            o += [("F", *JOBS2[i])]
    o += [("T", "f", c, kh, t) for c in range(2) for kh in range(2) for t in range(T)]
    return o


ORDER = tensor_order()
BLOCK = {b: n + 1 for n, b in enumerate(ORDER)}


def bank_of(b):
    kind = b[0]
    if kind == "tr":
        name, t, j = b[1:]
        return {"x": 2 * (t % 4) + j, "p": 4 + j, "x1": t + 4 * j, "h": 4 + (2 * t + j) % 4,
                "n": 4 + (2 * t + j) % 4}[name]
    if kind == "F":
        s, f = b[1:]
        if s in ("z4", "u4"):
            return 4 * (f // 2 % 2) + f % 2 + 2 * (s == "u4")
        if s in ("k5", "q5", "z5"):
            return [x[1:] for x in ORDER if x[0] == "F" and x[1] in ("k5", "q5", "z5")].index((s, f)) % 3
        return [x[1:] for x in ORDER if x[0] == "F"].index((s, f)) % 4
    if kind == "T":
        s, c, _, t = b[1:]
        return t + 4 * (1 if s == "v" else c % 2)
    if kind == "s4":
        return 4 * (b[1] // 2 % 2) + b[1] % 2
    return {"sc": lambda i, m: 4 + m, "tw": lambda i: 6, "pv": lambda i: 7, "ss": lambda h: 4 + h,
            "ple": lambda t, c: t + 4 * c, "wt": lambda j: 4 + j, "rw": lambda j: 6 + j,
            "v5": lambda t: t, "s5": lambda s, m: 4 + m, "t5": lambda s, kt: 6 + kt,
            "o5": lambda s: 3}[kind](*b[1:])


def opens(b):
    if b[0] == "T":
        return b[3] == 0
    if b[0] == "pv":
        return STEPS1[b[1]][1] == 0
    return True


def previous_in_bank():
    last, before = {}, {}
    for b in ORDER:
        bank = bank_of(b)
        if opens(b):
            before[b] = last.get(bank)
        last[bank] = b
    return before


BEFORE = previous_in_bank()


def program(nc, x, p, pre_norm_gain, w_in, lambda_q1, lambda_k1, lambda_q2, lambda_k2, subln_gain,
            conv_w, w_out, post_norm_gain, w_ple_proj, ple_norm_gain, w_ple_gate, a_w_in_2,
            a_ln_g_2, a_ln_b_2, a_w_s_2, a_b_s_2, a_w_out_2, a_pre_g_2, a_post_g_2, kv_norm_g_2,
            w_k_2, w_v_2, b_w_in_2, b_sinks_2, b_w_out_2, b_pre_g_2, b_post_g_2, out):
    f32, f32r = mybir.dt.float32, mybir.dt.float32r
    ALU, ACT, AX = mybir.AluOpType, mybir.ActivationFunctionType, mybir.AxisListType
    MATRICES = {"w_in": w_in[0], "w_out": w_out[0], "w_ple_proj": w_ple_proj[0],
                "w_ple_gate": w_ple_gate[0], "a_w_in_2": a_w_in_2[0], "a_w_out_2": a_w_out_2[0],
                "w_v_2": w_v_2, "w_k_2": w_k_2, "b_w_in_2": b_w_in_2[0], "b_w_out_2": b_w_out_2[0]}
    ctx = ExitStack()
    with ctx:
        sb = lambda name, shape, dt=f32: ctx.enter_context(nc.sbuf_tensor(name, shape, dt))
        sem = lambda name: ctx.enter_context(nc.semaphore(name))

        raw = sb("raw", [P, 4, RAW])
        whi = sb("whi", [P, 2, UNIT], f32r)
        wlo = sb("wlo", [P, 2, UNIT], f32r)
        actA_hi, actA_lo = sb("actA_hi", [P, KD, S], f32r), sb("actA_lo", [P, KD, S], f32r)
        actB_hi, actB_lo = sb("actB_hi", [P, KD, S], f32r), sb("actB_lo", [P, KD, S], f32r)
        resid = sb("resid", [P, T, D])
        big = sb("big", [P, 4, AW])
        gain = sb("gain", [P, 3, D])
        tok = sb("tok", [P, 2, D])
        smA, smB, smC = sb("smA", [P, D]), sb("smB", [P, D]), sb("smC", [P, D])
        gcv = sb("gcv", [P, 2, 2 + S])
        acc = sb("acc", [P, 2, HALF])
        th = sb("th", [P, HALF])
        junk = sb("junk", [P, HALF])
        ident, ones = sb("ident", [P, P]), sb("ones", [P, P])
        lamv, lams = sb("lamv", [P, 4, DQK1]), sb("lams", [P, 8])
        subg, convc = sb("subg", [P, 2]), sb("convc", [P, 3, 4])
        lng, lnb = sb("lng", [P, KA]), sb("lnb", [P, KA])
        kvg, bg = sb("kvg", [P, KD]), sb("bg", [P, KD])
        sinks = sb("sinks", [P, NQ])
        ss = sb("ss", [P, 8, T, 4])
        ms = sb("ms", [P, 8, T])
        rstd = sb("rstd", [P, 8, T])
        mhalf, eps_sub = sb("mhalf", [P, 1]), sb("eps_sub", [P, 1])
        mx, nmx, rs, rr = sb("mx", [P, 4]), sb("nmx", [P, 4]), sb("rs", [P, 4]), sb("rr", [P, 4])
        esk, den = sb("esk", [P, 4]), sb("den", [P, 4])
        vsum, nmu = sb("vsum", [P, T, 4]), sb("nmu", [P, 2, T])
        iot = smC[:, 0:HALF].bitcast(mybir.dt.int32)

        psum = [ctx.enter_context(nc.psum_tensor(f"bank{b}", [P, HALF], f32)) for b in range(8)]

        qT, kT, vtok, zaT = big[:, 0], big[:, 1], big[:, 2], big[:, 3]
        tile = lambda region, n: region[:, n * HALF:(n + 1) * HALF]
        base1 = smB[:, 0:HALF]
        bias1 = lambda h: smA[:, (h % 2) * HALF:(h % 2 + 1) * HALF]
        prob1 = lambda m: tok[:, 0, m * HALF:(m + 1) * HALF]
        wgt1, wgtT1 = tok[:, 1, 0:HALF], tok[:, 1, HALF:D]
        ptok = smC
        e_sb = lambda t: big[:, t, 0:D]
        wsr = gcv[:, :, :].rearrange("p a b -> p (a b)")[:, 0:NG * P]
        wcT, rwB, bsB = smA, smB, smC
        part_ = lambda t, c: big[:, t, c * HALF:(c + 1) * HALF]
        v5 = lambda t: big[:, t, D:D + 512].rearrange("p (g d e) -> p g d e", g=NKV, d=2)
        kdup = lambda g: big[:, g, D + 512:D + 1024]
        q5 = lambda f: big[:, f // 2, (f % 2) * HALF:(f % 2 + 1) * HALF]
        bias2 = lambda g: (smA if g % 2 == 0 else smB)[:, :].rearrange("p (h k) -> p h k", h=4)
        dist2 = smC[:, 0:256]
        prob2 = lambda s: tok[:, s % 2, :].rearrange("p (h k) -> p h k", h=4)
        prT2 = lambda kt: gcv[:, kt, 0:HALF]

        ACTS = {"x": (actA_hi, actA_lo), "p": (actA_hi, actA_lo), "x1": (actA_hi, actA_lo),
                "h": (actB_hi, actB_lo), "n": (actB_hi, actB_lo)}
        READS = {**dict.fromkeys(("q", "k", "v", "za", "b", "c", "u", "zc"), (actA_hi, actA_lo)),
                 "wo": (actB_hi, actB_lo), "gate": (actA_hi, actA_lo),
                 **dict.fromkeys(("v4", "z4", "u4"), (actB_hi, actB_lo)),
                 "a0": (actA_hi, actA_lo), "a1": (actA_hi, actA_lo),
                 **dict.fromkeys(("v5", "k5", "q5", "z5"), (actB_hi, actB_lo)),
                 "f": (actA_hi, actA_lo)}

        x_in = [sem(f"x_in{t}") for t in range(T)]
        raw_in = [sem(f"raw_in{n}") for n in range(4)]
        small_in, pre_in, post_in, ple_in = sem("small_in"), sem("pre_in"), sem("post_in"), sem("ple_in")
        apre_in, apost_in, bpost_in = sem("apre_in"), sem("apost_in"), sem("bpost_in")
        p_in, ws_in, bs_in, stored = sem("p_in"), sem("ws_in"), sem("bs_in"), sem("stored")
        w_scaled, w_hi, w_lo = sem("w_scaled"), sem("w_hi"), sem("w_lo")
        pe_block = sem("pe_block")
        NORMS = {n: k for k, n in enumerate(("x", "m1", "e", "x2", "ln", "a", "h3", "f"))}
        squared = {n: sem(f"squared_{n}") for n in NORMS}
        ms_ready = {n: sem(f"ms_{n}") for n in NORMS}
        rstd_ready = {n: sem(f"rstd_{n}") for n in NORMS}
        tok_ready = {n: sem(f"tok_{n}") for n in ("x", "h", "n")}
        hi = {n: sem(f"hi_{n}") for n in ("x", "p", "x1", "h", "n", "conv", "attn", "y4", "y5")}
        lo = {n: sem(f"lo_{n}") for n in hi}
        ident_set, ident_made, ones_made = sem("ident_set"), sem("ident_made"), sem("ones_made")
        mhalf_made, iota_made, ws_masked = sem("mhalf_made"), sem("iota_made"), sem("ws_masked")
        pads_made, consts_made = sem("pads_made"), sem("consts_made")
        base_step, lam_step, lam_exp, cols_scaled = (sem("base_step"), sem("lam_step"), sem("lam_exp"),
                                                     sem("cols_scaled"))
        q_copied, k_copied, v_copied = sem("q_copied"), sem("k_copied"), sem("v_copied")
        za_tanh, za_gated, c_copied, g_made = sem("za_tanh"), sem("za_gated"), sem("c_copied"), sem("g_made")
        taps, b_mult, zc_tanh, zc_gated, conv_out = (sem("taps"), sem("b_mult"), sem("zc_tanh"),
                                                     sem("zc_gated"), sem("conv_out"))
        bias_made, scored, negmax, exped = sem("bias_made"), sem("scored"), sem("negmax"), sem("exped")
        recip1, lam_scaled, weighed = sem("recip1"), sem("lam_scaled"), sem("weighed")
        wt_copied, attn_copied, attn_sq = sem("wt_copied"), sem("attn_copied"), sem("attn_sq")
        ss_rooted, ss_recip, attn_normed, attn_out = (sem("ss_rooted"), sem("ss_recip"),
                                                      sem("attn_normed"), sem("attn_out"))
        post_scaled, x1_ready, e_copied, e_normed = (sem("post_scaled"), sem("x1_ready"),
                                                     sem("e_copied"), sem("e_normed"))
        wct_copied, rw_copied = sem("wct_copied"), sem("rw_copied")
        gate_tanh, gate_mult, x2_ready = sem("gate_tanh"), sem("gate_mult"), sem("x2_ready")
        v_gelu, mu_step, v_normed = sem("v_gelu"), sem("mu_step"), sem("v_normed")
        z4_tanh, z4_gated, u4_gelu, zu_made = sem("z4_tanh"), sem("z4_gated"), sem("u4_gelu"), sem("zu_made")
        s4_bias, s4_scaled, y4_made = sem("s4_bias"), sem("s4_scaled"), sem("y4_made")
        part_copied, part_added, a_scaled, h3_ready = (sem("part_copied"), sem("part_added"),
                                                       sem("a_scaled"), sem("h3_ready"))
        v5_copied, k5_copied, q5_copied = sem("v5_copied"), sem("k5_copied"), sem("q5_copied")
        dist_made, bias2_made = sem("dist_made"), sem("bias2_made")
        s5_scored, neg5, sink5, exp5, den5, rec5, prob5 = (
            sem("s5_scored"), sem("neg5"), sem("sink5"), sem("exp5"), sem("den5"), sem("rec5"), sem("prob5"))
        pt0_copied, pt1_copied, o5_copied = sem("pt0_copied"), sem("pt1_copied"), sem("o5_copied")
        z5_tanh, z5_gated, y5_made = sem("z5_tanh"), sem("z5_gated"), sem("y5_made")
        f_scaled, out_ready = sem("f_scaled"), sem("out_ready")

        def kt0_steps(s):
            g, b = STEPS2[s]
            return 3 * g + b

        def emptied(b):
            kind = b[0]
            if kind == "tr":
                name, t, j = b[1:]
                return lo[name], (2 * t + j if name != "p" else j) + 1
            if kind == "F":
                s, f = b[1:]
                if s == "k5":
                    return k5_copied, 4 * (f + 1)
                return {"q": q_copied, "k": k_copied, "za": za_gated, "c": c_copied, "u": g_made,
                        "b": b_mult, "zc": zc_gated, "z4": z4_gated, "u4": u4_gelu,
                        "q5": q5_copied, "z5": z5_gated}[s], f + 1
            if kind == "T":
                s, c, _, t = b[1:]
                return {"v": (v_copied, t + 1), "wo": (post_scaled, 2 * t + c + 1),
                        "gate": (gate_tanh, 4 * c + t + 1), "v4": (v_gelu, 4 * c + t + 1),
                        "a0": (part_copied, 4 * c + t + 1), "a1": (part_added, 4 * c + t + 1),
                        "f": (f_scaled, 2 * t + c + 1)}[s]
            a = b[1]
            if kind == "t5":
                return (pt1_copied, a + 1) if b[2] else (pt0_copied, kt0_steps(a))
            return {"sc": (scored, 2 * a + b[-1] + 1), "tw": (wt_copied, a + 1),
                    "pv": (attn_copied, a // 4 + 1), "ss": (ss_rooted, a + 1),
                    "ple": (squared["e"], 2 * a + b[-1] + 1), "wt": (wct_copied, a + 1),
                    "rw": (rw_copied, a + 1), "s4": (s4_scaled, a + 1), "v5": (v5_copied, 2 * a + 2),
                    "s5": (s5_scored, 4 * a + 2 * b[-1] + 2), "o5": (o5_copied, 2 * a + 2)}[kind]

        def last_block(n):
            s, j, kind = UNITS[n][:3]
            if kind == "P":
                return BLOCK["ple", T - 1, 1]
            if s == "v5":
                return BLOCK["v5", T - 1]
            if kind == "F":
                return BLOCK["F", s, 2 * j + 1]
            return BLOCK["T", s, j // 2, j % 2, T - 1]

        block = ctx.enter_context(nc.Block())

        @block.sync
        def _(sp):
            def load_half(n):
                s, j, kind, name, k0, c0 = UNITS[n // 2]
                if n >= 4:
                    sp.wait_ge(w_lo, n - 3)
                tiles, cols = {"F": (4, 256), "T": (2, 512), "P": (1, 1024)}[kind]
                k = k0 + tiles * (n % 2)
                src = MATRICES[name][k * P:(k + tiles) * P, c0:c0 + cols].rearrange("(k p) c -> p k c", p=P)
                dst = raw[:, n % 4, :].rearrange("p (k c) -> p k c", k=tiles)
                sp.dma_start(dst, src).then_inc(raw_in[n % 4], 16)

            spread = lambda row, n: row.to_broadcast([P, n])
            for t in range(T):
                sp.dma_start(resid[:, t], x[0, t * P:(t + 1) * P, :]).then_inc(x_in[t], 16)
                if t == 0:
                    sp.dma_start(gain[:, 0], spread(pre_norm_gain[0:1, :], D)).then_inc(pre_in, 16)
            for n in range(4):
                load_half(n)
            for n, v in enumerate((lambda_q1, lambda_k1, lambda_q2, lambda_k2)):
                sp.dma_start(lamv[:, n], spread(v[0:1, :], DQK1)).then_inc(small_in, 16)
            sp.dma_start(sinks[:, :], spread(b_sinks_2[0:1, :], NQ)).then_inc(small_in, 16)
            with nc.allow_non_contiguous_dma(reason="columns of gains, a few KB"):
                sp.dma_start(subg[:, 0:1], subln_gain[0].rearrange("(p a) -> p a", a=1)).then_inc(small_in, 16)
                for j in range(3):
                    sp.dma_start(convc[:, j], conv_w[0, j].rearrange("(f p) -> p f", p=P)).then_inc(small_in, 16)
                for dst, src in ((lng, a_ln_g_2[0]), (lnb, a_ln_b_2[0]), (kvg, kv_norm_g_2), (bg, b_pre_g_2[0])):
                    sp.dma_start(dst[:, :], src.rearrange("(f p) -> p f", p=P)).then_inc(small_in, 16)
            sp.dma_start(gain[:, 1], spread(post_norm_gain[0:1, :], D)).then_inc(post_in, 16)
            sp.dma_start(gain[:, 2], spread(ple_norm_gain[0:1, :], D)).then_inc(ple_in, 16)

            def p_load():
                sp.wait_ge(base_step, 1)
                sp.dma_start(ptok[:, :].rearrange("p (t c) -> p t c", t=T),
                             p[0, 0].rearrange("(t p) c -> p t c", p=P)).then_inc(p_in, 16)

            def apre_load():
                sp.wait_ge(tok_ready["x"], T)
                sp.dma_start(gain[:, 0], spread(a_pre_g_2[0:1, :], D)).then_inc(apre_in, 16)

            def ws_load():
                sp.wait_ge(conv_out, 4)
                sp.dma_start(wsr.rearrange("t (g s) -> t g s", g=NG),
                             a_w_s_2[0].rearrange("g t s -> t g s")).then_inc(ws_in, 16)

            def bs_load():
                sp.wait_ge(pe_block, BLOCK["tr", "p", 0, 1])
                sp.dma_start(bsB[:, :], spread(a_b_s_2[0:1].rearrange("a g t -> a (g t)"), NG * P))\
                  .then_inc(bs_in, 16)

            def apost_load():
                sp.wait_ge(e_normed, T)
                sp.dma_start(gain[:, 2], spread(a_post_g_2[0:1, :], D)).then_inc(apost_in, 16)

            def bpost_load():
                sp.wait_ge(x1_ready, T)
                sp.dma_start(gain[:, 1], spread(b_post_g_2[0:1, :], D)).then_inc(bpost_in, 16)

            late = {UNIT_NO["v", 0]: apre_load, UNIT_NO["za", 0]: p_load, UNIT_NO["wo", 3]: ws_load,
                    UNIT_NO["ple", 0]: bs_load, UNIT_NO["v4", 2]: apost_load, UNIT_NO["v4", 4]: bpost_load}
            for n in range(4, 2 * len(UNITS)):
                if n % 2 == 0 and n // 2 in late:
                    late[n // 2]()
                load_half(n)
            for t in range(T):
                sp.wait_ge(out_ready, t + 1)
                sp.dma_start(out[0, t * P:(t + 1) * P, :], resid[:, t]).then_inc(stored, 16)
            sp.wait_ge(stored, 16 * T)

        @block.gpsimd
        def _(pool):
            pool.memset(ident[:, :], 0.0).then_inc(ident_set, 1)
            pool.memset(mhalf[:, :], -0.5).then_inc(mhalf_made, 1)
            pool.memset(ones[:, :], 1.0).then_inc(ones_made, 1)
            pool.wait_ge(ident_set, 1)
            pool.affine_select(out=ident[:, :], in_=ident[:, :], compare_op=ALU.not_equal, fill=1.0,
                               base=0, pattern=[[-1, P]], channel_multiplier=1).then_inc(ident_made, 1)
            pool.iota(iot, pattern=[[-1, HALF]], base=HALF - P, channel_multiplier=1).then_inc(iota_made, 1)
            pool.wait_ge(mhalf_made, 1)

            def root(name, t, width):
                n = NORMS[name]
                count = T + t + 1 if name in ("m1", "a", "f") else t + 1 if name == "ln" else 2 * (t + 1)
                pool.wait_ge(squared[name], count)
                m = ms[:, n, t:t + 1]
                if name == "ln":
                    pool.tensor_scalar(m, ss[:, n, t, 0:1], 1.0 / width, EPS, ALU.mult, ALU.add)\
                        .then_inc(ms_ready[name], 1)
                else:
                    pool.tensor_scalar(m, ss[:, n, t, 0:1], ss[:, n, t, 1:2], EPS, ALU.add,
                                       ALU.add).then_inc(ms_ready[name], 1)
                pool.wait_ge(ms_ready[name], t + 1)
                pool.tensor_tensor(rstd[:, n, t:t + 1], m, mhalf[:, 0:1], ALU.pow).then_inc(rstd_ready[name], 1)

            halves = [0, 0]

            def split_half(n):
                u = n // 2
                s, kind = UNITS[u][0], UNITS[u][2]
                src = raw[:, n % 4, :]
                a = (n % 2) * RAW
                pool.wait_ge(raw_in[n % 4], 16 * (n // 4 + 1))
                if s in ("v5", "k5", "q5", "z5"):
                    g = kvg if s in ("v5", "k5") else bg
                    pool.wait_ge(small_in, 16 * 13)
                    for k in range(4):
                        pool.tensor_scalar(src[:, k * 256:(k + 1) * 256], src[:, k * 256:(k + 1) * 256],
                                           g[:, 4 * (n % 2) + k:4 * (n % 2) + k + 1], 1.0, ALU.mult,
                                           ALU.mult).then_inc(w_scaled, 1)
                    halves[0] += 4
                    pool.wait_ge(w_scaled, halves[0])
                if u >= 2:
                    pool.wait_ge(pe_block, last_block(u - 2))
                for i in range(2):
                    c = slice(a + i * HALF, a + (i + 1) * HALF)
                    pool.tensor_scalar(whi[:, u % 2, c], src[:, i * HALF:(i + 1) * HALF], 1.0, 1.0,
                                       ALU.mult, ALU.mult).then_inc(w_hi, 1)
                for i in range(2):
                    c = slice(a + i * HALF, a + (i + 1) * HALF)
                    pool.wait_ge(w_hi, 2 * n + i + 1)
                    ins = pool.tensor_tensor(wlo[:, u % 2, c], src[:, i * HALF:(i + 1) * HALF],
                                             whi[:, u % 2, c].bitcast(f32), ALU.subtract)
                ins.then_inc(w_lo, 1)

            def mask_ws():
                pool.wait_ge(ws_in, 16)
                w = wsr.rearrange("t (g s) -> t g s", g=NG)
                pool.affine_select(out=w, in_=w, compare_op=ALU.is_ge, fill=0.0, base=0,
                                   pattern=[[0, NG], [-1, P]], channel_multiplier=1).then_inc(ws_masked, 1)

            def make_dist():
                pool.wait_ge(s4_bias, KA)
                pool.iota(smC[:, 256:512].bitcast(mybir.dt.int32), pattern=[[-1, 256]], base=P,
                          channel_multiplier=1).then_inc(dist_made, 1)
                pool.wait_ge(dist_made, 1)
                pool.tensor_copy(dist2, smC[:, 256:512].bitcast(mybir.dt.int32)).then_inc(dist_made, 1)
                pool.wait_ge(dist_made, 2)
                pool.affine_select(out=dist2, in_=dist2, compare_op=ALU.is_ge, fill=MASKED, base=P,
                                   pattern=[[-1, 256]], channel_multiplier=1).then_inc(dist_made, 1)
                pool.wait_ge(dist_made, 3)
                pool.affine_select(out=dist2, in_=dist2, compare_op=ALU.is_ge, fill=MASKED, base=-1,
                                   pattern=[[1, 256]], channel_multiplier=-1).then_inc(dist_made, 1)

            for t in range(T):
                root("x", t, D)
            after = {}
            at = lambda s, j, h: 2 * UNIT_NO[s, j] + h
            after[at("ple", 0, 0)] = [lambda: root("m1", 0, D)]
            after[at("ple", 0, 1)] = [lambda t=t: root("m1", t, D) for t in range(1, T)]
            after[at("gate", 1, 0)] = [lambda t=t: root("e", t, D) for t in range(T)]
            after[at("gate", 0, 1)] = [mask_ws]
            after[at("v4", 0, 0)] = [lambda: root("x2", 0, D)]
            after[at("v4", 0, 1)] = [lambda t=t: root("x2", t, D) for t in range(1, T)]
            after[at("u4", 0, 1)] = [lambda t=t: root("ln", t, AW) for t in range(T)]
            after[at("a1", 3, 1)] = [make_dist]
            after[at("v5", 0, 1)] = [lambda t=t, n=n: root(n, t, D) for t in range(T) for n in ("a", "h3")]
            for n in range(2 * len(UNITS)):
                split_half(n)
                for f in after.get(n, ()):
                    f()
            for t in range(T):
                root("f", t, D)

        @block.scalar
        def _(act):
            A = nc.scalar.activation

            last_square = []

            def square(name, t, c, src):
                if last_square:
                    act.wait_ge(*last_square)
                value = T * c + t + 1 if name in ("m1", "a", "f") else 2 * t + c + 1
                last_square[:] = squared[name], value
                A(junk[:, :], src, ACT.Square, scale=1.0 / 32, accum_out=ss[:, NORMS[name], t, c:c + 1])\
                    .then_inc(squared[name], 1)

            def turned(name, t, j):
                b = ("tr", name, t, j)
                act.wait_ge(pe_block, BLOCK[b])
                bank = psum[bank_of(b)][:, :]
                if name == "p":
                    A(actA_hi[:, j, :], bank, ACT.Copy).then_inc(hi[name], 1)
                else:
                    A(ACTS[name][0][:, 4 * j:4 * j + 4, t * P:(t + 1) * P],
                      bank.rearrange("p (k c) -> p k c", k=4), ACT.Copy).then_inc(hi[name], 1)

            for t in range(T):
                act.wait_ge(x_in[t], 16)
                for c in range(2):
                    square("x", t, c, resid[:, t, c * HALF:(c + 1) * HALF])
            for t in range(T):
                for j in range(2):
                    turned("x", t, j)
                if t == 1:
                    act.wait_ge(lam_step, 2)
                    A(lams[:, 2:4], lams[:, 0:2], ACT.Exp).then_inc(lam_exp, 1)
            for f in range(4):
                act.wait_ge(pe_block, BLOCK["F", "q", f])
                A(tile(qT, f), psum[bank_of(("F", "q", f))][:, :], ACT.Copy, scale=DQK1 ** -0.5)\
                    .then_inc(q_copied, 1)
            for f in range(4):
                act.wait_ge(pe_block, BLOCK["F", "k", f])
                A(tile(kT, f), psum[bank_of(("F", "k", f))][:, :], ACT.Copy).then_inc(k_copied, 1)
            for t in range(T):
                b = ("T", "v", 0, 1, t)
                act.wait_ge(pe_block, BLOCK[b])
                A(tile(vtok, t), psum[bank_of(b)][:, :], ACT.Copy).then_inc(v_copied, 1)

            def job_out(i):
                s, f = JOBS1[i]
                act.wait_ge(pe_block, BLOCK["F", s, f])
                bank = psum[bank_of(("F", s, f))][:, :]
                if s == "za":
                    if f:
                        act.wait_ge(za_gated, f)
                    A(th[:, :], bank, ACT.Tanh, scale=0.5).then_inc(za_tanh, 1)
                if s == "c":
                    act.wait_ge(pads_made, 1)
                    if f >= 2:
                        act.wait_ge(conv_out, f - 1)
                    A(gcv[:, f % 2, 2:2 + S], bank, ACT.Copy).then_inc(c_copied, 1)
                if s == "zc":
                    act.wait_ge(za_gated, 4)
                    if f:
                        act.wait_ge(zc_gated, f)
                    A(th[:, :], bank, ACT.Tanh, scale=0.5).then_inc(zc_tanh, 1)

            def conv_hi(i):
                s, f = JOBS1[i]
                if s == "zc":
                    act.wait_ge(conv_out, f + 1)
                    A(actB_hi[:, 4 + f, :], acc[:, f % 2, :], ACT.Copy).then_inc(hi["conv"], 1)

            for i in range(SLOTS1 + 2):
                if 1 <= i <= SLOTS1:
                    job_out(i - 1)
                if 2 <= i:
                    conv_hi(i - 2)
                if 1 <= i < 17:
                    h, qt = STEPS1[i - 1]
                    b = ("tw", i - 1)
                    act.wait_ge(pe_block, BLOCK[b])
                    n = (qt + 1) * P
                    A(wgtT1[:, 0:n], psum[bank_of(b)][:, 0:n], ACT.Copy).then_inc(wt_copied, 1)
                if 2 <= i < 18 and STEPS1[i - 2][1] == 3:
                    h = STEPS1[i - 2][0]
                    act.wait_ge(pe_block, BLOCK["pv", i - 2])
                    A(tile(qT, h), psum[7][:, :], ACT.Copy).then_inc(attn_copied, 1)
                if i < 16:
                    h, qt = STEPS1[i]
                    n = (qt + 1) * P
                    act.wait_ge(negmax, i + 1)
                    for m in range(2):
                        A(prob1(m)[:, 0:n], prob1(m)[:, 0:n], ACT.Exp, bias=nmx[:, m:m + 1],
                          accum_out=rs[:, m:m + 1]).then_inc(exped, 1)
                if i == 17:
                    for h in range(NH1):
                        act.wait_ge(attn_copied, h + 1)
                        A(tile(kT, h), tile(qT, h), ACT.Square).then_inc(attn_sq, 1)
                if i == 18:
                    for h in range(NH1):
                        act.wait_ge(pe_block, BLOCK["ss", h])
                        A(tile(kT, h), psum[bank_of(("ss", h))][:, :], ACT.Sqrt, scale=1.0 / DV1,
                          bias=eps_sub[:, 0:1]).then_inc(ss_rooted, 1)
                if i == 19:
                    for h in range(NH1):
                        act.wait_ge(attn_out, h + 1)
                        A(actB_hi[:, h, :], tile(qT, h), ACT.Copy).then_inc(hi["attn"], 1)
            for c in range(2):
                if c == 0:
                    for k in range(2):
                        turned("p", 0, k)
                for t in range(T):
                    act.wait_ge(pe_block, BLOCK["T", "wo", c, 1, t])
                    square("m1", t, c, psum[t + 4 * c][:, :])

            def ple_out(t):
                for c in range(2):
                    b = ("ple", t, c)
                    act.wait_ge(pe_block, BLOCK[b])
                    A(e_sb(t)[:, c * HALF:(c + 1) * HALF], psum[bank_of(b)][:, :], ACT.Copy).then_inc(e_copied, 1)
                    square("e", t, c, psum[bank_of(b)][:, :])

            for t in range(T):
                ple_out(t)
                if t:
                    for j in range(2):
                        turned("x1", t - 1, j)
            for j in range(2):
                turned("x1", 3, j)
            for j in range(2):
                act.wait_ge(pe_block, BLOCK["wt", j])
                A(wcT[:, j * HALF:(j + 1) * HALF], psum[bank_of(("wt", j))][:, :], ACT.Copy).then_inc(wct_copied, 1)
            for j in range(2):
                act.wait_ge(pe_block, BLOCK["rw", j])
                A(rwB[:, j * HALF:(j + 1) * HALF], psum[bank_of(("rw", j))][:, :], ACT.Copy).then_inc(rw_copied, 1)

            def gate_out(c, t):
                n = 4 * c + t
                act.wait_ge(pe_block, BLOCK["T", "gate", c, 1, t])
                if n:
                    act.wait_ge(gate_mult, n)
                else:
                    act.wait_ge(zc_gated, 4)
                A(th[:, :], psum[t + 4 * c][:, :], ACT.Tanh, scale=0.5).then_inc(gate_tanh, 1)

            def square_x2(t):
                act.wait_ge(x2_ready, T + t + 1)
                for c in range(2):
                    square("x2", t, c, resid[:, t, c * HALF:(c + 1) * HALF])

            for t in range(T):
                gate_out(0, t)
            gate_out(1, 0)
            for t in range(1, T):
                gate_out(1, t)
                square_x2(t - 1)
            square_x2(3)
            for t in range(T):
                for j in range(2):
                    turned("h", t, j)

            def ln_square(t):
                act.wait_ge(mu_step, 2 * (t + 1))
                if t:
                    act.wait_ge(squared["ln"], t)
                A(tok[:, :, :].rearrange("p a b -> p (a b)"), big[:, t, :], ACT.Square,
                  bias=nmu[:, 1, t:t + 1], accum_out=ss[:, NORMS["ln"], t, 0:1]).then_inc(squared["ln"], 1)

            for c in range(4):
                for t in range(T):
                    b = ("T", "v4", c, 1, t)
                    act.wait_ge(pe_block, BLOCK[b])
                    A(big[:, t, c * HALF:(c + 1) * HALF], psum[bank_of(b)][:, :], ACT.Gelu_apprx_tanh,
                      accum_out=vsum[:, t, c:c + 1]).then_inc(v_gelu, 1)
            for t in range(T):
                ln_square(t)

            def z4_out(f):
                act.wait_ge(pe_block, BLOCK["F", "z4", f])
                act.wait_ge(z4_gated, f) if f else act.wait_ge(gate_mult, 8)
                A(th[:, :], psum[bank_of(("F", "z4", f))][:, :], ACT.Tanh, scale=0.5).then_inc(z4_tanh, 1)

            def u4_out(f):
                act.wait_ge(pe_block, BLOCK["F", "u4", f])
                if f >= 2:
                    act.wait_ge(zu_made, f - 1)
                A(gcv[:, f % 2, 0:S], psum[bank_of(("F", "u4", f))][:, :], ACT.Gelu_apprx_tanh)\
                    .then_inc(u4_gelu, 1)

            def h3_out(t):
                act.wait_ge(h3_ready, t + 1)
                for c in range(2):
                    square("h3", t, c, resid[:, t, c * HALF:(c + 1) * HALF])

            for half in range(2):
                for j in range(4 * half, 4 * half + 4):
                    for f in range(2):
                        z4_out(2 * j + f)
                    for f in range(2):
                        u4_out(2 * j + f)
                    for f in (2 * j, 2 * j + 1):
                        act.wait_ge(y4_made, f + 1)
                        A(actA_hi[:, f % KD, :], acc[:, f % 2, :], ACT.Copy).then_inc(hi["y4"], 1)
                for c in range(2):
                    for t in range(T):
                        if half == 0:
                            act.wait_ge(pe_block, BLOCK["T", "a0", c, 1, t])
                            A(part_(t, c), psum[t + 4 * c][:, :], ACT.Copy).then_inc(part_copied, 1)
                        else:
                            act.wait_ge(part_added, 4 * c + t + 1)
                            square("a", t, c, part_(t, c))
                        if half == 1 and c == 1 and t:
                            h3_out(t - 1)
                if half == 1:
                    h3_out(3)

            def k5_out(j):
                act.wait_ge(pe_block, BLOCK["F", "k5", j])
                bank = psum[bank_of(("F", "k5", j))]
                for g in range(2):
                    for half in range(2):
                        A(kdup(2 * j + g)[half * DH:(half + 1) * DH, :], bank[g * DH:(g + 1) * DH, :],
                          ACT.Copy).then_inc(k5_copied, 1)

            def q5_out(f):
                act.wait_ge(pe_block, BLOCK["F", "q5", f])
                A(q5(f), psum[bank_of(("F", "q5", f))][:, :], ACT.Copy, scale=DH ** -0.5).then_inc(q5_copied, 1)

            for t in range(T):
                for j in range(2):
                    turned("n", t, j)
                act.wait_ge(pe_block, BLOCK["v5", t])
                src = psum[bank_of(("v5", t))][:, 0:256].rearrange("p (g e) -> p g e", g=NKV)
                for d in range(2):
                    A(v5(t)[:, :, d, :], src, ACT.Copy).then_inc(v5_copied, 1)
            for j in range(2):
                k5_out(j)
            for f in range(2):
                q5_out(f)
            for i in range(SLOTS2 + 2):
                if i - 1 in JOBS2:
                    s, f = JOBS2[i - 1]
                    if s == "q5":
                        q5_out(f)
                    else:
                        act.wait_ge(pe_block, BLOCK["F", s, f])
                        act.wait_ge(z5_gated, f) if f else act.wait_ge(z4_gated, KA)
                        A(th[:, :], psum[bank_of(("F", s, f))][:, :], ACT.Tanh, scale=0.5).then_inc(z5_tanh, 1)
                if 1 <= i < 17 and STEPS2[i - 1][1]:
                    b = ("t5", i - 1, 0)
                    act.wait_ge(pe_block, BLOCK[b])
                    A(prT2(0), psum[bank_of(b)][:, :], ACT.Copy).then_inc(pt0_copied, 1)
                if 2 <= i < 18:
                    g, b = STEPS2[i - 2]
                    act.wait_ge(pe_block, BLOCK["o5", i - 2])
                    for half in range(2):
                        rows = slice(half * DH, (half + 1) * DH)
                        dst = big[rows, g, 0:D].rearrange("p (f s) -> p f s", f=2)[:, :, b * P:(b + 1) * P]
                        src = psum[3][rows, :].rearrange("p (f h s) -> p f h s", f=2, h=2)[:, :, half, :]
                        A(dst, src, ACT.Copy).then_inc(o5_copied, 1)
                if i < 16:
                    g, b = STEPS2[i]
                    k0 = 0 if b else P
                    act.wait_ge(sink5, i + 1)
                    for h in range(4):
                        pr = prob2(i)[:, h, k0:256]
                        A(pr, pr, ACT.Exp, bias=nmx[:, h:h + 1], accum_out=rs[:, h:h + 1]).then_inc(exp5, 1)
                    A(esk[:, :], den[:, :], ACT.Exp).then_inc(exp5, 1)
                if i - 2 in JOBS2 and JOBS2[i - 2][0] == "z5":
                    f = JOBS2[i - 2][1]
                    act.wait_ge(y5_made, f + 1)
                    A(actA_hi[:, f, :], acc[:, f % 2, :], ACT.Copy).then_inc(hi["y5"], 1)
            for c in range(2):
                for t in range(T):
                    act.wait_ge(pe_block, BLOCK["T", "f", c, 1, t])
                    square("f", t, c, psum[t + 4 * c][:, :])

        @block.vector
        def _(dve):
            V = nc.vector

            def rest(name, t, j):
                b = ("tr", name, t, j)
                n = 2 * t + j if name != "p" else j
                dve.wait_ge(hi[name], n + 1)
                bank = psum[bank_of(b)][:, :]
                H, L = ACTS[name]
                if name == "p":
                    V.tensor_tensor(L[:, j, :], bank, H[:, j, :].bitcast(f32), ALU.subtract).then_inc(lo[name], 1)
                else:
                    at = (slice(None), slice(4 * j, 4 * j + 4), slice(t * P, (t + 1) * P))
                    V.tensor_tensor(L[at], bank.rearrange("p (k c) -> p k c", k=4), H[at].bitcast(f32),
                                    ALU.subtract).then_inc(lo[name], 1)

            def normed(name, norm, t, g, turn):
                dve.wait_ge(rstd_ready[norm], t + 1)
                if t >= 2:
                    dve.wait_ge(pe_block, BLOCK["tr", turn, t - 2, 1])
                r = rstd[:, NORMS[norm], t:t + 1]
                if g is None:
                    ins = V.tensor_scalar(tok[:, t % 2], resid[:, t], r, None, ALU.mult)
                else:
                    ins = V.scalar_tensor_tensor(tok[:, t % 2], resid[:, t], r, gain[:, g], ALU.mult, ALU.mult)
                ins.then_inc(tok_ready[turn], 1)

            V.memset(gcv[:, :, 0:2], 0.0).then_inc(pads_made, 1)
            V.memset(eps_sub[:, :], SUBLN_EPS).then_inc(consts_made, 1)
            dve.wait_ge(iota_made, 1)
            V.tensor_copy(base1, iot).then_inc(base_step, 1)
            dve.wait_ge(base_step, 1)
            V.scalar_tensor_tensor(base1, base1, -1.0, base1, ALU.mult, ALU.max).then_inc(base_step, 1)
            dve.wait_ge(base_step, 2)
            V.memset(base1[0:64, HALF - 64:HALF], MASKED).then_inc(base_step, 1)
            dve.wait_ge(pre_in, 16)
            for t in range(T):
                normed("x", "x", t, 0, "x")
                if t:
                    for j in range(2):
                        rest("x", t - 1, j)
                if t == 1:
                    dve.wait_ge(small_in, 16 * 13)
                    for n in range(2):
                        V.tensor_tensor_reduce(lamv[:, 2 * n], lamv[:, 2 * n], lamv[:, 2 * n + 1], 1.0, 0.0,
                                               ALU.mult, ALU.add, lams[:, n:n + 1]).then_inc(lam_step, 1)
            for j in range(2):
                rest("x", 3, j)
            dve.wait_ge(lam_exp, 1)
            V.tensor_tensor(lams[:, 4:5], lams[:, 3:4], lams[:, 2:3], ALU.subtract).then_inc(lam_step, 1)
            dve.wait_ge(lam_step, 3)
            V.tensor_scalar(lams[:, 5:6], lams[:, 4:5], -LAM_INIT, None, ALU.add).then_inc(lam_step, 1)
            V.tensor_scalar(subg[:, 1:2], subg[:, 0:1], 0.5 * (1.0 - LAM_INIT), None, ALU.mult).then_inc(cols_scaled, 1)
            V.tensor_scalar(convc[:, :, :], convc[:, :, :], 0.5, None, ALU.mult).then_inc(cols_scaled, 1)
            V.tensor_scalar(lng[:, :], lng[:, :], 0.5, None, ALU.mult).then_inc(cols_scaled, 1)
            V.tensor_scalar(lnb[:, :], lnb[:, :], 0.5, None, ALU.mult).then_inc(cols_scaled, 1)
            dve.wait_ge(base_step, 3)

            def job_in(i):
                s, f = JOBS1[i]
                bank = psum[bank_of(("F", s, f))][:, :]
                g0 = gcv[:, f % 2, :]
                if s == "za":
                    dve.wait_ge(za_tanh, f + 1)
                    V.scalar_tensor_tensor(tile(zaT, f), th[:, :], 1.0, bank, ALU.add, ALU.mult)\
                        .then_inc(za_gated, 1)
                if s == "u":
                    dve.wait_ge(c_copied, f + 1)
                    dve.wait_ge(pe_block, BLOCK["F", s, f])
                    V.tensor_tensor(g0[:, 2:2 + S], bank, g0[:, 2:2 + S], ALU.mult).then_inc(g_made, 1)
                if s == "b":
                    a = acc[:, f % 2, :]
                    dve.wait_ge(cols_scaled, 2)
                    dve.wait_ge(g_made, f + 1)
                    if f >= 2:
                        dve.wait_ge(lo["conv"], f - 1)
                    V.tensor_scalar(a, g0[:, 0:S], convc[:, 0, f:f + 1], None, ALU.mult).then_inc(taps, 1)
                    for j in (1, 2):
                        dve.wait_ge(taps, 3 * f + j)
                        V.scalar_tensor_tensor(a, g0[:, j:j + S], convc[:, j, f:f + 1], a, ALU.mult, ALU.add)\
                            .then_inc(taps, 1)
                    dve.wait_ge(taps, 3 * f + 3)
                    dve.wait_ge(pe_block, BLOCK["F", s, f])
                    V.tensor_tensor(a, bank, a, ALU.mult).then_inc(b_mult, 1)
                if s == "zc":
                    dve.wait_ge(zc_tanh, f + 1)
                    V.scalar_tensor_tensor(g0[:, 2:2 + S], th[:, :], 1.0, bank, ALU.add, ALU.mult)\
                        .then_inc(zc_gated, 1)
                    dve.wait_ge(zc_gated, f + 1)
                    dve.wait_ge(b_mult, f + 1)
                    V.tensor_tensor(acc[:, f % 2, :], acc[:, f % 2, :], g0[:, 2:2 + S], ALU.mult)\
                        .then_inc(conv_out, 1)

            def conv_lo(i):
                s, f = JOBS1[i]
                if s == "zc":
                    dve.wait_ge(hi["conv"], f + 1)
                    V.tensor_tensor(actB_lo[:, 4 + f, :], acc[:, f % 2, :], actB_hi[:, 4 + f, :].bitcast(f32),
                                    ALU.subtract).then_inc(lo["conv"], 1)

            def scores(i):
                h, qt = STEPS1[i]
                n = (qt + 1) * P
                if qt == 0:
                    V.tensor_scalar(bias1(h), base1, -SLOPE1[h], None, ALU.mult).then_inc(bias_made, 1)
                    dve.wait_ge(bias_made, h + 1)
                for m in range(2):
                    b = ("sc", i, m)
                    dve.wait_ge(pe_block, BLOCK[b])
                    V.tensor_tensor_reduce(prob1(m)[:, 0:n], psum[bank_of(b)][:, 0:n], bias1(h)[:, HALF - n:HALF],
                                           1.0, -3e38, ALU.add, ALU.max, mx[:, m:m + 1]).then_inc(scored, 1)
                dve.wait_ge(scored, 2 * i + 2)
                V.tensor_scalar(nmx[:, 0:2], mx[:, 0:2], -1.0, None, ALU.mult).then_inc(negmax, 1)

            def weights(i):
                h, qt = STEPS1[i]
                n = (qt + 1) * P
                dve.wait_ge(exped, 2 * i + 2)
                V.reciprocal(rr[:, 0:2], rs[:, 0:2]).then_inc(recip1, 1)
                dve.wait_ge(recip1, i + 1)
                dve.wait_ge(lam_step, 4)
                V.tensor_scalar(prob1(1)[:, 0:n], prob1(1)[:, 0:n], rr[:, 1:2], lams[:, 5:6], ALU.mult, ALU.mult)\
                    .then_inc(lam_scaled, 1)
                dve.wait_ge(lam_scaled, i + 1)
                if i:
                    dve.wait_ge(pe_block, BLOCK["tw", i - 1])
                V.scalar_tensor_tensor(wgt1[:, 0:n], prob1(0)[:, 0:n], rr[:, 0:1], prob1(1)[:, 0:n],
                                       ALU.mult, ALU.add).then_inc(weighed, 1)

            for i in range(SLOTS1 + 2):
                if i < 16:
                    scores(i)
                if 1 <= i <= SLOTS1:
                    job_in(i - 1)
                if 2 <= i:
                    conv_lo(i - 2)
                if i < 16:
                    weights(i)
                if i == 18:
                    dve.wait_ge(cols_scaled, 1)
                    for h in range(NH1):
                        dve.wait_ge(ss_rooted, h + 1)
                        V.reciprocal(tile(kT, h), tile(kT, h)).then_inc(ss_recip, 1)
                        dve.wait_ge(ss_recip, h + 1)
                        V.tensor_tensor(tile(qT, h), tile(qT, h), tile(kT, h), ALU.mult).then_inc(attn_normed, 1)
                        dve.wait_ge(attn_normed, h + 1)
                        V.scalar_tensor_tensor(tile(qT, h), tile(qT, h), subg[:, 1:2], tile(zaT, h), ALU.mult,
                                               ALU.mult).then_inc(attn_out, 1)
                if i == 19:
                    for h in range(NH1):
                        dve.wait_ge(hi["attn"], h + 1)
                        V.tensor_tensor(actB_lo[:, h, :], tile(qT, h), actB_hi[:, h, :].bitcast(f32),
                                        ALU.subtract).then_inc(lo["attn"], 1)

            def post(name, done, t, g, ready):
                dve.wait_ge(rstd_ready[name], t + 1)
                if t:
                    dve.wait_ge(ready, t)
                for c in range(2):
                    V.scalar_tensor_tensor(acc[:, c, :], psum[t + 4 * c][:, :], rstd[:, NORMS[name], t:t + 1],
                                           gain[:, g, c * HALF:(c + 1) * HALF], ALU.mult, ALU.mult)\
                        .then_inc(done, 1)
                dve.wait_ge(done, 2 * t + 2)
                V.tensor_tensor(resid[:, t], resid[:, t], acc[:, :, :].rearrange("p a b -> p (a b)"), ALU.add)\
                    .then_inc(ready, 1)

            for k in range(2):
                rest("p", 0, k)
            dve.wait_ge(post_in, 16)
            for t in range(T):
                post("m1", post_scaled, t, 1, x1_ready)
                if t == 2:
                    for j in range(2):
                        rest("x1", 0, j)
            for t in range(1, T):
                for j in range(2):
                    rest("x1", t, j)
            dve.wait_ge(ple_in, 16)
            for t in range(T):
                dve.wait_ge(rstd_ready["e"], t + 1)
                V.scalar_tensor_tensor(e_sb(t), e_sb(t), rstd[:, NORMS["e"], t:t + 1], gain[:, 2], ALU.mult,
                                       ALU.mult).then_inc(e_normed, 1)

            def gate_in(c, t):
                n = 4 * c + t
                half = slice(c * HALF, (c + 1) * HALF)
                dve.wait_ge(gate_tanh, n + 1)
                dve.wait_ge(e_normed, t + 1)
                if n:
                    dve.wait_ge(x2_ready, n)
                V.scalar_tensor_tensor(acc[:, 0, :], th[:, :], 1.0, e_sb(t)[:, half], ALU.add, ALU.mult)\
                    .then_inc(gate_mult, 1)
                dve.wait_ge(gate_mult, n + 1)
                V.scalar_tensor_tensor(resid[:, t, half], acc[:, 0, :], 0.5, resid[:, t, half], ALU.mult,
                                       ALU.add).then_inc(x2_ready, 1)

            for t in range(T):
                gate_in(0, t)
            gate_in(1, 0)
            gate_in(1, 1)
            gate_in(1, 2)
            dve.wait_ge(apre_in, 16)
            normed("h", "x2", 0, 0, "h")
            gate_in(1, 3)
            normed("h", "x2", 1, 0, "h")
            for t in range(T):
                for j in range(2):
                    rest("h", t, j)
                if t + 2 < T:
                    normed("h", "x2", t + 2, 0, "h")
            dve.wait_ge(bs_in, 16)
            V.tensor_scalar(bsB[:, :], bsB[:, :], 0.5, None, ALU.mult).then_inc(cols_scaled, 1)
            for t in range(T):
                dve.wait_ge(v_gelu, 12 + t + 1)
                V.tensor_reduce(nmu[:, 0, t:t + 1], vsum[:, t, :], AX.X, ALU.add).then_inc(mu_step, 1)
                dve.wait_ge(mu_step, 2 * t + 1)
                V.tensor_scalar(nmu[:, 1, t:t + 1], nmu[:, 0, t:t + 1], -1.0 / AW, None, ALU.mult).then_inc(mu_step, 1)

            def z4_in(f):
                dve.wait_ge(z4_tanh, f + 1)
                if f >= 2:
                    dve.wait_ge(lo["y4"], f - 1)
                V.scalar_tensor_tensor(acc[:, f % 2, :], th[:, :], 1.0, psum[bank_of(("F", "z4", f))][:, :],
                                       ALU.add, ALU.mult).then_inc(z4_gated, 1)

            def u4_in(f):
                dve.wait_ge(u4_gelu, f + 1)
                dve.wait_ge(z4_gated, f + 1)
                V.tensor_tensor(acc[:, f % 2, :], acc[:, f % 2, :], gcv[:, f % 2, 0:S], ALU.mult).then_inc(zu_made, 1)

            def s4_in(f):
                g = f // 2
                bias = tok[:, f % 2, HALF:HALF + P]
                s = tok[:, f % 2, 0:HALF]
                dve.wait_ge(cols_scaled, 5)
                dve.wait_ge(rw_copied, 2)
                if f >= 2:
                    dve.wait_ge(s4_scaled, f - 1)
                V.scalar_tensor_tensor(bias, rwB[:, g * P:(g + 1) * P], lnb[:, f:f + 1], bsB[:, g * P:(g + 1) * P],
                                       ALU.mult, ALU.add).then_inc(s4_bias, 1)
                dve.wait_ge(s4_bias, f + 1)
                b = ("s4", f)
                dve.wait_ge(pe_block, BLOCK[b])
                if f >= 2:
                    dve.wait_ge(y4_made, f - 1)
                V.scalar_tensor_tensor(s.rearrange("p (t c) -> p t c", t=T),
                                       psum[bank_of(b)][:, :].rearrange("p (t c) -> p t c", t=T), lng[:, f:f + 1],
                                       bias.unsqueeze(1).to_broadcast([P, T, P]), ALU.mult, ALU.add)\
                    .then_inc(s4_scaled, 1)
                dve.wait_ge(s4_scaled, f + 1)
                dve.wait_ge(zu_made, f + 1)
                V.tensor_tensor(acc[:, f % 2, :], acc[:, f % 2, :], s, ALU.mult).then_inc(y4_made, 1)

            for half in range(2):
                for j in range(4 * half, 4 * half + 4):
                    for f in range(2):
                        z4_in(2 * j + f)
                        if j == 0:
                            for t in (2 * f, 2 * f + 1):
                                dve.wait_ge(rstd_ready["ln"], t + 1)
                                V.tensor_scalar(big[:, t, :], big[:, t, :], nmu[:, 1, t:t + 1],
                                                rstd[:, NORMS["ln"], t:t + 1], ALU.add, ALU.mult)\
                                    .then_inc(v_normed, 1)
                    for f in range(2):
                        u4_in(2 * j + f)
                    for f in (2 * j, 2 * j + 1):
                        s4_in(f)
                    for f in (2 * j, 2 * j + 1):
                        dve.wait_ge(hi["y4"], f + 1)
                        V.tensor_tensor(actA_lo[:, f % KD, :], acc[:, f % 2, :], actA_hi[:, f % KD, :].bitcast(f32),
                                        ALU.subtract).then_inc(lo["y4"], 1)

            def part_in(c, t):
                dve.wait_ge(pe_block, BLOCK["T", "a1", c, 1, t])
                dve.wait_ge(part_copied, 4 * c + t + 1)
                V.tensor_tensor(part_(t, c), psum[t + 4 * c][:, :], part_(t, c), ALU.add).then_inc(part_added, 1)

            def h3_in(t):
                dve.wait_ge(rstd_ready["a"], t + 1)
                V.scalar_tensor_tensor(big[:, t, 0:D], big[:, t, 0:D], rstd[:, NORMS["a"], t:t + 1], gain[:, 2],
                                       ALU.mult, ALU.mult).then_inc(a_scaled, 1)
                dve.wait_ge(a_scaled, t + 1)
                V.tensor_tensor(resid[:, t], resid[:, t], big[:, t, 0:D], ALU.add).then_inc(h3_ready, 1)

            for t in range(T):
                part_in(0, t)
            dve.wait_ge(apost_in, 16)
            for t in range(T):
                part_in(1, t)
                if t >= 2:
                    h3_in(t - 2)
            h3_in(2)
            normed("n", "h3", 0, None, "n")
            h3_in(3)
            for t in range(1, T):
                normed("n", "h3", t, None, "n")
                for j in range(2):
                    rest("n", t - 1, j)
            for j in range(2):
                rest("n", 3, j)

            def scores2(i):
                g, b = STEPS2[i]
                k0 = 0 if b else P
                if b == 0:
                    dve.wait_ge(pe_block, BLOCK["s4", KA - 1])
                    for h in range(4):
                        V.tensor_scalar(bias2(g)[:, h, :], dist2, -SLOPE2[4 * g + h], None, ALU.mult)\
                            .then_inc(bias2_made, 1)
                    dve.wait_ge(bias2_made, 4 * g + 4)
                if i >= 2:
                    dve.wait_ge(pe_block, BLOCK["t5", i - 2, 1])
                for h in (0, 2, 1, 3):
                    blk = ("s5", i, h % 2)
                    dve.wait_ge(pe_block, BLOCK[blk])
                    src = psum[bank_of(blk)][:, (h // 2) * 256 + k0:(h // 2) * 256 + 256]
                    V.tensor_tensor_reduce(prob2(i)[:, h, k0:256], src, bias2(g)[:, h, k0:256], 1.0,
                                           sinks[:, 4 * g + h:4 * g + h + 1], ALU.add, ALU.max, mx[:, h:h + 1])\
                        .then_inc(s5_scored, 1)
                dve.wait_ge(s5_scored, 4 * i + 4)
                V.tensor_scalar(nmx[:, :], mx[:, :], -1.0, None, ALU.mult).then_inc(neg5, 1)
                dve.wait_ge(neg5, i + 1)
                V.tensor_tensor(den[:, :], sinks[:, 4 * g:4 * g + 4], nmx[:, :], ALU.add).then_inc(sink5, 1)

            def probs2(i):
                g, b = STEPS2[i]
                k0 = 0 if b else P
                dve.wait_ge(exp5, 5 * i + 5)
                V.tensor_tensor(den[:, :], rs[:, :], esk[:, :], ALU.add).then_inc(den5, 1)
                dve.wait_ge(den5, i + 1)
                V.reciprocal(rr[:, :], den[:, :]).then_inc(rec5, 1)
                dve.wait_ge(rec5, i + 1)
                for h in range(4):
                    pr = prob2(i)[:, h, k0:256]
                    V.tensor_scalar(pr, pr, rr[:, h:h + 1], None, ALU.mult).then_inc(prob5, 1)

            dve.wait_ge(dist_made, 4)
            for i in range(SLOTS2 + 2):
                if i < 16:
                    scores2(i)
                if i - 1 in JOBS2 and JOBS2[i - 1][0] == "z5":
                    f = JOBS2[i - 1][1]
                    a = acc[:, f % 2, :]
                    dve.wait_ge(z5_tanh, f + 1)
                    if f >= 2:
                        dve.wait_ge(lo["y5"], f - 1)
                    V.scalar_tensor_tensor(a, th[:, :], 1.0, psum[bank_of(("F", "z5", f))][:, :], ALU.add,
                                           ALU.mult).then_inc(z5_gated, 1)
                    dve.wait_ge(z5_gated, f + 1)
                    dve.wait_ge(o5_copied, 8 * (f // 2 + 1))
                    V.scalar_tensor_tensor(a, a, 0.5, q5(f), ALU.mult, ALU.mult).then_inc(y5_made, 1)
                if i - 2 in JOBS2 and JOBS2[i - 2][0] == "z5":
                    f = JOBS2[i - 2][1]
                    dve.wait_ge(hi["y5"], f + 1)
                    V.tensor_tensor(actA_lo[:, f, :], acc[:, f % 2, :], actA_hi[:, f, :].bitcast(f32),
                                    ALU.subtract).then_inc(lo["y5"], 1)
                if 1 <= i < 17:
                    b = ("t5", i - 1, 1)
                    dve.wait_ge(pe_block, BLOCK[b])
                    V.tensor_copy(prT2(1), psum[bank_of(b)][:, :]).then_inc(pt1_copied, 1)
                if i < 16:
                    probs2(i)
            dve.wait_ge(bpost_in, 16)
            for t in range(T):
                post("f", f_scaled, t, 1, out_ready)

        @block.tensor
        def _(pe):
            M = nc.tensor.matmul

            def exact(out_, whi_, wlo_, xhi_, xlo_, start, stop):
                M(out_, whi_, xhi_, start=start, stop=False)
                M(out_, whi_, xlo_, start=False, stop=False)
                return M(out_, wlo_, xhi_, start=False, stop=stop)

            def weights_of(stage, j):
                n = UNIT_NO[stage, j]
                pe.wait_ge(w_lo, 2 * n + 2)
                return whi[:, n % 2, :], wlo[:, n % 2, :]

            def feature_major(stage, f):
                H, L = weights_of(stage, f // 2)
                aH, aL = READS[stage]
                out_ = psum[bank_of(("F", stage, f))][:, :]
                for k in range(KD):
                    c = slice(k * 256 + (f % 2) * P, k * 256 + (f % 2) * P + P)
                    ins = exact(out_, H[:, c], L[:, c], aH[:, k, :], aL[:, k, :], k == 0, k == KD - 1)
                return ins

            def token_major(stage, c, kh, t):
                H, L = weights_of(stage, 2 * c + kh)
                aH, aL = READS[stage]
                bank = bank_of(("T", stage, c, kh, t))
                rows = slice(t * P, (t + 1) * P)
                for k in range(4):
                    w = slice(k * HALF, (k + 1) * HALF)
                    a = 4 * kh + k
                    ins = exact(psum[bank][:, :], aH[:, a, rows], aL[:, a, rows], H[:, w], L[:, w],
                                kh == 0 and k == 0, kh == 1 and k == 3)
                return ins

            def turn(name, t, j):
                bank = psum[bank_of(("tr", name, t, j))]
                for k in range(4):
                    if name == "p":
                        src = ptok[:, k * PLE + j * P:k * PLE + (j + 1) * P]
                    elif name == "x1":
                        src = resid[:, t, (4 * j + k) * P:(4 * j + k + 1) * P]
                    else:
                        src = tok[:, t % 2, (4 * j + k) * P:(4 * j + k + 1) * P]
                    ins = nc.tensor.transpose(bank[:, k * P:(k + 1) * P], src, ident[:, :])
                return ins

            def ready(b):
                kind = b[0]
                if kind == "tr":
                    name, t, j = b[1:]
                    if name == "p":
                        pe.wait_ge(p_in, 16)
                    elif name == "x1":
                        pe.wait_ge(x1_ready, t + 1)
                    else:
                        pe.wait_ge(tok_ready[name], t + 1)
                    return
                s = b[1]
                if kind == "F":
                    if s == "q":
                        pe.wait_ge(lo["x"], 2 * T)
                    if s == "k5":
                        pe.wait_ge(lo["n"], 2 * T)
                if kind == "T":
                    c, kh, t = b[2:]
                    if s == "wo":
                        pe.wait_ge(*((lo["attn"], NH1) if kh == 0 else (lo["conv"], 4)))
                    if s in ("gate", "v4"):
                        pe.wait_ge(lo["x1" if s == "gate" else "h"], 2 * (t + 1))
                    if s in ("a0", "a1"):
                        pe.wait_ge(lo["y4"], KD * int(s[1]) + 4 * (kh + 1))
                    if s == "f":
                        pe.wait_ge(lo["y5"], 4 * (kh + 1))
                if kind == "ple":
                    pe.wait_ge(lo["p"], 2)
                if kind == "v5":
                    pe.wait_ge(lo["n"], 2 * (s + 1))
                if kind == "sc":
                    pe.wait_ge(k_copied, s // 4 + 1)
                if kind == "tw":
                    pe.wait_ge(weighed, s + 1)
                if kind == "pv":
                    pe.wait_ge(wt_copied, s + 1)
                    pe.wait_ge(v_copied, T)
                if kind == "ss":
                    pe.wait_ge(attn_sq, s + 1)
                if kind == "wt":
                    pe.wait_ge(ws_masked, 1)
                if kind == "rw":
                    pe.wait_ge(wct_copied, 2)
                if kind == "s4":
                    pe.wait_ge(v_normed, T)
                if kind == "s5":
                    pe.wait_ge(q5_copied, 2 * (s // 4) + 2)
                    pe.wait_ge(k5_copied, 8)
                if kind == "t5":
                    pe.wait_ge(prob5, 4 * (s + 1))
                if kind == "o5":
                    pe.wait_ge(pt1_copied, s + 1)
                    if STEPS2[s][1]:
                        pe.wait_ge(pt0_copied, kt0_steps(s))

            def work(b):
                kind = b[0]
                bank = psum[bank_of(b)]
                if kind == "tr":
                    return turn(*b[1:])
                if kind == "F":
                    return feature_major(*b[1:])
                if kind == "T":
                    return token_major(*b[1:])
                if kind == "sc":
                    i, m = b[1:]
                    h, qt = STEPS1[i]
                    rows = slice(m * DQK1, (m + 1) * DQK1)
                    n = (qt + 1) * P
                    return M(bank[:, 0:n], tile(qT, h)[rows, qt * P:(qt + 1) * P], tile(kT, h)[rows, 0:n],
                             start=True, stop=True)
                if kind == "tw":
                    for k in range(STEPS1[b[1]][1] + 1):
                        c = slice(k * P, (k + 1) * P)
                        ins = nc.tensor.transpose(bank[:, c], wgt1[:, c], ident[:, :])
                    return ins
                if kind == "pv":
                    h, qt = STEPS1[b[1]]
                    for k in range(qt + 1):
                        ins = M(bank[:, qt * P:(qt + 1) * P], tile(vtok, k)[:, h * P:(h + 1) * P],
                                wgtT1[:, k * P:(k + 1) * P], start=k == 0, stop=k == qt)
                    return ins
                if kind == "ss":
                    return M(bank[:, :], ones[:, :], tile(kT, b[1]), start=True, stop=True)
                if kind == "ple":
                    t, c = b[1:]
                    H, L = weights_of("ple", 0)
                    rows = slice(t * P, (t + 1) * P)
                    for k in range(2):
                        w = slice(k * D + c * HALF, k * D + (c + 1) * HALF)
                        ins = exact(bank[:, :], actA_hi[:, k, rows], actA_lo[:, k, rows], H[:, w], L[:, w],
                                    k == 0, k == 1)
                    return ins
                if kind == "wt":
                    for k in range(4):
                        g = 4 * b[1] + k
                        ins = nc.tensor.transpose(bank[:, k * P:(k + 1) * P], wsr[:, g * P:(g + 1) * P], ident[:, :])
                    return ins
                if kind == "rw":
                    return M(bank[:, :], ones[:, :], wcT[:, b[1] * HALF:(b[1] + 1) * HALF], start=True, stop=True)
                if kind == "s4":
                    f = b[1]
                    for n in range(T):
                        ins = M(bank[:, n * P:(n + 1) * P], big[:, n, f * P:(f + 1) * P],
                                wcT[:, (f // 2) * P:(f // 2 + 1) * P], start=True, stop=True)
                    return ins
                if kind == "v5":
                    t = b[1]
                    H, L = weights_of("v5", 0)
                    rows = slice(t * P, (t + 1) * P)
                    for k in range(KD):
                        w = slice(k * 256, (k + 1) * 256)
                        ins = exact(bank[:, 0:256], actB_hi[:, k, rows], actB_lo[:, k, rows], H[:, w], L[:, w],
                                    k == 0, k == KD - 1)
                    return ins
                if kind == "s5":
                    i, m = b[1:]
                    g, blk = STEPS2[i]
                    k0 = 0 if blk else P
                    keys = slice((blk - 1) * P + k0, (blk + 1) * P)
                    rows = slice(m * DH, (m + 1) * DH)
                    for j in range(2):
                        ins = M(bank[:, j * 256 + k0:(j + 1) * 256], q5(2 * g + j)[rows, blk * P:(blk + 1) * P],
                                kdup(g)[rows, keys], start=True, stop=True)
                    return ins
                if kind == "t5":
                    i, kt = b[1:]
                    for h in range(4):
                        ins = nc.tensor.transpose(bank[:, h * P:(h + 1) * P],
                                                  prob2(i)[:, h, kt * P:(kt + 1) * P], ident[:, :])
                    return ins
                if kind == "o5":
                    g, blk = STEPS2[b[1]]
                    kts = (0, 1) if blk else (1,)
                    for kt in kts:
                        v = v5(blk - 1 + kt)[:, g, :, :].rearrange("p d e -> p (d e)")
                        ins = M(bank[:, :], v, prT2(kt), start=kt == kts[0], stop=kt == 1)
                    return ins

            pe.wait_ge(ident_made, 1)
            pe.wait_ge(ones_made, 1)
            for b in ORDER:
                if BEFORE.get(b) is not None:
                    pe.wait_ge(*emptied(BEFORE[b]))
                ready(b)
                work(b).then_inc(pe_block, 1)


_INS = ["x", "p", "pre_norm_gain", "w_in", "lambda_q1", "lambda_k1", "lambda_q2", "lambda_k2",
        "subln_gain", "conv_w", "w_out", "post_norm_gain", "w_ple_proj", "ple_norm_gain", "w_ple_gate",
        "a_w_in_2", "a_ln_g_2", "a_ln_b_2", "a_w_s_2", "a_b_s_2", "a_w_out_2", "a_pre_g_2",
        "a_post_g_2", "kv_norm_g_2", "w_k_2", "w_v_2", "b_w_in_2", "b_sinks_2", "b_w_out_2",
        "b_pre_g_2", "b_post_g_2"]


def kernel(**inputs):
    import numpy as np
    import concourse.bacc as bacc
    from concourse.bass_utils import run_bass_kernel_spmd

    nc = bacc.Bacc("TRN2", target_bir_lowering=False, num_devices=1)
    arrays, args = {}, []
    for name in _INS:
        a = np.ascontiguousarray(inputs[name])
        arrays[f"in_{name}"] = a
        args.append(nc.dram_tensor(f"in_{name}", a.shape, mybir.dt.from_np(a.dtype), kind="ExternalInput").ap())
    args.append(nc.dram_tensor("out_dram", (1, S, D), mybir.dt.float32, kind="ExternalOutput").ap())
    program(nc, *args)
    r = run_bass_kernel_spmd(nc, [arrays], core_ids=[0])
    return r.results[0]["out_dram"]
```

```python
import math
from contextlib import ExitStack

import concourse.bass as bass
from concourse import mybir

P = 128
S = 512
T = S // P
D = 1024
KD = D // P
HALF = 512
NH1, DV1, DQK1 = 4, 128, 64
LAM_INIT = 0.8 - 0.6 * math.exp(0.0)
AW = 2048
KA = AW // P
NG = 8
NQ, NKV, DH = 16, 4, 64
PLE = 256
EPS, SUBLN_EPS = 1e-6, 1e-5
MASKED = 1e30
SLOPE1 = [2.0 ** (-8.0 * (h + 1) / NH1) for h in range(NH1)]
SLOPE2 = [2.0 ** (-8.0 * (h + 1) / NQ) for h in range(NQ)]
UNIT = 2048
RAW = UNIT // 2


def weight_units():
    u = []
    part = lambda n: n * 512
    u += [("v", kh, "T", "w_in", 4 * kh, part(2)) for kh in range(2)]
    for stage, n in (("q", 0), ("k", 1)):
        u += [(stage, j, "F", "w_in", 0, part(n) + 256 * j) for j in range(2)]
    u += [("za", j, "F", "w_in", 0, part(3) + 256 * j) for j in range(2)]
    for j in range(2):
        for stage, n in (("c", 5), ("u", 6), ("b", 4), ("zc", 7)):
            u += [(stage, j, "F", "w_in", 0, part(n) + 256 * j)]
    u += [("wo", 2 * c + kh, "T", "w_out", 4 * kh, 512 * c) for c in range(2) for kh in range(2)]
    u += [("ple", 0, "P", "w_ple_proj", 0, 0)]
    u += [("gate", 2 * c + kh, "T", "w_ple_gate", 4 * kh, 512 * c) for c in range(2) for kh in range(2)]
    u += [("v4", 2 * c + kh, "T", "a_w_in_2", 4 * kh, AW + 512 * c) for c in range(4) for kh in range(2)]
    for half in range(2):
        for j in range(4 * half, 4 * half + 4):
            u += [("z4", j, "F", "a_w_in_2", 0, 2 * AW + 256 * j), ("u4", j, "F", "a_w_in_2", 0, 256 * j)]
        u += [(f"a{half}", 2 * c + kh, "T", "a_w_out_2", 8 * half + 4 * kh, 512 * c)
              for c in range(2) for kh in range(2)]
    u += [("v5", 0, "F", "w_v_2", 0, 0), ("k5", 0, "F", "w_k_2", 0, 0)]
    u += [("q5", j, "F", "b_w_in_2", 0, 256 * j) for j in range(4)]
    u += [("z5", j, "F", "b_w_in_2", 0, 1024 + 256 * j) for j in range(4)]
    u += [("f", 2 * c + kh, "T", "b_w_out_2", 4 * kh, 512 * c) for c in range(2) for kh in range(2)]
    return u


UNITS = weight_units()
SLOTTED = [n for n, u in enumerate(UNITS) if u[0] != "v5"]
SLOT = {n: k % 2 for k, n in enumerate(SLOTTED)}
SLOT_BEFORE = {n: SLOTTED[k - 2] for k, n in enumerate(SLOTTED) if k >= 2}
UNIT_NO = {(s, j): n for n, (s, j, *_) in enumerate(UNITS)}

STEPS1 = [(h, qt) for h in range(NH1) for qt in range(T)]
JOBS1 = [("za", f) for f in range(4)]
for _j in range(2):
    for _s in ("c", "u", "b", "zc"):
        JOBS1 += [(_s, 2 * _j), (_s, 2 * _j + 1)]
SLOTS1 = len(JOBS1)
STEPS2 = [(g, b) for g in range(NKV) for b in range(T)]
JOBS2 = [("q5", f) for f in range(2, 8)] + [("z5", f) for f in range(8)]
_parts = [(kind, *job) for job in JOBS2 for kind in ("Fk", "F")]
SLOTS2 = 18
PARTS2 = {}
for _i, (_g, _b) in enumerate(STEPS2):
    PARTS2[_i] = [_parts.pop(0) for _ in range(2 if _b else 1)]
DONE2 = {i: [p[1:] for p in ps if p[0] == "F"] for i, ps in PARTS2.items()}
MEET2 = {f: max(4 * (f // 2) + 6, 2 + min(i for i in DONE2 if ("z5", f) in DONE2[i])) for f in range(8)}


HEADS = {("v", 0, 0): 2, ("wo", 0, 0): 3}


def tensor_order():
    o = []
    for t in range(T):
        o += [("tr", "x", t, j) for j in range(2)] + [("Th", "v", 0, 0, t)]
    o += [("T", "v", 0, kh, t) for kh in range(2) for t in range(T)]
    o += [("F", "q", f) for f in range(4)] + [("F", "k", f) for f in range(4)]
    for i in range(SLOTS1):
        if 2 <= i < 18:
            o += [("pv", i - 2)]
        if 1 <= i < 17:
            o += [("tw", i - 1)]
        if i < 16:
            o += [("sc", i, m) for m in range(2)]
        o += [("F", *JOBS1[i])]
        if i >= 6 and i % 4 == 2:
            o += [("ta", i // 4 - 1)]
    o += [("Th", "wo", 0, 0, t) for t in range(T)] + [("tr", "p", 0, k) for k in range(2)]
    o += [("T", "wo", 0, 0, t) for t in range(T)]
    o += [("T", "wo", 0, 1, t) for t in range(T)]
    o += [("T", "wo", 1, kh, t) for kh in range(2) for t in range(T)]
    for t in range(T):
        o += [("ple", t, c) for c in range(2)]
        if t:
            o += [("tr", "x1", t - 1, j) for j in range(2)]
    o += [("T", "gate", 0, 0, 0)] + [("tr", "x1", 3, j) for j in range(2)]
    o += [("T", "gate", 0, 0, t) for t in range(1, T)] + [("wt", j) for j in range(2)]
    o += [("T", "gate", 0, 1, t) for t in range(2)] + [("rw", j) for j in range(2)]
    o += [("T", "gate", 0, 1, t) for t in range(2, T)]
    o += [("T", "gate", 1, kh, t) for kh in range(2) for t in range(T)]
    for t in range(T):
        o += [("tr", "h", t, j) for j in range(2)] + [("T", "v4", 0, 0, t)]
    o += [("T", "v4", 0, 1, t) for t in range(T)]
    o += [("T", "v4", c, kh, t) for c in range(1, 4) for kh in range(2) for t in range(T)]
    for half in range(2):
        for j in range(4 * half, 4 * half + 4):
            o += [("F", s, 2 * j + f) for s in ("z4", "u4") for f in range(2)]
            o += [("s4", 2 * j + f) for f in range(2)]
        o += [("T", f"a{half}", c, kh, t) for c in range(2 - half) for kh in range(2) for t in range(T)]
    turn = lambda t: [("tr", "n", t, j) for j in range(2)]
    o += [("T", "a1", 1, kh, t) for kh in range(2) for t in (0, 1)] + [("T", "a1", 1, 0, t) for t in (2, 3)]
    o += turn(0) + [("T", "a1", 1, 1, 2)] + turn(1) + [("T", "a1", 1, 1, 3)]
    o += [("v5", 0), ("v5", 1)] + turn(2) + [("Fa", "k5", 0), ("Fa", "k5", 1)] + turn(3)
    o += [("v5", 2), ("v5", 3)] + [("F", "k5", f) for f in range(2)] + [("F", "q5", f) for f in range(2)]
    for i in range(SLOTS2):
        if 2 <= i < 18:
            o += [("o5", i - 2)]
        if 1 <= i < 17:
            o += [("t5", i - 1, kt) for kt in ((0, 1) if STEPS2[i - 1][1] else (1,))]
        if i < 16:
            o += [("s5", i, m) for m in range(2)]
        o += PARTS2.get(i, [])
    o += [("T", "f", c, kh, t) for c in range(2) for kh in range(2) for t in range(T)]
    return o


ORDER = tensor_order()
BLOCK = {b: n + 1 for n, b in enumerate(ORDER)}


def bank_of(b):
    kind = b[0]
    if kind == "tr":
        name, t, j = b[1:]
        return {"x": (2 * t + j) % 4, "p": 4 + j, "x1": t + 4 * j, "h": 4 + (2 * t + j) % 4,
                "n": (2 * t + j) % 4}[name]
    if kind in ("F", "Fa", "Fk"):
        s, f = b[1:]
        if s in ("z4", "u4"):
            return 4 * (f // 2 % 2) + f % 2 + 2 * (s == "u4")
        if s == "k5":
            return 6 + f
        if s in ("q5", "z5"):
            return (f + 8 * (s == "z5")) % 3
        return [x[1:] for x in ORDER if x[0] == "F"].index((s, f)) % 4
    if kind in ("T", "Th"):
        s, c, _, t = b[1:]
        return t + 4 * (1 if s == "v" else c % 2)
    if kind == "s4":
        return 4 * (b[1] // 2 % 2) + b[1] % 2
    return {"sc": lambda i, m: 4 + m, "tw": lambda i: 6, "pv": lambda i: 7, "ta": lambda h: 4,
            "ple": lambda t, c: t + 4 * c, "wt": lambda j: 4 + j, "rw": lambda j: 6 + j,
            "v5": lambda t: 4 + t % 2, "s5": lambda s, m: 4 + m, "t5": lambda s, kt: 6 + kt,
            "o5": lambda s: 3}[kind](*b[1:])


def opens(b):
    if b[0] == "T":
        return b[3] == 0 and b[1:4] not in HEADS
    if b[0] == "F":
        return b[1] != "k5" and b[1:] not in JOBS2
    if b[0] == "pv":
        return STEPS1[b[1]][1] == 0
    return True


def previous_in_bank():
    last, before = {}, {}
    for b in ORDER:
        bank = bank_of(b)
        if opens(b):
            before[b] = last.get(bank)
        last[bank] = b
    return before


BEFORE = previous_in_bank()


def program(nc, x, p, pre_norm_gain, w_in, lambda_q1, lambda_k1, lambda_q2, lambda_k2, subln_gain,
            conv_w, w_out, post_norm_gain, w_ple_proj, ple_norm_gain, w_ple_gate, a_w_in_2,
            a_ln_g_2, a_ln_b_2, a_w_s_2, a_b_s_2, a_w_out_2, a_pre_g_2, a_post_g_2, kv_norm_g_2,
            w_k_2, w_v_2, b_w_in_2, b_sinks_2, b_w_out_2, b_pre_g_2, b_post_g_2, out):
    f32, f32r = mybir.dt.float32, mybir.dt.float32r
    ALU, ACT, AX = mybir.AluOpType, mybir.ActivationFunctionType, mybir.AxisListType
    MATRICES = {"w_in": w_in[0], "w_out": w_out[0], "w_ple_proj": w_ple_proj[0],
                "w_ple_gate": w_ple_gate[0], "a_w_in_2": a_w_in_2[0], "a_w_out_2": a_w_out_2[0],
                "w_v_2": w_v_2, "w_k_2": w_k_2, "b_w_in_2": b_w_in_2[0], "b_w_out_2": b_w_out_2[0]}
    ctx = ExitStack()
    with ctx:
        sb = lambda name, shape, dt=f32: ctx.enter_context(nc.sbuf_tensor(name, shape, dt))
        sem = lambda name: ctx.enter_context(nc.semaphore(name))

        raw = sb("raw", [P, 4, RAW])
        whi = sb("whi", [P, 2, UNIT], f32r)
        wlo = sb("wlo", [P, 2, UNIT], f32r)
        with nc.sbuf_tensor("zg", [P, KD, S], f32) as zg:
            pass
        actA_lo, actA_hi = sb("actA_lo", [P, KD, S], f32r), sb("actA_hi", [P, KD, S], f32r)
        actB_hi, actB_lo = sb("actB_hi", [P, KD, S], f32r), sb("actB_lo", [P, KD, S], f32r)
        resid = sb("resid", [P, T, D])
        big = sb("big", [P, 4, AW])
        gain = sb("gain", [P, 3, D])
        tok = sb("tok", [P, 2, D])
        acc = sb("acc", [P, 2, HALF])
        th = sb("th", [P, HALF])
        junk = sb("junk", [P, HALF])
        ident, ones = sb("ident", [P, P]), sb("ones", [P, P])
        lamv, lams = sb("lamv", [P, 4, DQK1]), sb("lams", [P, 8])
        subg, convc = sb("subg", [P, 2]), sb("convc", [P, 3, 4])
        lng, lnb = sb("lng", [P, KA]), sb("lnb", [P, KA])
        kvg, bg = sb("kvg", [P, KD]), sb("bg", [P, KD])
        sinks = sb("sinks", [P, NQ])
        ss = sb("ss", [P, 8, T, 4])
        ms = sb("ms", [P, 8, T])
        rstd = sb("rstd", [P, 8, T])
        mhalf = sb("mhalf", [P, 1])
        ss_attn, ms_attn, r_attn = (sb(n, [P, NH1, T]) for n in ("ss_attn", "ms_attn", "r_attn"))
        mx, nmx, rs, rr = sb("mx", [P, 4]), sb("nmx", [P, 4]), sb("rs", [P, 4]), sb("rr", [P, 4])
        esk, den = sb("esk", [P, 4]), sb("den", [P, 4])
        vsum, nmu = sb("vsum", [P, T, 4]), sb("nmu", [P, 2, T])
        with ExitStack() as place:
            small = lambda name, shape: place.enter_context(nc.sbuf_tensor(name, shape, f32))
            smA, smB, smC = small("smA", [P, D]), small("smB", [P, D]), small("smC", [P, D])
            gcv = small("gcv", [P, 2, 2 + S])
        v5hi, v5lo = sb("v5hi", [P, UNIT], f32r), sb("v5lo", [P, UNIT], f32r)
        iot = smC[:, 0:HALF].bitcast(mybir.dt.int32)

        psum = [ctx.enter_context(nc.psum_tensor(f"bank{b}", [P, HALF], f32)) for b in range(8)]

        qT, kT, vtok, zaT = big[:, 0], big[:, 1], big[:, 2], big[:, 3]
        tile = lambda region, n: region[:, n * HALF:(n + 1) * HALF]
        base1 = smB[:, 0:HALF]
        bias1 = lambda h: smA[:, (h % 2) * HALF:(h % 2 + 1) * HALF]
        prob1 = lambda m: tok[:, 0, m * HALF:(m + 1) * HALF]
        wgt1, wgtT1 = tok[:, 1, 0:HALF], tok[:, 1, HALF:D]
        ptok = smC
        e_sb = lambda t: big[:, t, 0:D]
        wsr = gcv[:, :, :].rearrange("p a b -> p (a b)")[:, 0:NG * P]
        wcT, rwB, bsB = smA, smB, smC
        part_ = lambda t, c: big[:, t, c * HALF:(c + 1) * HALF]
        v5 = lambda t: big[:, t, D:D + 512].rearrange("p (g d e) -> p g d e", g=NKV, d=2)
        kdup = lambda g: big[:, g, D + 512:D + 1024]
        q5 = lambda f: big[:, f // 2, (f % 2) * HALF:(f % 2 + 1) * HALF]
        bias2 = lambda g: (smA if g % 2 == 0 else smB)[:, :].rearrange("p (h k) -> p h k", h=4)
        dist2 = smC[:, 0:256]
        prob2 = lambda s: tok[:, s % 2, :].rearrange("p (h k) -> p h k", h=4)
        prT2 = lambda kt: gcv[:, kt, 0:HALF]


        def halves_of(n, c):
            w = slice(c * HALF, (c + 1) * HALF)
            if UNITS[n][0] == "v5":
                return v5hi[:, w], v5lo[:, w]
            return whi[:, SLOT[n], w], wlo[:, SLOT[n], w]

        ACTS = {"x": (actA_hi, actA_lo), "p": (actA_hi, actA_lo), "x1": (actA_hi, actA_lo),
                "h": (actB_hi, actB_lo), "n": (actB_hi, actB_lo)}
        READS = {**dict.fromkeys(("q", "k", "v", "za", "b", "c", "u", "zc"), (actA_hi, actA_lo)),
                 "wo": (actB_hi, actB_lo), "gate": (actA_hi, actA_lo),
                 **dict.fromkeys(("v4", "z4", "u4"), (actB_hi, actB_lo)),
                 "a0": (actA_hi, actA_lo), "a1": (actA_hi, actA_lo),
                 **dict.fromkeys(("v5", "k5", "q5", "z5"), (actB_hi, actB_lo)),
                 "f": (actA_hi, actA_lo)}

        x_in = [sem(f"x_in{t}") for t in range(T)]
        raw_in = [sem(f"raw_in{n}") for n in range(4)]
        small_in, pre_in, post_in, ple_in = sem("small_in"), sem("pre_in"), sem("post_in"), sem("ple_in")
        apre_in, apost_in, bpost_in = sem("apre_in"), sem("apost_in"), sem("bpost_in")
        p_in, ws_in, bs_in, stored = sem("p_in"), sem("ws_in"), sem("bs_in"), sem("stored")
        w_scaled, w_hi, w_lo = sem("w_scaled"), sem("w_hi"), sem("w_lo")
        pe_block = sem("pe_block")
        NORMS = {n: k for k, n in enumerate(("x", "m1", "e", "x2", "ln", "a", "h3", "f"))}
        squared = {n: sem(f"squared_{n}") for n in NORMS}
        ms_ready = {n: sem(f"ms_{n}") for n in NORMS}
        rstd_ready = {n: sem(f"rstd_{n}") for n in NORMS}
        tok_ready = {n: sem(f"tok_{n}") for n in ("x", "h", "n")}
        hi = {n: sem(f"hi_{n}") for n in ("x", "p", "x1", "h", "n", "conv", "attn", "y4", "y5")}
        lo = {n: sem(f"lo_{n}") for n in hi}
        ident_set, ident_made, ones_made = sem("ident_set"), sem("ident_made"), sem("ones_made")
        mhalf_made, iota_made, ws_masked = sem("mhalf_made"), sem("iota_made"), sem("ws_masked")
        pads_made = sem("pads_made")
        base_step, lam_step, lam_exp, cols_scaled = (sem("base_step"), sem("lam_step"), sem("lam_exp"),
                                                     sem("cols_scaled"))
        q_copied, k_copied, v_copied = sem("q_copied"), sem("k_copied"), sem("v_copied")
        za_tanh, za_gated, c_copied, g_made = sem("za_tanh"), sem("za_gated"), sem("c_copied"), sem("g_made")
        taps, b_mult, zc_tanh, zc_gated, conv_out = (sem("taps"), sem("b_mult"), sem("zc_tanh"),
                                                     sem("zc_gated"), sem("conv_out"))
        bias_made, scored, negmax, exped = sem("bias_made"), sem("scored"), sem("negmax"), sem("exped")
        recip1, lam_scaled, weighed = sem("recip1"), sem("lam_scaled"), sem("weighed")
        wt_copied, attn_copied, attn_sq = sem("wt_copied"), sem("attn_copied"), sem("attn_sq")
        msq_attn, rstd_attn, attn_normed, attn_out = (sem("msq_attn"), sem("rstd_attn"),
                                                      sem("attn_normed"), sem("attn_out"))
        post_scaled, x1_ready, e_copied, e_normed = (sem("post_scaled"), sem("x1_ready"),
                                                     sem("e_copied"), sem("e_normed"))
        wct_copied, rw_copied = sem("wct_copied"), sem("rw_copied")
        gate_tanh, gate_mult, x2_ready = sem("gate_tanh"), sem("gate_mult"), sem("x2_ready")
        v_gelu, mu_step, v_normed = sem("v_gelu"), sem("mu_step"), sem("v_normed")
        z4_tanh, z4_gated, u4_gelu, zu_made = sem("z4_tanh"), sem("z4_gated"), sem("u4_gelu"), sem("zu_made")
        s4_bias, s4_scaled, y4_made = sem("s4_bias"), sem("s4_scaled"), sem("y4_made")
        part_copied, part_added, a_gained, h3_ready = (sem("part_copied"), sem("part_added"),
                                                       sem("a_gained"), sem("h3_ready"))
        v5_copied, k5_copied, q5_copied = sem("v5_copied"), sem("k5_copied"), sem("q5_copied")
        dist_made, bias2_made = sem("dist_made"), sem("bias2_made")
        s5_scored, neg5, sink5, exp5, den5, rec5, prob5 = (
            sem("s5_scored"), sem("neg5"), sem("sink5"), sem("exp5"), sem("den5"), sem("rec5"), sem("prob5"))
        pt0_copied, pt1_copied, o5_copied = sem("pt0_copied"), sem("pt1_copied"), sem("o5_copied")
        z5_tanh, z5_gated, y5_made = sem("z5_tanh"), sem("z5_gated"), sem("y5_made")
        f_scaled, out_ready = sem("f_scaled"), sem("out_ready")

        def kt0_steps(s):
            g, b = STEPS2[s]
            return 3 * g + b

        def emptied(b):
            kind = b[0]
            if kind == "tr":
                name, t, j = b[1:]
                return lo[name], (2 * t + j if name != "p" else j) + 1
            if kind == "F":
                s, f = b[1:]
                if s == "k5":
                    return k5_copied, 4 * (f + 1)
                return {"q": q_copied, "k": k_copied, "za": za_gated, "c": c_copied, "u": g_made,
                        "b": b_mult, "zc": zc_gated, "z4": z4_gated, "u4": u4_gelu,
                        "q5": q5_copied, "z5": z5_gated}[s], f + 1
            if kind == "T":
                s, c, _, t = b[1:]
                return {"v": (v_copied, t + 1), "wo": (post_scaled, 2 * t + c + 1),
                        "gate": (gate_tanh, 4 * c + t + 1), "v4": (v_gelu, 4 * c + t + 1),
                        "a0": (part_copied, 4 * c + t + 1), "a1": (part_added, 4 * c + t + 1),
                        "f": (f_scaled, 2 * t + c + 1)}[s]
            a = b[1]
            if kind == "t5":
                return (pt1_copied, a + 1) if b[2] else (pt0_copied, kt0_steps(a))
            return {"sc": (scored, 2 * a + b[-1] + 1), "tw": (wt_copied, a + 1),
                    "pv": (attn_copied, a // 4 + 1), "ta": (attn_out, a + 1),
                    "ple": (squared["e"], 2 * a + b[-1] + 1), "wt": (wct_copied, a + 1),
                    "rw": (rw_copied, a + 1), "s4": (s4_scaled, a + 1), "v5": (v5_copied, 2 * a + 2),
                    "s5": (s5_scored, 4 * a + 2 * b[-1] + 2), "o5": (o5_copied, 2 * a + 2)}[kind]

        def last_block(n):
            s, j, kind = UNITS[n][:3]
            if kind == "P":
                return BLOCK["ple", T - 1, 1]
            if s == "v5":
                return BLOCK["v5", T - 1]
            if kind == "F":
                return BLOCK["F", s, 2 * j + 1]
            return BLOCK["T", s, j // 2, j % 2, T - 1]

        block = ctx.enter_context(nc.Block())

        @block.sync
        def _(sp):
            def load_half(n):
                s, j, kind, name, k0, c0 = UNITS[n // 2]
                if n >= 4:
                    sp.wait_ge(w_lo, n - 3)
                tiles, cols = {"F": (4, 256), "T": (2, 512), "P": (1, 1024)}[kind]
                k = k0 + tiles * (n % 2)
                src = MATRICES[name][k * P:(k + tiles) * P, c0:c0 + cols].rearrange("(k p) c -> p k c", p=P)
                dst = raw[:, n % 4, :].rearrange("p (k c) -> p k c", k=tiles)
                sp.dma_start(dst, src).then_inc(raw_in[n % 4], 16)

            spread = lambda row, n: row.to_broadcast([P, n])

            def x_load(t):
                sp.dma_start(resid[:, t], x[0, t * P:(t + 1) * P, :]).then_inc(x_in[t], 16)

            x_load(0)
            sp.dma_start(gain[:, 0], spread(pre_norm_gain[0:1, :], D)).then_inc(pre_in, 16)
            load_half(0)
            x_load(1)
            x_load(2)
            load_half(1)
            x_load(3)
            for n in (2, 3):
                load_half(n)
            for n, v in enumerate((lambda_q1, lambda_k1, lambda_q2, lambda_k2)):
                sp.dma_start(lamv[:, n], spread(v[0:1, :], DQK1)).then_inc(small_in, 16)
            sp.dma_start(sinks[:, :], spread(b_sinks_2[0:1, :], NQ)).then_inc(small_in, 16)
            with nc.allow_non_contiguous_dma(reason="columns of gains, a few KB"):
                sp.dma_start(subg[:, 0:1], subln_gain[0].rearrange("(p a) -> p a", a=1)).then_inc(small_in, 16)
                for j in range(3):
                    sp.dma_start(convc[:, j], conv_w[0, j].rearrange("(f p) -> p f", p=P)).then_inc(small_in, 16)
                for dst, src in ((lng, a_ln_g_2[0]), (lnb, a_ln_b_2[0]), (kvg, kv_norm_g_2), (bg, b_pre_g_2[0])):
                    sp.dma_start(dst[:, :], src.rearrange("(f p) -> p f", p=P)).then_inc(small_in, 16)
            sp.dma_start(gain[:, 1], spread(post_norm_gain[0:1, :], D)).then_inc(post_in, 16)
            sp.dma_start(gain[:, 2], spread(ple_norm_gain[0:1, :], D)).then_inc(ple_in, 16)

            def p_load():
                sp.wait_ge(base_step, 1)
                sp.dma_start(ptok[:, :].rearrange("p (t c) -> p t c", t=T),
                             p[0, 0].rearrange("(t p) c -> p t c", p=P)).then_inc(p_in, 16)

            def apre_load():
                sp.wait_ge(tok_ready["x"], T)
                sp.dma_start(gain[:, 0], spread(a_pre_g_2[0:1, :], D)).then_inc(apre_in, 16)

            def ws_load():
                sp.wait_ge(conv_out, 4)
                sp.dma_start(wsr.rearrange("t (g s) -> t g s", g=NG),
                             a_w_s_2[0].rearrange("g t s -> t g s")).then_inc(ws_in, 16)

            def bs_load():
                sp.wait_ge(pe_block, BLOCK["tr", "p", 0, 1])
                sp.dma_start(bsB[:, :], spread(a_b_s_2[0:1].rearrange("a g t -> a (g t)"), NG * P))\
                  .then_inc(bs_in, 16)

            def apost_load():
                sp.wait_ge(e_normed, T)
                sp.dma_start(gain[:, 2], spread(a_post_g_2[0:1, :], D)).then_inc(apost_in, 16)

            def bpost_load():
                sp.wait_ge(x1_ready, T)
                sp.dma_start(gain[:, 1], spread(b_post_g_2[0:1, :], D)).then_inc(bpost_in, 16)

            late = {UNIT_NO["k", 0]: apre_load, UNIT_NO["za", 0]: p_load, UNIT_NO["wo", 3]: ws_load,
                    UNIT_NO["ple", 0]: bs_load, UNIT_NO["v4", 2]: apost_load, UNIT_NO["v4", 4]: bpost_load}
            for n in range(4, 2 * len(UNITS)):
                if n % 2 == 0 and n // 2 in late:
                    late[n // 2]()
                load_half(n)
            for t in range(T):
                sp.wait_ge(out_ready, t + 1)
                sp.dma_start(out[0, t * P:(t + 1) * P, :], resid[:, t]).then_inc(stored, 16)
            sp.wait_ge(stored, 16 * T)

        @block.gpsimd
        def _(pool):
            pool.memset(ident[:, :], 0.0).then_inc(ident_set, 1)
            pool.memset(mhalf[:, :], -0.5).then_inc(mhalf_made, 1)
            pool.memset(ones[:, :], 1.0).then_inc(ones_made, 1)
            pool.wait_ge(ident_set, 1)
            pool.affine_select(out=ident[:, :], in_=ident[:, :], compare_op=ALU.not_equal, fill=1.0,
                               base=0, pattern=[[-1, P]], channel_multiplier=1).then_inc(ident_made, 1)
            pool.iota(iot, pattern=[[-1, HALF]], base=HALF - P, channel_multiplier=1).then_inc(iota_made, 1)
            pool.wait_ge(mhalf_made, 1)

            def root(name, t, width):
                n = NORMS[name]
                count = T + t + 1 if name in ("m1", "a", "f") else t + 1 if name == "ln" else 2 * (t + 1)
                pool.wait_ge(squared[name], count)
                m = ms[:, n, t:t + 1]
                if name == "ln":
                    pool.tensor_scalar(m, ss[:, n, t, 0:1], 1.0 / width, EPS, ALU.mult, ALU.add)\
                        .then_inc(ms_ready[name], 1)
                else:
                    pool.tensor_scalar(m, ss[:, n, t, 0:1], ss[:, n, t, 1:2], EPS, ALU.add,
                                       ALU.add).then_inc(ms_ready[name], 1)
                pool.wait_ge(ms_ready[name], t + 1)
                pool.tensor_tensor(rstd[:, n, t:t + 1], m, mhalf[:, 0:1], ALU.pow).then_inc(rstd_ready[name], 1)

            def root_attn(h):
                pool.wait_ge(attn_sq, 4 * h + 4)
                pool.tensor_scalar(ms_attn[:, h, :], ss_attn[:, h, :], 1.0 / DV1, SUBLN_EPS, ALU.mult, ALU.add)\
                    .then_inc(msq_attn, 1)
                pool.wait_ge(msq_attn, h + 1)
                pool.tensor_tensor(r_attn[:, h, :], ms_attn[:, h, :], mhalf[:, 0:1].to_broadcast([P, T]), ALU.pow)\
                    .then_inc(rstd_attn, 1)

            scaled = [0]

            def split_half(n):
                u = n // 2
                s, kind = UNITS[u][0], UNITS[u][2]
                src = raw[:, n % 4, :]
                pool.wait_ge(raw_in[n % 4], 16 * (n // 4 + 1))
                if s in ("v5", "k5", "q5", "z5"):
                    g = kvg if s in ("v5", "k5") else bg
                    pool.wait_ge(small_in, 16 * 13)
                    for k in range(4):
                        pool.tensor_scalar(src[:, k * 256:(k + 1) * 256], src[:, k * 256:(k + 1) * 256],
                                           g[:, 4 * (n % 2) + k:4 * (n % 2) + k + 1], 1.0, ALU.mult,
                                           ALU.mult).then_inc(w_scaled, 1)
                    scaled[0] += 4
                    pool.wait_ge(w_scaled, scaled[0])
                if u in SLOT_BEFORE:
                    pool.wait_ge(pe_block, last_block(SLOT_BEFORE[u]))
                if s == "v5":
                    pool.wait_ge(pe_block, BLOCK["s4", KA - 1])
                    pool.wait_ge(s4_bias, KA)
                    pool.wait_ge(zu_made, KA)
                for i in range(2):
                    H, _ = halves_of(u, 2 * (n % 2) + i)
                    pool.tensor_scalar(H, src[:, i * HALF:(i + 1) * HALF], 1.0, 1.0,
                                       ALU.mult, ALU.mult).then_inc(w_hi, 1)
                for f in after.get(n - 0.5, ()):
                    f()
                for i in range(2):
                    H, L = halves_of(u, 2 * (n % 2) + i)
                    pool.wait_ge(w_hi, 2 * n + i + 1)
                    ins = pool.tensor_tensor(L, src[:, i * HALF:(i + 1) * HALF], H.bitcast(f32), ALU.subtract)
                ins.then_inc(w_lo, 1)

            def mask_ws():
                pool.wait_ge(ws_in, 16)
                w = wsr.rearrange("t (g s) -> t g s", g=NG)
                pool.affine_select(out=w, in_=w, compare_op=ALU.is_ge, fill=0.0, base=0,
                                   pattern=[[0, NG], [-1, P]], channel_multiplier=1).then_inc(ws_masked, 1)

            def make_dist():
                pool.wait_ge(pe_block, BLOCK["v5", T - 1])
                pool.iota(smC[:, 256:512].bitcast(mybir.dt.int32), pattern=[[-1, 256]], base=P,
                          channel_multiplier=1).then_inc(dist_made, 1)
                pool.wait_ge(dist_made, 1)
                pool.tensor_copy(dist2, smC[:, 256:512].bitcast(mybir.dt.int32)).then_inc(dist_made, 1)
                pool.wait_ge(dist_made, 2)
                pool.affine_select(out=dist2, in_=dist2, compare_op=ALU.is_ge, fill=MASKED, base=P,
                                   pattern=[[-1, 256]], channel_multiplier=1).then_inc(dist_made, 1)
                pool.wait_ge(dist_made, 3)
                pool.affine_select(out=dist2, in_=dist2, compare_op=ALU.is_ge, fill=MASKED, base=-1,
                                   pattern=[[1, 256]], channel_multiplier=-1).then_inc(dist_made, 1)

            root("x", 0, D)
            after = {}
            at = lambda s, j, h: 2 * UNIT_NO[s, j] + h
            for h in range(NH1):
                after[2 * (UNIT_NO["za", 0] + 2 * h + 3) + 1] = [lambda h=h: root_attn(h)]
            after[0] = [lambda: root("x", 1, D), lambda: root("x", 2, D)]
            after[1] = [lambda: root("x", 3, D)]
            after[at("ple", 0, 0)] = [lambda: root("m1", 0, D)]
            after[at("ple", 0, 1)] = [lambda t=t: root("m1", t, D) for t in range(1, T)]
            after[at("gate", 1, 0)] = [lambda t=t: root("e", t, D) for t in range(T)]
            after[at("gate", 0, 1)] = [mask_ws]
            after[at("v4", 0, 0)] = [lambda: root("x2", 0, D)]
            after[at("v4", 0, 1)] = [lambda t=t: root("x2", t, D) for t in range(1, T)]
            after[at("u4", 0, 1)] = [lambda t=t: root("ln", t, AW) for t in range(T)]
            after[at("q5", 1, 1)] = [make_dist]
            after[at("v5", 0, 0)] = [lambda: root("a", 0, D)]
            after[at("v5", 0, 1) - 0.5] = [lambda: root("h3", 0, D), lambda: root("a", 1, D)]
            after[at("v5", 0, 1)] = [lambda: root("h3", 1, D)]
            after[at("k5", 0, 0)] = [lambda: root("a", 2, D)]
            after[at("k5", 0, 1) - 0.5] = [lambda: root("h3", 2, D), lambda: root("a", 3, D)]
            after[at("k5", 0, 1)] = [lambda: root("h3", 3, D)]
            for n in range(2 * len(UNITS)):
                split_half(n)
                for f in after.get(n, ()):
                    f()
            for t in range(T):
                root("f", t, D)

        @block.scalar
        def _(act):
            A = nc.scalar.activation

            last_square = []

            def square(name, t, c, src):
                if last_square:
                    act.wait_ge(*last_square)
                value = T * c + t + 1 if name in ("m1", "a", "f") else 2 * t + c + 1
                last_square[:] = squared[name], value
                A(junk[:, :], src, ACT.Square, scale=1.0 / 32, accum_out=ss[:, NORMS[name], t, c:c + 1])\
                    .then_inc(squared[name], 1)

            def turned(name, t, j):
                b = ("tr", name, t, j)
                act.wait_ge(pe_block, BLOCK[b])
                bank = psum[bank_of(b)][:, :]
                if name == "p":
                    A(actA_hi[:, j, :], bank, ACT.Copy).then_inc(hi[name], 1)
                else:
                    A(ACTS[name][0][:, 4 * j:4 * j + 4, t * P:(t + 1) * P],
                      bank.rearrange("p (k c) -> p k c", k=4), ACT.Copy).then_inc(hi[name], 1)

            def square_x(t):
                act.wait_ge(x_in[t], 16)
                for c in range(2):
                    square("x", t, c, resid[:, t, c * HALF:(c + 1) * HALF])

            square_x(0)
            square_x(1)
            for t in range(T):
                for j in range(2):
                    turned("x", t, j)
                if t == 0:
                    square_x(2)
                    square_x(3)
            act.wait_ge(lam_step, 2)
            A(lams[:, 2:4], lams[:, 0:2], ACT.Exp).then_inc(lam_exp, 1)
            for t in range(T):
                b = ("T", "v", 0, 1, t)
                act.wait_ge(pe_block, BLOCK[b])
                A(tile(vtok, t), psum[bank_of(b)][:, :], ACT.Copy).then_inc(v_copied, 1)
            for f in range(4):
                act.wait_ge(pe_block, BLOCK["F", "q", f])
                A(tile(qT, f), psum[bank_of(("F", "q", f))][:, :], ACT.Copy, scale=DQK1 ** -0.5)\
                    .then_inc(q_copied, 1)
            for f in range(4):
                act.wait_ge(pe_block, BLOCK["F", "k", f])
                A(tile(kT, f), psum[bank_of(("F", "k", f))][:, :], ACT.Copy).then_inc(k_copied, 1)

            def job_out(i):
                s, f = JOBS1[i]
                act.wait_ge(pe_block, BLOCK["F", s, f])
                bank = psum[bank_of(("F", s, f))][:, :]
                if s == "za":
                    if f:
                        act.wait_ge(za_gated, f)
                    A(th[:, :], bank, ACT.Tanh, scale=0.5).then_inc(za_tanh, 1)
                if s == "c":
                    act.wait_ge(pads_made, 1)
                    if f >= 2:
                        act.wait_ge(conv_out, f - 1)
                    A(gcv[:, f % 2, 2:2 + S], bank, ACT.Copy).then_inc(c_copied, 1)
                if s == "zc":
                    act.wait_ge(za_gated, 4)
                    if f:
                        act.wait_ge(zc_gated, f)
                    A(th[:, :], bank, ACT.Tanh, scale=0.5).then_inc(zc_tanh, 1)

            def conv_hi(i):
                s, f = JOBS1[i]
                if s == "zc":
                    act.wait_ge(conv_out, f + 1)
                    A(actB_hi[:, 4 + f, :], acc[:, f % 2, :], ACT.Copy).then_inc(hi["conv"], 1)

            for i in range(SLOTS1 + 2):
                if 1 <= i <= SLOTS1:
                    job_out(i - 1)
                if 2 <= i:
                    conv_hi(i - 2)
                if 1 <= i < 17:
                    h, qt = STEPS1[i - 1]
                    b = ("tw", i - 1)
                    act.wait_ge(pe_block, BLOCK[b])
                    n = (qt + 1) * P
                    A(wgtT1[:, 0:n], psum[bank_of(b)][:, 0:n], ACT.Copy).then_inc(wt_copied, 1)
                if 2 <= i < 18:
                    h, qt = STEPS1[i - 2]
                    act.wait_ge(pe_block, BLOCK["pv", i - 2])
                    act.wait_ge(attn_sq, i - 2) if i > 2 else act.wait_ge(*last_square)
                    A(junk[:, 0:P], psum[7][:, qt * P:(qt + 1) * P], ACT.Square,
                      accum_out=ss_attn[:, h, qt:qt + 1]).then_inc(attn_sq, 1)
                    if qt == 3:
                        A(tile(qT, h), psum[7][:, :], ACT.Copy).then_inc(attn_copied, 1)
                if i < 16:
                    h, qt = STEPS1[i]
                    n = (qt + 1) * P
                    act.wait_ge(negmax, i + 1)
                    for m in range(2):
                        A(prob1(m)[:, 0:n], prob1(m)[:, 0:n], ACT.Exp, bias=nmx[:, m:m + 1],
                          accum_out=rs[:, m:m + 1]).then_inc(exped, 1)
                if i >= 7 and i % 4 == 3:
                    h = i // 4 - 1
                    act.wait_ge(attn_out, h + 1)
                    A(actB_hi[:, h, :], tile(kT, h), ACT.Copy).then_inc(hi["attn"], 1)
            last_square[:] = attn_sq, 16
            for c in range(2):
                if c == 0:
                    for k in range(2):
                        turned("p", 0, k)
                for t in range(T):
                    act.wait_ge(pe_block, BLOCK["T", "wo", c, 1, t])
                    square("m1", t, c, psum[t + 4 * c][:, :])

            def ple_out(t):
                for c in range(2):
                    b = ("ple", t, c)
                    act.wait_ge(pe_block, BLOCK[b])
                    A(e_sb(t)[:, c * HALF:(c + 1) * HALF], psum[bank_of(b)][:, :], ACT.Copy).then_inc(e_copied, 1)
                    square("e", t, c, psum[bank_of(b)][:, :])

            for t in range(T):
                ple_out(t)
                if t:
                    for j in range(2):
                        turned("x1", t - 1, j)
            for j in range(2):
                turned("x1", 3, j)
            for j in range(2):
                act.wait_ge(pe_block, BLOCK["wt", j])
                A(wcT[:, j * HALF:(j + 1) * HALF], psum[bank_of(("wt", j))][:, :], ACT.Copy).then_inc(wct_copied, 1)
            for j in range(2):
                act.wait_ge(pe_block, BLOCK["rw", j])
                A(rwB[:, j * HALF:(j + 1) * HALF], psum[bank_of(("rw", j))][:, :], ACT.Copy).then_inc(rw_copied, 1)

            def gate_out(c, t):
                n = 4 * c + t
                act.wait_ge(pe_block, BLOCK["T", "gate", c, 1, t])
                if n:
                    act.wait_ge(gate_mult, n)
                else:
                    act.wait_ge(zc_gated, 4)
                A(th[:, :], psum[t + 4 * c][:, :], ACT.Tanh, scale=0.5).then_inc(gate_tanh, 1)

            def square_x2(t):
                act.wait_ge(x2_ready, T + t + 1)
                for c in range(2):
                    square("x2", t, c, resid[:, t, c * HALF:(c + 1) * HALF])

            for t in range(T):
                gate_out(0, t)
            gate_out(1, 0)
            for t in range(1, T):
                gate_out(1, t)
                square_x2(t - 1)
            square_x2(3)
            for t in range(T):
                for j in range(2):
                    turned("h", t, j)

            def ln_square(t):
                act.wait_ge(mu_step, 2 * (t + 1))
                if t:
                    act.wait_ge(squared["ln"], t)
                A(tok[:, :, :].rearrange("p a b -> p (a b)"), big[:, t, :], ACT.Square,
                  bias=nmu[:, 1, t:t + 1], accum_out=ss[:, NORMS["ln"], t, 0:1]).then_inc(squared["ln"], 1)

            for c in range(4):
                for t in range(T):
                    b = ("T", "v4", c, 1, t)
                    act.wait_ge(pe_block, BLOCK[b])
                    A(big[:, t, c * HALF:(c + 1) * HALF], psum[bank_of(b)][:, :], ACT.Gelu_apprx_tanh,
                      accum_out=vsum[:, t, c:c + 1]).then_inc(v_gelu, 1)
            for t in range(T):
                ln_square(t)

            def z4_out(f):
                act.wait_ge(pe_block, BLOCK["F", "z4", f])
                act.wait_ge(z4_gated, f) if f else act.wait_ge(gate_mult, 8)
                A(th[:, :], psum[bank_of(("F", "z4", f))][:, :], ACT.Tanh, scale=0.5).then_inc(z4_tanh, 1)

            def u4_out(f):
                act.wait_ge(pe_block, BLOCK["F", "u4", f])
                if f >= 2:
                    act.wait_ge(zu_made, f - 1)
                A(gcv[:, f % 2, 0:S], psum[bank_of(("F", "u4", f))][:, :], ACT.Gelu_apprx_tanh)\
                    .then_inc(u4_gelu, 1)

            def a_out(c, t):
                act.wait_ge(part_added, 4 * c + t + 1)
                square("a", t, c, part_(t, c))

            def h3_out(t):
                for c in range(2):
                    act.wait_ge(h3_ready, 2 * t + c + 1)
                    square("h3", t, c, resid[:, t, c * HALF:(c + 1) * HALF])

            for half in range(2):
                for j in range(4 * half, 4 * half + 4):
                    for f in range(2):
                        z4_out(2 * j + f)
                    for f in range(2):
                        u4_out(2 * j + f)
                    for f in (2 * j, 2 * j + 1):
                        act.wait_ge(y4_made, f + 1)
                        A(actA_hi[:, f % KD, :], acc[:, f % 2, :], ACT.Copy).then_inc(hi["y4"], 1)
                if half == 0:
                    for c in range(2):
                        for t in range(T):
                            act.wait_ge(pe_block, BLOCK["T", "a0", c, 1, t])
                            A(part_(t, c), psum[t + 4 * c][:, :], ACT.Copy).then_inc(part_copied, 1)

            def k5_out(j):
                act.wait_ge(pe_block, BLOCK["F", "k5", j])
                bank = psum[bank_of(("F", "k5", j))]
                for g in range(2):
                    for half in range(2):
                        A(kdup(2 * j + g)[half * DH:(half + 1) * DH, :], bank[g * DH:(g + 1) * DH, :],
                          ACT.Copy).then_inc(k5_copied, 1)

            def q5_out(f):
                act.wait_ge(pe_block, BLOCK["F", "q5", f])
                A(q5(f), psum[bank_of(("F", "q5", f))][:, :], ACT.Copy, scale=DH ** -0.5).then_inc(q5_copied, 1)

            def turned_n(t):
                for j in range(2):
                    turned("n", t, j)

            def v5_out(t):
                act.wait_ge(pe_block, BLOCK["v5", t])
                src = psum[bank_of(("v5", t))][:, 0:256].rearrange("p (g e) -> p g e", g=NKV)
                for d in range(2):
                    A(v5(t)[:, :, d, :], src, ACT.Copy).then_inc(v5_copied, 1)

            for t in range(T):
                a_out(0, t)
            a_out(1, 0)
            h3_out(0)
            a_out(1, 1)
            h3_out(1)
            turned_n(0)
            a_out(1, 2)
            turned_n(1)
            h3_out(2)
            a_out(1, 3)
            v5_out(0)
            h3_out(3)
            v5_out(1)
            turned_n(2)
            turned_n(3)
            v5_out(2)
            v5_out(3)
            for j in range(2):
                k5_out(j)
            for f in range(2):
                q5_out(f)
            for i in range(SLOTS2 + 2):
                for s, f in DONE2.get(i - 1, ()):
                    if s == "q5":
                        q5_out(f)
                    else:
                        act.wait_ge(pe_block, BLOCK["F", s, f])
                        act.wait_ge(z5_gated, f) if f else act.wait_ge(z4_gated, KA)
                        A(th[:, :], psum[bank_of(("F", s, f))][:, :], ACT.Tanh, scale=0.5).then_inc(z5_tanh, 1)
                if 1 <= i < 17 and STEPS2[i - 1][1]:
                    b = ("t5", i - 1, 0)
                    act.wait_ge(pe_block, BLOCK[b])
                    A(prT2(0), psum[bank_of(b)][:, :], ACT.Copy).then_inc(pt0_copied, 1)
                if 2 <= i < 18:
                    g, b = STEPS2[i - 2]
                    act.wait_ge(pe_block, BLOCK["o5", i - 2])
                    for half in range(2):
                        rows = slice(half * DH, (half + 1) * DH)
                        dst = big[rows, g, 0:D].rearrange("p (f s) -> p f s", f=2)[:, :, b * P:(b + 1) * P]
                        src = psum[3][rows, :].rearrange("p (f h s) -> p f h s", f=2, h=2)[:, :, half, :]
                        A(dst, src, ACT.Copy).then_inc(o5_copied, 1)
                if i < 16:
                    g, b = STEPS2[i]
                    k0 = 0 if b else P
                    act.wait_ge(sink5, i + 1)
                    for h in range(4):
                        pr = prob2(i)[:, h, k0:256]
                        A(pr, pr, ACT.Exp, bias=nmx[:, h:h + 1], accum_out=rs[:, h:h + 1]).then_inc(exp5, 1)
                    A(esk[:, :], den[:, :], ACT.Exp).then_inc(exp5, 1)
                for f in (f for f in MEET2 if MEET2[f] == i):
                    act.wait_ge(y5_made, f + 1)
                    A(actA_hi[:, f, :], acc[:, f % 2, :], ACT.Copy).then_inc(hi["y5"], 1)
            for c in range(2):
                for t in range(T):
                    act.wait_ge(pe_block, BLOCK["T", "f", c, 1, t])
                    square("f", t, c, psum[t + 4 * c][:, :])

        @block.vector
        def _(dve):
            V = nc.vector

            def rest(name, t, j):
                b = ("tr", name, t, j)
                n = 2 * t + j if name != "p" else j
                dve.wait_ge(hi[name], n + 1)
                bank = psum[bank_of(b)][:, :]
                H, L = ACTS[name]
                if name == "p":
                    V.tensor_tensor(L[:, j, :], bank, H[:, j, :].bitcast(f32), ALU.subtract).then_inc(lo[name], 1)
                else:
                    at = (slice(None), slice(4 * j, 4 * j + 4), slice(t * P, (t + 1) * P))
                    V.tensor_tensor(L[at], bank.rearrange("p (k c) -> p k c", k=4), H[at].bitcast(f32),
                                    ALU.subtract).then_inc(lo[name], 1)

            def normed(name, norm, t, g, turn):
                dve.wait_ge(rstd_ready[norm], t + 1)
                if t >= 2:
                    dve.wait_ge(pe_block, BLOCK["tr", turn, t - 2, 1])
                r = rstd[:, NORMS[norm], t:t + 1]
                if g is None:
                    ins = V.tensor_scalar(tok[:, t % 2], resid[:, t], r, None, ALU.mult)
                else:
                    ins = V.scalar_tensor_tensor(tok[:, t % 2], resid[:, t], r, gain[:, g], ALU.mult, ALU.mult)
                ins.then_inc(tok_ready[turn], 1)

            V.memset(gcv[:, :, 0:2], 0.0).then_inc(pads_made, 1)
            dve.wait_ge(iota_made, 1)
            V.tensor_copy(base1, iot).then_inc(base_step, 1)
            dve.wait_ge(base_step, 1)
            V.scalar_tensor_tensor(base1, base1, -1.0, base1, ALU.mult, ALU.max).then_inc(base_step, 1)
            dve.wait_ge(base_step, 2)
            V.memset(base1[0:64, HALF - 64:HALF], MASKED).then_inc(base_step, 1)
            dve.wait_ge(pre_in, 16)
            normed("x", "x", 0, 0, "x")
            for j in range(2):
                rest("x", 0, j)
            normed("x", "x", 1, 0, "x")
            for t in range(1, T):
                if t + 1 < T:
                    normed("x", "x", t + 1, 0, "x")
                for j in range(2):
                    rest("x", t, j)
            dve.wait_ge(small_in, 16 * 13)
            for n in range(2):
                V.tensor_tensor_reduce(lamv[:, 2 * n], lamv[:, 2 * n], lamv[:, 2 * n + 1], 1.0, 0.0,
                                       ALU.mult, ALU.add, lams[:, n:n + 1]).then_inc(lam_step, 1)
            dve.wait_ge(lam_exp, 1)
            V.tensor_tensor(lams[:, 4:5], lams[:, 3:4], lams[:, 2:3], ALU.subtract).then_inc(lam_step, 1)
            dve.wait_ge(lam_step, 3)
            V.tensor_scalar(lams[:, 5:6], lams[:, 4:5], -LAM_INIT, None, ALU.add).then_inc(lam_step, 1)
            V.tensor_scalar(subg[:, 1:2], subg[:, 0:1], 0.5 * (1.0 - LAM_INIT), None, ALU.mult).then_inc(cols_scaled, 1)
            V.tensor_scalar(convc[:, :, :], convc[:, :, :], 0.5, None, ALU.mult).then_inc(cols_scaled, 1)
            V.tensor_scalar(lng[:, :], lng[:, :], 0.5, None, ALU.mult).then_inc(cols_scaled, 1)
            V.tensor_scalar(lnb[:, :], lnb[:, :], 0.5, None, ALU.mult).then_inc(cols_scaled, 1)
            dve.wait_ge(base_step, 3)

            def job_in(i):
                s, f = JOBS1[i]
                bank = psum[bank_of(("F", s, f))][:, :]
                g0 = gcv[:, f % 2, :]
                if s == "za":
                    dve.wait_ge(za_tanh, f + 1)
                    V.scalar_tensor_tensor(tile(zaT, f), th[:, :], 1.0, bank, ALU.add, ALU.mult)\
                        .then_inc(za_gated, 1)
                if s == "u":
                    dve.wait_ge(c_copied, f + 1)
                    dve.wait_ge(pe_block, BLOCK["F", s, f])
                    V.tensor_tensor(g0[:, 2:2 + S], bank, g0[:, 2:2 + S], ALU.mult).then_inc(g_made, 1)
                if s == "b":
                    a = acc[:, f % 2, :]
                    dve.wait_ge(cols_scaled, 2)
                    dve.wait_ge(g_made, f + 1)
                    if f >= 2:
                        dve.wait_ge(lo["conv"], f - 1)
                    V.tensor_scalar(a, g0[:, 0:S], convc[:, 0, f:f + 1], None, ALU.mult).then_inc(taps, 1)
                    for j in (1, 2):
                        dve.wait_ge(taps, 3 * f + j)
                        V.scalar_tensor_tensor(a, g0[:, j:j + S], convc[:, j, f:f + 1], a, ALU.mult, ALU.add)\
                            .then_inc(taps, 1)
                    dve.wait_ge(taps, 3 * f + 3)
                    dve.wait_ge(pe_block, BLOCK["F", s, f])
                    V.tensor_tensor(a, bank, a, ALU.mult).then_inc(b_mult, 1)
                if s == "zc":
                    dve.wait_ge(zc_tanh, f + 1)
                    V.scalar_tensor_tensor(g0[:, 2:2 + S], th[:, :], 1.0, bank, ALU.add, ALU.mult)\
                        .then_inc(zc_gated, 1)
                    dve.wait_ge(zc_gated, f + 1)
                    dve.wait_ge(b_mult, f + 1)
                    V.tensor_tensor(acc[:, f % 2, :], acc[:, f % 2, :], g0[:, 2:2 + S], ALU.mult)\
                        .then_inc(conv_out, 1)

            def conv_lo(i):
                s, f = JOBS1[i]
                if s == "zc":
                    dve.wait_ge(hi["conv"], f + 1)
                    V.tensor_tensor(actB_lo[:, 4 + f, :], acc[:, f % 2, :], actB_hi[:, 4 + f, :].bitcast(f32),
                                    ALU.subtract).then_inc(lo["conv"], 1)

            def scores(i):
                h, qt = STEPS1[i]
                n = (qt + 1) * P
                if qt == 0:
                    V.tensor_scalar(bias1(h), base1, -SLOPE1[h], None, ALU.mult).then_inc(bias_made, 1)
                    dve.wait_ge(bias_made, h + 1)
                for m in range(2):
                    b = ("sc", i, m)
                    dve.wait_ge(pe_block, BLOCK[b])
                    V.tensor_tensor_reduce(prob1(m)[:, 0:n], psum[bank_of(b)][:, 0:n], bias1(h)[:, HALF - n:HALF],
                                           1.0, -3e38, ALU.add, ALU.max, mx[:, m:m + 1]).then_inc(scored, 1)
                dve.wait_ge(scored, 2 * i + 2)
                V.tensor_scalar(nmx[:, 0:2], mx[:, 0:2], -1.0, None, ALU.mult).then_inc(negmax, 1)

            def weights(i):
                h, qt = STEPS1[i]
                n = (qt + 1) * P
                dve.wait_ge(exped, 2 * i + 2)
                V.reciprocal(rr[:, 0:2], rs[:, 0:2]).then_inc(recip1, 1)
                dve.wait_ge(recip1, i + 1)
                dve.wait_ge(lam_step, 4)
                V.tensor_scalar(prob1(1)[:, 0:n], prob1(1)[:, 0:n], rr[:, 1:2], lams[:, 5:6], ALU.mult, ALU.mult)\
                    .then_inc(lam_scaled, 1)
                dve.wait_ge(lam_scaled, i + 1)
                if i:
                    dve.wait_ge(pe_block, BLOCK["tw", i - 1])
                V.scalar_tensor_tensor(wgt1[:, 0:n], prob1(0)[:, 0:n], rr[:, 0:1], prob1(1)[:, 0:n],
                                       ALU.mult, ALU.add).then_inc(weighed, 1)

            for i in range(SLOTS1 + 2):
                if i >= 7 and i % 4 == 3:
                    h = i // 4 - 1
                    dve.wait_ge(cols_scaled, 1)
                    dve.wait_ge(pe_block, BLOCK["ta", h])
                    V.scalar_tensor_tensor(tile(kT, h), psum[bank_of(("ta", h))][:, :], subg[:, 1:2], tile(zaT, h),
                                           ALU.mult, ALU.mult).then_inc(attn_out, 1)
                if i < 16:
                    scores(i)
                if 1 <= i <= SLOTS1:
                    job_in(i - 1)
                if 2 <= i:
                    conv_lo(i - 2)
                if i < 16:
                    weights(i)
                if i >= 6 and i % 4 == 2:
                    h = i // 4 - 1
                    a = tile(qT, h).rearrange("p (t c) -> p t c", t=T)
                    dve.wait_ge(rstd_attn, h + 1)
                    dve.wait_ge(attn_copied, h + 1)
                    V.tensor_tensor(a, a, r_attn[:, h, :].unsqueeze(2).to_broadcast([P, T, P]), ALU.mult)\
                        .then_inc(attn_normed, 1)
                if i >= 7 and i % 4 == 3:
                    h = i // 4 - 1
                    dve.wait_ge(hi["attn"], h + 1)
                    V.tensor_tensor(actB_lo[:, h, :], tile(kT, h), actB_hi[:, h, :].bitcast(f32),
                                    ALU.subtract).then_inc(lo["attn"], 1)

            def post(name, done, t, g, ready):
                dve.wait_ge(rstd_ready[name], t + 1)
                if t:
                    dve.wait_ge(ready, t)
                for c in range(2):
                    V.scalar_tensor_tensor(acc[:, c, :], psum[t + 4 * c][:, :], rstd[:, NORMS[name], t:t + 1],
                                           gain[:, g, c * HALF:(c + 1) * HALF], ALU.mult, ALU.mult)\
                        .then_inc(done, 1)
                dve.wait_ge(done, 2 * t + 2)
                V.tensor_tensor(resid[:, t], resid[:, t], acc[:, :, :].rearrange("p a b -> p (a b)"), ALU.add)\
                    .then_inc(ready, 1)

            for k in range(2):
                rest("p", 0, k)
            dve.wait_ge(post_in, 16)
            for t in range(T):
                post("m1", post_scaled, t, 1, x1_ready)
                if t == 2:
                    for j in range(2):
                        rest("x1", 0, j)
            for t in range(1, T):
                for j in range(2):
                    rest("x1", t, j)
            dve.wait_ge(ple_in, 16)
            for t in range(T):
                dve.wait_ge(rstd_ready["e"], t + 1)
                V.scalar_tensor_tensor(e_sb(t), e_sb(t), rstd[:, NORMS["e"], t:t + 1], gain[:, 2], ALU.mult,
                                       ALU.mult).then_inc(e_normed, 1)

            def gate_in(c, t):
                n = 4 * c + t
                half = slice(c * HALF, (c + 1) * HALF)
                dve.wait_ge(gate_tanh, n + 1)
                dve.wait_ge(e_normed, t + 1)
                if n:
                    dve.wait_ge(x2_ready, n)
                V.scalar_tensor_tensor(acc[:, 0, :], th[:, :], 1.0, e_sb(t)[:, half], ALU.add, ALU.mult)\
                    .then_inc(gate_mult, 1)
                dve.wait_ge(gate_mult, n + 1)
                V.scalar_tensor_tensor(resid[:, t, half], acc[:, 0, :], 0.5, resid[:, t, half], ALU.mult,
                                       ALU.add).then_inc(x2_ready, 1)

            for t in range(T):
                gate_in(0, t)
            gate_in(1, 0)
            gate_in(1, 1)
            gate_in(1, 2)
            dve.wait_ge(apre_in, 16)
            normed("h", "x2", 0, 0, "h")
            gate_in(1, 3)
            normed("h", "x2", 1, 0, "h")
            for t in range(T):
                for j in range(2):
                    rest("h", t, j)
                if t + 2 < T:
                    normed("h", "x2", t + 2, 0, "h")
            dve.wait_ge(bs_in, 16)
            V.tensor_scalar(bsB[:, :], bsB[:, :], 0.5, None, ALU.mult).then_inc(cols_scaled, 1)
            for t in range(T):
                dve.wait_ge(v_gelu, 12 + t + 1)
                V.tensor_reduce(nmu[:, 0, t:t + 1], vsum[:, t, :], AX.X, ALU.add).then_inc(mu_step, 1)
                dve.wait_ge(mu_step, 2 * t + 1)
                V.tensor_scalar(nmu[:, 1, t:t + 1], nmu[:, 0, t:t + 1], -1.0 / AW, None, ALU.mult).then_inc(mu_step, 1)

            def z4_in(f):
                dve.wait_ge(z4_tanh, f + 1)
                if f >= 2:
                    dve.wait_ge(lo["y4"], f - 1)
                V.scalar_tensor_tensor(acc[:, f % 2, :], th[:, :], 1.0, psum[bank_of(("F", "z4", f))][:, :],
                                       ALU.add, ALU.mult).then_inc(z4_gated, 1)

            def u4_in(f):
                dve.wait_ge(u4_gelu, f + 1)
                dve.wait_ge(z4_gated, f + 1)
                V.tensor_tensor(acc[:, f % 2, :], acc[:, f % 2, :], gcv[:, f % 2, 0:S], ALU.mult).then_inc(zu_made, 1)

            def s4_in(f):
                g = f // 2
                bias = tok[:, f % 2, HALF:HALF + P]
                s = tok[:, f % 2, 0:HALF]
                dve.wait_ge(cols_scaled, 5)
                dve.wait_ge(rw_copied, 2)
                if f >= 2:
                    dve.wait_ge(s4_scaled, f - 1)
                V.scalar_tensor_tensor(bias, rwB[:, g * P:(g + 1) * P], lnb[:, f:f + 1], bsB[:, g * P:(g + 1) * P],
                                       ALU.mult, ALU.add).then_inc(s4_bias, 1)
                dve.wait_ge(s4_bias, f + 1)
                b = ("s4", f)
                dve.wait_ge(pe_block, BLOCK[b])
                if f >= 2:
                    dve.wait_ge(y4_made, f - 1)
                V.scalar_tensor_tensor(s.rearrange("p (t c) -> p t c", t=T),
                                       psum[bank_of(b)][:, :].rearrange("p (t c) -> p t c", t=T), lng[:, f:f + 1],
                                       bias.unsqueeze(1).to_broadcast([P, T, P]), ALU.mult, ALU.add)\
                    .then_inc(s4_scaled, 1)
                dve.wait_ge(s4_scaled, f + 1)
                dve.wait_ge(zu_made, f + 1)
                V.tensor_tensor(acc[:, f % 2, :], acc[:, f % 2, :], s, ALU.mult).then_inc(y4_made, 1)

            for half in range(2):
                for j in range(4 * half, 4 * half + 4):
                    for f in range(2):
                        z4_in(2 * j + f)
                        if j == 0:
                            for t in (2 * f, 2 * f + 1):
                                dve.wait_ge(rstd_ready["ln"], t + 1)
                                V.tensor_scalar(big[:, t, :], big[:, t, :], nmu[:, 1, t:t + 1],
                                                rstd[:, NORMS["ln"], t:t + 1], ALU.add, ALU.mult)\
                                    .then_inc(v_normed, 1)
                    for f in range(2):
                        u4_in(2 * j + f)
                    for f in (2 * j, 2 * j + 1):
                        s4_in(f)
                    for f in (2 * j, 2 * j + 1):
                        dve.wait_ge(hi["y4"], f + 1)
                        V.tensor_tensor(actA_lo[:, f % KD, :], acc[:, f % 2, :], actA_hi[:, f % KD, :].bitcast(f32),
                                        ALU.subtract).then_inc(lo["y4"], 1)

            def part_in(c, t):
                dve.wait_ge(pe_block, BLOCK["T", "a1", c, 1, t])
                dve.wait_ge(part_copied, 4 * c + t + 1)
                V.tensor_tensor(part_(t, c), psum[t + 4 * c][:, :], part_(t, c), ALU.add).then_inc(part_added, 1)

            def gained(c):
                return lambda t: big[:, t, 0:HALF] if c == 0 else big[:, t, D:D + HALF]

            def part_gain(c, t):
                if c == 0:
                    dve.wait_ge(squared["a"], t + 1)
                dve.wait_ge(part_added, 4 * c + t + 1)
                V.tensor_tensor(gained(c)(t), part_(t, c), gain[:, 2, c * HALF:(c + 1) * HALF], ALU.mult)\
                    .then_inc(a_gained, 1)

            def h3_in(t):
                dve.wait_ge(rstd_ready["a"], t + 1)
                dve.wait_ge(a_gained, 4 + t + 1)
                for c in range(2):
                    half = slice(c * HALF, (c + 1) * HALF)
                    V.scalar_tensor_tensor(resid[:, t, half], gained(c)(t), rstd[:, NORMS["a"], t:t + 1],
                                           resid[:, t, half], ALU.mult, ALU.add).then_inc(h3_ready, 1)

            def rest_n(t):
                for j in range(2):
                    rest("n", t, j)

            dve.wait_ge(apost_in, 16)
            for t in range(T):
                part_in(0, t)
                if t:
                    part_gain(0, t - 1)
            part_gain(0, 3)
            part_in(1, 0)
            part_gain(1, 0)
            h3_in(0)
            part_in(1, 1)
            part_gain(1, 1)
            normed("n", "h3", 0, None, "n")
            h3_in(1)
            rest_n(0)
            normed("n", "h3", 1, None, "n")
            part_in(1, 2)
            part_gain(1, 2)
            rest_n(1)
            h3_in(2)
            part_in(1, 3)
            part_gain(1, 3)
            normed("n", "h3", 2, None, "n")
            h3_in(3)
            rest_n(2)
            normed("n", "h3", 3, None, "n")
            rest_n(3)

            def scores2(i):
                g, b = STEPS2[i]
                k0 = 0 if b else P
                if b == 0:
                    dve.wait_ge(pe_block, BLOCK["v5", T - 1])
                    for h in range(4):
                        V.tensor_scalar(bias2(g)[:, h, :], dist2, -SLOPE2[4 * g + h], None, ALU.mult)\
                            .then_inc(bias2_made, 1)
                    dve.wait_ge(bias2_made, 4 * g + 4)
                if i >= 2:
                    dve.wait_ge(pe_block, BLOCK["t5", i - 2, 1])
                for h in (0, 2, 1, 3):
                    blk = ("s5", i, h % 2)
                    dve.wait_ge(pe_block, BLOCK[blk])
                    src = psum[bank_of(blk)][:, (h // 2) * 256 + k0:(h // 2) * 256 + 256]
                    V.tensor_tensor_reduce(prob2(i)[:, h, k0:256], src, bias2(g)[:, h, k0:256], 1.0,
                                           sinks[:, 4 * g + h:4 * g + h + 1], ALU.add, ALU.max, mx[:, h:h + 1])\
                        .then_inc(s5_scored, 1)
                dve.wait_ge(s5_scored, 4 * i + 4)
                V.tensor_scalar(nmx[:, :], mx[:, :], -1.0, None, ALU.mult).then_inc(neg5, 1)
                dve.wait_ge(neg5, i + 1)
                V.tensor_tensor(den[:, :], sinks[:, 4 * g:4 * g + 4], nmx[:, :], ALU.add).then_inc(sink5, 1)

            def probs2(i):
                g, b = STEPS2[i]
                k0 = 0 if b else P
                dve.wait_ge(exp5, 5 * i + 5)
                V.tensor_tensor(den[:, :], rs[:, :], esk[:, :], ALU.add).then_inc(den5, 1)
                dve.wait_ge(den5, i + 1)
                V.reciprocal(rr[:, :], den[:, :]).then_inc(rec5, 1)
                dve.wait_ge(rec5, i + 1)
                for h in range(4):
                    pr = prob2(i)[:, h, k0:256]
                    V.tensor_scalar(pr, pr, rr[:, h:h + 1], None, ALU.mult).then_inc(prob5, 1)

            dve.wait_ge(dist_made, 4)
            for i in range(SLOTS2 + 2):
                if i < 16:
                    scores2(i)
                for f in (f for s, f in DONE2.get(i - 1, ()) if s == "z5"):
                    dve.wait_ge(z5_tanh, f + 1)
                    V.scalar_tensor_tensor(zg[:, f, :], th[:, :], 1.0, psum[bank_of(("F", "z5", f))][:, :], ALU.add,
                                           ALU.mult).then_inc(z5_gated, 1)
                for f in (f for f in MEET2 if MEET2[f] == i - 1):
                    dve.wait_ge(hi["y5"], f + 1)
                    V.tensor_tensor(actA_lo[:, f, :], acc[:, f % 2, :], actA_hi[:, f, :].bitcast(f32),
                                    ALU.subtract).then_inc(lo["y5"], 1)
                for f in (f for f in MEET2 if MEET2[f] == i):
                    if f >= 2:
                        dve.wait_ge(lo["y5"], f - 1)
                    dve.wait_ge(z5_gated, f + 1)
                    dve.wait_ge(o5_copied, 8 * (f // 2 + 1))
                    V.scalar_tensor_tensor(acc[:, f % 2, :], zg[:, f, :], 0.5, q5(f), ALU.mult, ALU.mult)\
                        .then_inc(y5_made, 1)
                if 1 <= i < 17:
                    b = ("t5", i - 1, 1)
                    dve.wait_ge(pe_block, BLOCK[b])
                    V.tensor_copy(prT2(1), psum[bank_of(b)][:, :]).then_inc(pt1_copied, 1)
                if i < 16:
                    probs2(i)
            dve.wait_ge(bpost_in, 16)
            for t in range(T):
                post("f", f_scaled, t, 1, out_ready)

        @block.tensor
        def _(pe):
            M = nc.tensor.matmul

            def exact(out_, whi_, wlo_, xhi_, xlo_, start, stop):
                M(out_, whi_, xhi_, start=start, stop=False)
                M(out_, whi_, xlo_, start=False, stop=False)
                return M(out_, wlo_, xhi_, start=False, stop=stop)

            def weights_of(stage, j, first_half=False):
                n = UNIT_NO[stage, j]
                pe.wait_ge(w_lo, 2 * n + (1 if first_half else 2))
                return whi[:, SLOT[n], :], wlo[:, SLOT[n], :]

            def feature_major(kind, stage, f):
                H, L = weights_of(stage, f // 2)
                aH, aL = READS[stage]
                tokens = slice(0, S)
                if stage == "k5":
                    tokens = slice(0, S // 2) if kind == "Fa" else slice(S // 2, S)
                aH, aL = aH[:, :, tokens], aL[:, :, tokens]
                out_ = psum[bank_of(("F", stage, f))][:, tokens]
                first, last = (0, KD // 2) if kind == "Fk" else (KD // 2 * ((stage, f) in JOBS2), KD)
                for k in range(first, last):
                    c = slice(k * 256 + (f % 2) * P, k * 256 + (f % 2) * P + P)
                    ins = exact(out_, H[:, c], L[:, c], aH[:, k, :], aL[:, k, :], k == 0, k == KD - 1)
                return ins

            def token_major(stage, c, kh, t, head=False):
                first = HEADS.get((stage, c, kh), 0)
                H, L = weights_of(stage, 2 * c + kh, head and first <= 2)
                aH, aL = READS[stage]
                bank = bank_of(("T", stage, c, kh, t))
                rows = slice(t * P, (t + 1) * P)
                for k in range(first) if head else range(first, 4):
                    w = slice(k * HALF, (k + 1) * HALF)
                    a = 4 * kh + k
                    ins = exact(psum[bank][:, :], aH[:, a, rows], aL[:, a, rows], H[:, w], L[:, w],
                                kh == 0 and k == 0, kh == 1 and k == 3)
                return ins

            def turn(name, t, j):
                bank = psum[bank_of(("tr", name, t, j))]
                for k in range(4):
                    if name == "p":
                        src = ptok[:, k * PLE + j * P:k * PLE + (j + 1) * P]
                    elif name == "x1":
                        src = resid[:, t, (4 * j + k) * P:(4 * j + k + 1) * P]
                    else:
                        src = tok[:, t % 2, (4 * j + k) * P:(4 * j + k + 1) * P]
                    ins = nc.tensor.transpose(bank[:, k * P:(k + 1) * P], src, ident[:, :])
                return ins

            def ready(b):
                kind = b[0]
                if kind == "tr":
                    name, t, j = b[1:]
                    if name == "p":
                        pe.wait_ge(p_in, 16)
                    elif name == "x1":
                        pe.wait_ge(x1_ready, t + 1)
                    else:
                        pe.wait_ge(tok_ready[name], t + 1)
                    return
                s = b[1]
                if kind in ("F", "Fa"):
                    if s == "q":
                        pe.wait_ge(lo["x"], 2 * T)
                    if s == "k5":
                        pe.wait_ge(lo["n"], T if kind == "Fa" else 2 * T)
                if kind in ("T", "Th"):
                    c, kh, t = b[2:]
                    if s == "v":
                        pe.wait_ge(lo["x"], 2 * t + 1 + kh)
                    if s == "wo":
                        pe.wait_ge(*((lo["attn"], NH1 - (kind == "Th")) if kh == 0 else (lo["conv"], 4)))
                    if s in ("gate", "v4"):
                        pe.wait_ge(lo["x1" if s == "gate" else "h"], 2 * (t + 1))
                    if s in ("a0", "a1"):
                        pe.wait_ge(lo["y4"], KD * int(s[1]) + 4 * (kh + 1))
                    if s == "f":
                        pe.wait_ge(lo["y5"], 4 * (kh + 1))
                if kind == "ple":
                    pe.wait_ge(lo["p"], 2)
                if kind == "v5":
                    pe.wait_ge(lo["n"], 2 * (s + 1))
                if kind == "sc":
                    pe.wait_ge(k_copied, s // 4 + 1)
                if kind == "tw":
                    pe.wait_ge(weighed, s + 1)
                if kind == "pv":
                    pe.wait_ge(wt_copied, s + 1)
                    if s:
                        pe.wait_ge(attn_sq, s)
                    pe.wait_ge(v_copied, T)
                if kind == "ta":
                    pe.wait_ge(attn_normed, s + 1)
                if kind == "wt":
                    pe.wait_ge(ws_masked, 1)
                if kind == "rw":
                    pe.wait_ge(wct_copied, 2)
                if kind == "s4":
                    pe.wait_ge(v_normed, T)
                if kind == "s5":
                    pe.wait_ge(q5_copied, 2 * (s // 4) + 2)
                    pe.wait_ge(k5_copied, 8)
                if kind == "t5":
                    pe.wait_ge(prob5, 4 * (s + 1))
                if kind == "o5":
                    pe.wait_ge(pt1_copied, s + 1)
                    if STEPS2[s][1]:
                        pe.wait_ge(pt0_copied, kt0_steps(s))

            def work(b):
                kind = b[0]
                bank = psum[bank_of(b)]
                if kind == "tr":
                    return turn(*b[1:])
                if kind in ("F", "Fa", "Fk"):
                    return feature_major(*b)
                if kind in ("T", "Th"):
                    return token_major(*b[1:], head=kind == "Th")
                if kind == "sc":
                    i, m = b[1:]
                    h, qt = STEPS1[i]
                    rows = slice(m * DQK1, (m + 1) * DQK1)
                    n = (qt + 1) * P
                    return M(bank[:, 0:n], tile(qT, h)[rows, qt * P:(qt + 1) * P], tile(kT, h)[rows, 0:n],
                             start=True, stop=True)
                if kind == "tw":
                    for k in range(STEPS1[b[1]][1] + 1):
                        c = slice(k * P, (k + 1) * P)
                        ins = nc.tensor.transpose(bank[:, c], wgt1[:, c], ident[:, :])
                    return ins
                if kind == "pv":
                    h, qt = STEPS1[b[1]]
                    for k in range(qt + 1):
                        ins = M(bank[:, qt * P:(qt + 1) * P], wgtT1[:, k * P:(k + 1) * P],
                                tile(vtok, k)[:, h * P:(h + 1) * P], start=k == 0, stop=k == qt)
                    return ins
                if kind == "ta":
                    for k in range(T):
                        c = slice(k * P, (k + 1) * P)
                        ins = nc.tensor.transpose(bank[:, c], tile(qT, b[1])[:, c], ident[:, :])
                    return ins
                if kind == "ple":
                    t, c = b[1:]
                    H, L = weights_of("ple", 0)
                    rows = slice(t * P, (t + 1) * P)
                    for k in range(2):
                        w = slice(k * D + c * HALF, k * D + (c + 1) * HALF)
                        ins = exact(bank[:, :], actA_hi[:, k, rows], actA_lo[:, k, rows], H[:, w], L[:, w],
                                    k == 0, k == 1)
                    return ins
                if kind == "wt":
                    for k in range(4):
                        g = 4 * b[1] + k
                        ins = nc.tensor.transpose(bank[:, k * P:(k + 1) * P], wsr[:, g * P:(g + 1) * P], ident[:, :])
                    return ins
                if kind == "rw":
                    return M(bank[:, :], ones[:, :], wcT[:, b[1] * HALF:(b[1] + 1) * HALF], start=True, stop=True)
                if kind == "s4":
                    f = b[1]
                    for n in range(T):
                        ins = M(bank[:, n * P:(n + 1) * P], big[:, n, f * P:(f + 1) * P],
                                wcT[:, (f // 2) * P:(f // 2 + 1) * P], start=True, stop=True)
                    return ins
                if kind == "v5":
                    t = b[1]
                    n = UNIT_NO["v5", 0]
                    pe.wait_ge(w_lo, 2 * n + 2)
                    rows = slice(t * P, (t + 1) * P)
                    for k in range(KD):
                        H, L = halves_of(n, k // 2)
                        w = slice((k % 2) * 256, (k % 2 + 1) * 256)
                        ins = exact(bank[:, 0:256], actB_hi[:, k, rows], actB_lo[:, k, rows], H[:, w], L[:, w],
                                    k == 0, k == KD - 1)
                    return ins
                if kind == "s5":
                    i, m = b[1:]
                    g, blk = STEPS2[i]
                    k0 = 0 if blk else P
                    keys = slice((blk - 1) * P + k0, (blk + 1) * P)
                    rows = slice(m * DH, (m + 1) * DH)
                    for j in range(2):
                        ins = M(bank[:, j * 256 + k0:(j + 1) * 256], q5(2 * g + j)[rows, blk * P:(blk + 1) * P],
                                kdup(g)[rows, keys], start=True, stop=True)
                    return ins
                if kind == "t5":
                    i, kt = b[1:]
                    for h in range(4):
                        ins = nc.tensor.transpose(bank[:, h * P:(h + 1) * P],
                                                  prob2(i)[:, h, kt * P:(kt + 1) * P], ident[:, :])
                    return ins
                if kind == "o5":
                    g, blk = STEPS2[b[1]]
                    kts = (0, 1) if blk else (1,)
                    for kt in kts:
                        v = v5(blk - 1 + kt)[:, g, :, :].rearrange("p d e -> p (d e)")
                        ins = M(bank[:, :], v, prT2(kt), start=kt == kts[0], stop=kt == 1)
                    return ins

            pe.wait_ge(ident_made, 1)
            pe.wait_ge(ones_made, 1)
            for b in ORDER:
                if BEFORE.get(b) is not None:
                    pe.wait_ge(*emptied(BEFORE[b]))
                ready(b)
                work(b).then_inc(pe_block, 1)


_INS = ["x", "p", "pre_norm_gain", "w_in", "lambda_q1", "lambda_k1", "lambda_q2", "lambda_k2",
        "subln_gain", "conv_w", "w_out", "post_norm_gain", "w_ple_proj", "ple_norm_gain", "w_ple_gate",
        "a_w_in_2", "a_ln_g_2", "a_ln_b_2", "a_w_s_2", "a_b_s_2", "a_w_out_2", "a_pre_g_2",
        "a_post_g_2", "kv_norm_g_2", "w_k_2", "w_v_2", "b_w_in_2", "b_sinks_2", "b_w_out_2",
        "b_pre_g_2", "b_post_g_2"]


def kernel(**inputs):
    import numpy as np
    import concourse.bacc as bacc
    from concourse.bass_utils import run_bass_kernel_spmd

    nc = bacc.Bacc("TRN2", target_bir_lowering=False, num_devices=1)
    arrays, args = {}, []
    for name in _INS:
        a = np.ascontiguousarray(inputs[name])
        arrays[f"in_{name}"] = a
        args.append(nc.dram_tensor(f"in_{name}", a.shape, mybir.dt.from_np(a.dtype), kind="ExternalInput").ap())
    args.append(nc.dram_tensor("out_dram", (1, S, D), mybir.dt.float32, kind="ExternalOutput").ap())
    program(nc, *args)
    r = run_bass_kernel_spmd(nc, [arrays], core_ids=[0])
    return r.results[0]["out_dram"]
```

```python
import math
from contextlib import ExitStack

import concourse.bass as bass
from concourse import mybir

P = 128
S = 512
T = S // P
D = 1024
KD = D // P
HALF = 512
NH1, DV1, DQK1 = 4, 128, 64
LAM_INIT = 0.8 - 0.6 * math.exp(0.0)
AW = 2048
KA = AW // P
NG = 8
NQ, NKV, DH = 16, 4, 64
PLE = 256
EPS, SUBLN_EPS = 1e-6, 1e-5
MASKED = 1e30
SLOPE1 = [2.0 ** (-8.0 * (h + 1) / NH1) for h in range(NH1)]
SLOPE2 = [2.0 ** (-8.0 * (h + 1) / NQ) for h in range(NQ)]
UNIT = 2048
RAW = UNIT // 2


def weight_units():
    u = []
    part = lambda n: n * 512
    u += [("v", kh, "T", "w_in", 4 * kh, part(2)) for kh in range(2)]
    for stage, n in (("q", 0), ("k", 1)):
        u += [(stage, j, "F", "w_in", 0, part(n) + 256 * j) for j in range(2)]
    u += [("za", j, "F", "w_in", 0, part(3) + 256 * j) for j in range(2)]
    for j in range(2):
        for stage, n in (("c", 5), ("u", 6), ("b", 4), ("zc", 7)):
            u += [(stage, j, "F", "w_in", 0, part(n) + 256 * j)]
    u += [("wo", 2 * c + kh, "T", "w_out", 4 * kh, 512 * c) for c in range(2) for kh in range(2)]
    u += [("ple", 0, "P", "w_ple_proj", 0, 0)]
    u += [("gate", 2 * c + kh, "T", "w_ple_gate", 4 * kh, 512 * c) for c in range(2) for kh in range(2)]
    u += [("v4", 2 * c + kh, "T", "a_w_in_2", 4 * kh, AW + 512 * c) for c in range(4) for kh in range(2)]
    for half in range(2):
        for j in range(4 * half, 4 * half + 4):
            u += [("z4", j, "F", "a_w_in_2", 0, 2 * AW + 256 * j), ("u4", j, "F", "a_w_in_2", 0, 256 * j)]
        u += [(f"a{half}", 2 * c + kh, "T", "a_w_out_2", 8 * half + 4 * kh, 512 * c)
              for c in range(2) for kh in range(2)]
    u += [("v5", 0, "F", "w_v_2", 0, 0), ("k5", 0, "F", "w_k_2", 0, 0)]
    for stage, j in (("q5", 0), ("q5", 1), ("z5", 0), ("q5", 2), ("z5", 1), ("q5", 3), ("z5", 2), ("z5", 3)):
        u += [(stage, j, "F", "b_w_in_2", 0, 1024 * (stage == "z5") + 256 * j)]
    u += [("f", 2 * c + kh, "T", "b_w_out_2", 4 * kh, 512 * c) for c in range(2) for kh in range(2)]
    return u


UNITS = weight_units()
SLOTTED = [n for n, u in enumerate(UNITS) if u[0] != "v5"]
SLOT = {n: k % 2 for k, n in enumerate(SLOTTED)}
SLOT_BEFORE = {n: SLOTTED[k - 2] for k, n in enumerate(SLOTTED) if k >= 2}
UNIT_NO = {(s, j): n for n, (s, j, *_) in enumerate(UNITS)}

STEPS1 = [(h, qt) for h in range(NH1) for qt in range(T)]
JOBS1 = [("za", f) for f in range(4)]
for _j in range(2):
    for _s in ("c", "u", "b", "zc"):
        JOBS1 += [(_s, 2 * _j), (_s, 2 * _j + 1)]
SLOTS1 = len(JOBS1)
STEPS2 = [(g, b) for g in range(NKV) for b in range(T)]
JOBS2 = [(s, f) for s, *fs in (("q5", 2, 3), ("z5", 0, 1), ("q5", 4, 5), ("z5", 2, 3), ("q5", 6, 7),
                               ("z5", 4, 5, 6, 7)) for f in fs]
_parts = [(kind, *job) for job in JOBS2 for kind in ("Fk", "F")]
SLOTS2 = 18
PARTS2 = {i: [_parts.pop(0) for _ in range(1 if i in (-1, 4, 8, 12) else 2)] for i in range(-1, 15)}
DONE2 = {i: [p[1:] for p in ps if p[0] == "F"] for i, ps in PARTS2.items()}
MEET2 = {f: max(4 * (f // 2) + 6 + f % 2 * (f < 6), 2 + min(i for i in DONE2 if ("z5", f) in DONE2[i])) for f in range(8)}


HEADS = {("v", 0, 0, t): 2 for t in range(T)} | {("wo", 0, 0, t): 3 for t in range(T)}
HEADS |= {("gate", 1, 1, 3): 2, ("a1", 1, 1, 2): 2, ("a1", 1, 1, 3): 2}


def tensor_order():
    o = []
    for t in range(T):
        o += [("tr", "x", t, j) for j in range(2)] + [("Th", "v", 0, 0, t)]
    o += [("T", "v", 0, kh, t) for kh in range(2) for t in range(T)]
    o += [("F", "q", f) for f in range(4)] + [("F", "k", f) for f in range(4)]
    for i in range(SLOTS1):
        if 2 <= i < 18:
            o += [("pv", i - 2)]
        if 1 <= i < 17:
            o += [("tw", i - 1)]
        if i < 16:
            o += [("sc", i, m) for m in range(2)]
        o += [("F", *JOBS1[i])]
        if i >= 6 and i % 4 == 2:
            o += [("ta", i // 4 - 1)]
    o += [("Th", "wo", 0, 0, t) for t in range(T)] + [("tr", "p", 0, k) for k in range(2)]
    o += [("T", "wo", 0, 0, t) for t in range(T)]
    o += [("T", "wo", 0, 1, t) for t in range(T)]
    o += [("T", "wo", 1, kh, t) for kh in range(2) for t in range(T)]
    for t in range(T):
        o += [("ple", t, c) for c in range(2)]
        if t:
            o += [("tr", "x1", t - 1, j) for j in range(2)]
    o += [("T", "gate", 0, 0, 0)] + [("tr", "x1", 3, j) for j in range(2)]
    o += [("T", "gate", 0, 0, t) for t in range(1, T)] + [("wt", j) for j in range(2)]
    o += [("T", "gate", 0, 1, t) for t in range(2)] + [("rw", j) for j in range(2)]
    o += [("T", "gate", 0, 1, t) for t in range(2, T)]
    turn = lambda name, t: [("tr", name, t, j) for j in range(2)]
    o += [("T", "gate", 1, 0, t) for t in range(T)] + [("T", "gate", 1, 1, t) for t in range(3)]
    o += [("Th", "gate", 1, 1, 3)] + turn("h", 0) + [("T", "gate", 1, 1, 3)] + turn("h", 1) + [("T", "v4", 0, 0, 0)]
    o += turn("h", 2) + [("T", "v4", 0, 0, 1)] + turn("h", 3) + [("T", "v4", 0, 0, t) for t in (2, 3)]
    o += [("T", "v4", 0, 1, t) for t in range(T)]
    o += [("T", "v4", c, kh, t) for c in range(1, 4) for kh in range(2) for t in range(T)]
    for half in range(2):
        for j in range(4 * half, 4 * half + 4):
            o += [("F", s, 2 * j + f) for s in ("z4", "u4") for f in range(2)]
            o += [("s4", 2 * j + f) for f in range(2)]
        o += [("T", f"a{half}", c, kh, t) for c in range(2 - half) for kh in range(2) for t in range(T)]
    o += [("T", "a1", 1, 0, t) for t in (0, 1, 2)] + [("T", "a1", 1, 1, t) for t in (0, 1)] + [("T", "a1", 1, 0, 3)]
    o += [("Th", "a1", 1, 1, 2)] + turn("n", 0) + [("T", "a1", 1, 1, 2), ("Th", "a1", 1, 1, 3)]
    o += turn("n", 1) + [("T", "a1", 1, 1, 3)]
    o += [("v5", 0), ("v5", 1), ("Fa", "k5", 0)] + turn("n", 2) + [("Fa", "k5", 1)] + turn("n", 3)
    o += [("v5", 2), ("v5", 3)] + [("F", "k5", f) for f in range(2)] + [("F", "q5", f) for f in range(2)]
    for i in range(SLOTS2):
        if i == 17:
            o += [("T", "f", 0, 0, 0)]
        if 2 <= i < 18:
            o += [("o5", i - 2)]
        if 1 <= i < 17:
            o += [("t5", i - 1, kt) for kt in ((0, 1) if STEPS2[i - 1][1] else (1,))]
        if i == 0:
            o += PARTS2[-1]
        if i < 16:
            o += [("s5", i, m) for m in range(2)]
        o += PARTS2.get(i, [])
        if i == 15:
            o += [("T", "f", 0, 0, t) for t in (1, 2)]
    o += [("T", "f", 0, 0, 3)] + [("T", "f", 0, 1, t) for t in range(T)]
    o += [("T", "f", 1, kh, t) for kh in range(2) for t in range(T)]
    return o


ORDER = tensor_order()
BLOCK = {b: n + 1 for n, b in enumerate(ORDER)}


def bank_of(b):
    kind = b[0]
    if kind == "tr":
        name, t, j = b[1:]
        return {"x": (2 * t + j) % 4, "p": 4 + j, "x1": t + 4 * j, "h": (2 * t + j) % 4,
                "n": (2 * t + j) % 4}[name]
    if kind in ("F", "Fa", "Fk"):
        s, f = b[1:]
        if s in ("z4", "u4"):
            return 4 * (f // 2 % 2) + f % 2 + 2 * (s == "u4")
        if s == "k5":
            return 6 + f
        if s in ("q5", "z5"):
            return ([("q5", 0), ("q5", 1)] + JOBS2).index((s, f)) % 3
        return [x[1:] for x in ORDER if x[0] == "F"].index((s, f)) % 4
    if kind in ("T", "Th"):
        s, c, _, t = b[1:]
        return t + 4 * (1 if s == "v" else (c + (s == "v4")) % 2)
    if kind == "s4":
        return 4 * (b[1] // 2 % 2) + b[1] % 2
    return {"sc": lambda i, m: 4 + m, "tw": lambda i: 6, "pv": lambda i: 7, "ta": lambda h: 4,
            "ple": lambda t, c: t + 4 * c, "wt": lambda j: 4 + j, "rw": lambda j: 6 + j,
            "v5": lambda t: 4 + t % 2, "s5": lambda s, m: 4 + m, "t5": lambda s, kt: 6 + kt,
            "o5": lambda s: 3}[kind](*b[1:])


def opens(b):
    if b[0] == "T":
        return b[3] == 0 and b[1:] not in HEADS
    if b[0] == "Th":
        return b[3] == 0
    if b[0] == "F":
        return b[1] != "k5" and b[1:] not in JOBS2
    if b[0] == "pv":
        return STEPS1[b[1]][1] == 0
    return True


def previous_in_bank():
    last, before = {}, {}
    for b in ORDER:
        bank = bank_of(b)
        if opens(b):
            before[b] = last.get(bank)
        last[bank] = b
    return before


BEFORE = previous_in_bank()


def program(nc, x, p, pre_norm_gain, w_in, lambda_q1, lambda_k1, lambda_q2, lambda_k2, subln_gain,
            conv_w, w_out, post_norm_gain, w_ple_proj, ple_norm_gain, w_ple_gate, a_w_in_2,
            a_ln_g_2, a_ln_b_2, a_w_s_2, a_b_s_2, a_w_out_2, a_pre_g_2, a_post_g_2, kv_norm_g_2,
            w_k_2, w_v_2, b_w_in_2, b_sinks_2, b_w_out_2, b_pre_g_2, b_post_g_2, out):
    f32, f32r = mybir.dt.float32, mybir.dt.float32r
    ALU, ACT, AX = mybir.AluOpType, mybir.ActivationFunctionType, mybir.AxisListType
    MATRICES = {"w_in": w_in[0], "w_out": w_out[0], "w_ple_proj": w_ple_proj[0],
                "w_ple_gate": w_ple_gate[0], "a_w_in_2": a_w_in_2[0], "a_w_out_2": a_w_out_2[0],
                "w_v_2": w_v_2, "w_k_2": w_k_2, "b_w_in_2": b_w_in_2[0], "b_w_out_2": b_w_out_2[0]}
    ctx = ExitStack()
    with ctx:
        sb = lambda name, shape, dt=f32: ctx.enter_context(nc.sbuf_tensor(name, shape, dt))
        sem = lambda name: ctx.enter_context(nc.semaphore(name))

        raw = sb("raw", [P, 4, RAW])
        whi = sb("whi", [P, 2, UNIT], f32r)
        wlo = sb("wlo", [P, 2, UNIT], f32r)
        with nc.sbuf_tensor("zg", [P, KD, S], f32) as zg:
            pass
        actA_lo = sb("actA_lo", [P, KD, S], f32r)
        with nc.sbuf_tensor("o5", [P, KD, S], f32) as o5:
            pass
        actA_hi = sb("actA_hi", [P, KD, S], f32r)
        actB_hi, actB_lo = sb("actB_hi", [P, KD, S], f32r), sb("actB_lo", [P, KD, S], f32r)
        resid = sb("resid", [P, T, D])
        with nc.sbuf_tensor("parts", [P, 4, AW], f32r) as parts:
            pass
        big = sb("big", [P, 4, AW])
        with nc.sbuf_tensor("rests", [P, 6, HALF], f32r) as rests:
            pass
        gain = sb("gain", [P, 3, D])
        tok = sb("tok", [P, 2, D])
        acc = sb("acc", [P, 2, HALF])
        th = sb("th", [P, HALF])
        with nc.sbuf_tensor("pT1", [P, HALF], f32r) as pT1:
            pass
        junk = sb("junk", [P, HALF])
        ident, ones = sb("ident", [P, P]), sb("ones", [P, P])
        lamv, lams = sb("lamv", [P, 4, DQK1]), sb("lams", [P, 8])
        subg, convc = sb("subg", [P, 2]), sb("convc", [P, 3, 4])
        lng, lnb = sb("lng", [P, KA]), sb("lnb", [P, KA])
        kvg, bg = sb("kvg", [P, KD]), sb("bg", [P, KD])
        sinks = sb("sinks", [P, NQ])
        ss = sb("ss", [P, 8, T, 4])
        ms = sb("ms", [P, 8, T])
        rstd = sb("rstd", [P, 8, T])
        mhalf = sb("mhalf", [P, 1])
        ss_attn, ms_attn, r_attn = (sb(n, [P, NH1, T]) for n in ("ss_attn", "ms_attn", "r_attn"))
        mx, nmx, rs, rr = sb("mx", [P, 4]), sb("nmx", [P, 4]), sb("rs", [P, 4]), sb("rr", [P, 4])
        esk, den = sb("esk", [P, 4]), sb("den", [P, 4])
        vsum, nmu = sb("vsum", [P, T, 4]), sb("nmu", [P, 2, T])
        with ExitStack() as place:
            small = lambda name, shape: place.enter_context(nc.sbuf_tensor(name, shape, f32))
            smA, smB, smC = small("smA", [P, D]), small("smB", [P, D]), small("smC", [P, D])
            gcv = small("gcv", [P, 2, 2 + S])
        with ExitStack() as place:
            place.enter_context(nc.sbuf_tensor("kept", [P, 2 * D + HALF], f32))
            pT3 = place.enter_context(nc.sbuf_tensor("pT3", [P, 3, HALF], f32r))
        v5hi, v5lo = sb("v5hi", [P, UNIT], f32r), sb("v5lo", [P, UNIT], f32r)
        iot = smC[:, 0:HALF].bitcast(mybir.dt.int32)

        psum = [ctx.enter_context(nc.psum_tensor(f"bank{b}", [P, HALF], f32)) for b in range(8)]

        qT, kT, vtok, zaT = big[:, 0], big[:, 1], big[:, 2], big[:, 3]
        tile = lambda region, n: region[:, n * HALF:(n + 1) * HALF]
        q1 = lambda h, m: parts[:, m, h * HALF:(h + 1) * HALF]
        k1 = lambda h, m: (actB_hi, actB_lo)[m][:, h, :]
        k1_rest = lambda h: rests[:, h, :]
        base1 = smB[:, 0:HALF]
        bias1 = lambda h: smA[:, (h % 2) * HALF:(h % 2 + 1) * HALF]
        prob1 = lambda m: tok[:, 0, m * HALF:(m + 1) * HALF]
        wgt1, wgtT1 = tok[:, 1, 0:HALF], tok[:, 1, HALF:D]
        ptok = smC
        e_sb = lambda t: big[:, t, 0:D]
        wsr = gcv[:, :, :].rearrange("p a b -> p (a b)")[:, 0:NG * P]
        wcT, rwB, bsB = smA, smB, smC
        part_ = lambda t, c: big[:, t, c * HALF:(c + 1) * HALF]
        v5 = lambda t, part: parts[:, t, D + 256 * part:D + 256 * (part + 1)]
        khi = lambda g: parts[:, g, D + 512:D + 1024]
        klo = lambda g: rests[:, g + 2 * (g // 2), :]
        q5 = lambda f, m: parts[:, 2 * (f // 2 % 2) + f % 2, m * HALF:(m + 1) * HALF]
        bias2 = lambda g: (smA if g % 2 == 0 else smB)[:, :].rearrange("p (h k) -> p h k", h=4)
        dist2 = smC[:, 0:256]
        prob2 = lambda s: tok[:, s % 2, :].rearrange("p (h k) -> p h k", h=4)
        pThi = lambda kt: pT3[:, kt, :]
        pTlo = lambda kt: pT1[:, :] if kt else pT3[:, 2, :]


        def halves_of(n, c):
            w = slice(c * HALF, (c + 1) * HALF)
            if UNITS[n][0] == "v5":
                return v5hi[:, w], v5lo[:, w]
            return whi[:, SLOT[n], w], wlo[:, SLOT[n], w]

        ACTS = {"x": (actA_hi, actA_lo), "p": (actA_hi, actA_lo), "x1": (actA_hi, actA_lo),
                "h": (actB_hi, actB_lo), "n": (actB_hi, actB_lo)}
        READS = {**dict.fromkeys(("q", "k", "v", "za", "b", "c", "u", "zc"), (actA_hi, actA_lo)),
                 "wo": (actB_hi, actB_lo), "gate": (actA_hi, actA_lo),
                 **dict.fromkeys(("v4", "z4", "u4"), (actB_hi, actB_lo)),
                 "a0": (actA_hi, actA_lo), "a1": (actA_hi, actA_lo),
                 **dict.fromkeys(("v5", "k5", "q5", "z5"), (actB_hi, actB_lo)),
                 "f": (actA_hi, actA_lo)}

        x_in = [sem(f"x_in{t}") for t in range(T)]
        raw_in = [sem(f"raw_in{n}") for n in range(4)]
        small_in, pre_in, post_in, ple_in = sem("small_in"), sem("pre_in"), sem("post_in"), sem("ple_in")
        apre_in, apost_in, bpost_in = sem("apre_in"), sem("apost_in"), sem("bpost_in")
        p_in, ws_in, bs_in, stored = sem("p_in"), sem("ws_in"), sem("bs_in"), sem("stored")
        dve_scaled, w_scaled, w_hi, w_lo = sem("dve_scaled"), sem("w_scaled"), sem("w_hi"), sem("w_lo")
        pe_block = sem("pe_block")
        BY_HALF = ("m1", "x2", "a", "f")
        NORMS = {n: k for k, n in enumerate(("x", "m1", "e", "x2", "ln", "a", "h3", "f"))}
        squared = {n: sem(f"squared_{n}") for n in NORMS}
        ms_ready = {n: sem(f"ms_{n}") for n in NORMS}
        rstd_ready = {n: sem(f"rstd_{n}") for n in NORMS}
        tok_ready = {n: sem(f"tok_{n}") for n in ("x", "h", "n")}
        hi = {n: sem(f"hi_{n}") for n in ("x", "p", "x1", "h", "n", "conv", "attn", "y4", "y5")}
        lo = {n: sem(f"lo_{n}") for n in hi}
        ident_set, ident_made, ones_made = sem("ident_set"), sem("ident_made"), sem("ones_made")
        mhalf_made, iota_made, ws_masked = sem("mhalf_made"), sem("iota_made"), sem("ws_masked")
        pads_made = sem("pads_made")
        base_step, lam_step, lam_exp, cols_scaled = (sem("base_step"), sem("lam_step"), sem("lam_exp"),
                                                     sem("cols_scaled"))
        q1_hi, q1_lo, k1_hi, k1_lo, v_copied = (sem("q1_hi"), sem("q1_lo"), sem("k1_hi"), sem("k1_lo"),
                                                sem("v_copied"))
        za_tanh, za_gated, c_copied, g_made = sem("za_tanh"), sem("za_gated"), sem("c_copied"), sem("g_made")
        taps, b_mult, zc_tanh, zc_gated, conv_out = (sem("taps"), sem("b_mult"), sem("zc_tanh"),
                                                     sem("zc_gated"), sem("conv_out"))
        bias_made, scored, negmax, exped = sem("bias_made"), sem("scored"), sem("negmax"), sem("exped")
        recip1, lam_scaled, weighed = sem("recip1"), sem("lam_scaled"), sem("weighed")
        wt_copied, attn_copied, attn_sq = sem("wt_copied"), sem("attn_copied"), sem("attn_sq")
        msq_attn, rstd_attn, attn_normed, attn_out = (sem("msq_attn"), sem("rstd_attn"),
                                                      sem("attn_normed"), sem("attn_out"))
        post_scaled, x1_ready, e_copied, e_normed = (sem("post_scaled"), sem("x1_ready"),
                                                     sem("e_copied"), sem("e_normed"))
        wct_copied, rw_copied = sem("wct_copied"), sem("rw_copied")
        gate_tanh, gate_mult, x2_ready = sem("gate_tanh"), sem("gate_mult"), sem("x2_ready")
        v_gelu, mu_step, v_normed = sem("v_gelu"), sem("mu_step"), sem("v_normed")
        z4_tanh, z4_gated, u4_gelu, zu_made = sem("z4_tanh"), sem("z4_gated"), sem("u4_gelu"), sem("zu_made")
        s4_bias, s4_scaled, y4_made = sem("s4_bias"), sem("s4_scaled"), sem("y4_made")
        part_copied, part_added, a_gained, h3_ready = (sem("part_copied"), sem("part_added"),
                                                       sem("a_gained"), sem("h3_ready"))
        v5_hi, v5_lo, k5_hi, k5_lo, q5_hi, q5_lo = (sem("v5_hi"), sem("v5_lo"), sem("k5_hi"), sem("k5_lo"), sem("q5_hi"),
                                                 sem("q5_lo"))
        dist_made, bias2_made = sem("dist_made"), sem("bias2_made")
        s5_scored, neg5, sink5, exp5, den5, rec5, prob5 = (
            sem("s5_scored"), sem("neg5"), sem("sink5"), sem("exp5"), sem("den5"), sem("rec5"), sem("prob5"))
        pt_hi = [sem("pt0_hi"), sem("pt1_hi")]
        pt_lo = [sem("pt0_lo"), sem("pt1_lo")]
        o5_copied = sem("o5_copied")
        z5_tanh, z5_gated, y5_made = sem("z5_tanh"), sem("z5_gated"), sem("y5_made")
        f_gained, out_ready = sem("f_gained"), sem("out_ready")

        def kt0_steps(s):
            g, b = STEPS2[s]
            return 3 * g + b

        def emptied(b):
            kind = b[0]
            if kind == "tr":
                name, t, j = b[1:]
                return lo[name], (2 * t + j if name != "p" else j) + 1
            if kind == "F":
                s, f = b[1:]
                if s == "k5":
                    return k5_lo, 4 * (f + 1)
                if s == "q5":
                    return q5_lo, 2 * (f + 1)
                if s in ("q", "k"):
                    return {"q": q1_lo, "k": k1_lo}[s], 2 * (f + 1)
                return {"za": za_gated, "c": c_copied, "u": g_made,
                        "b": b_mult, "zc": zc_gated, "z4": z4_gated, "u4": u4_gelu,
                        "z5": z5_gated}[s], f + 1
            if kind == "T":
                s, c, _, t = b[1:]
                return {"v": (v_copied, t + 1), "wo": (post_scaled, 2 * t + c + 1),
                        "gate": (gate_tanh, 4 * c + t + 1), "v4": (v_gelu, 4 * c + t + 1),
                        "a0": (part_copied, 4 * c + t + 1), "a1": (part_added, 4 * c + t + 1),
                        "f": (f_gained, 4 * c + t + 1)}[s]
            a = b[1]
            if kind == "t5":
                return (pt_lo[1], a + 1) if b[2] else (pt_lo[0], kt0_steps(a))
            return {"sc": (scored, 2 * a + b[-1] + 1), "tw": (wt_copied, a + 1),
                    "pv": (attn_copied, a // 4 + 1), "ta": (attn_out, a + 1),
                    "ple": (squared["e"], 2 * a + b[-1] + 1), "wt": (wct_copied, a + 1),
                    "rw": (rw_copied, a + 1), "s4": (s4_scaled, a + 1), "v5": (v5_lo, a + 1),
                    "s5": (s5_scored, 4 * a + 2 * b[-1] + 2), "o5": (o5_copied, 2 * a + 2)}[kind]

        def last_block(n):
            s, j, kind = UNITS[n][:3]
            if kind == "P":
                return BLOCK["ple", T - 1, 1]
            if s == "v5":
                return BLOCK["v5", T - 1]
            if kind == "F":
                return BLOCK["F", s, 2 * j + 1]
            return BLOCK["T", s, j // 2, j % 2, T - 1]

        block = ctx.enter_context(nc.Block())

        @block.sync
        def _(sp):
            def load_half(n):
                s, j, kind, name, k0, c0 = UNITS[n // 2]
                if n >= 4:
                    sp.wait_ge(w_lo, n - 3)
                tiles, cols = {"F": (4, 256), "T": (2, 512), "P": (1, 1024)}[kind]
                k = k0 + tiles * (n % 2)
                src = MATRICES[name][k * P:(k + tiles) * P, c0:c0 + cols].rearrange("(k p) c -> p k c", p=P)
                dst = raw[:, n % 4, :].rearrange("p (k c) -> p k c", k=tiles)
                sp.dma_start(dst, src).then_inc(raw_in[n % 4], 16)

            spread = lambda row, n: row.to_broadcast([P, n])

            def x_load(t):
                sp.dma_start(resid[:, t], x[0, t * P:(t + 1) * P, :]).then_inc(x_in[t], 16)

            x_load(0)
            sp.dma_start(gain[:, 0], spread(pre_norm_gain[0:1, :], D)).then_inc(pre_in, 16)
            load_half(0)
            x_load(1)
            x_load(2)
            load_half(1)
            x_load(3)
            for n in (2, 3):
                load_half(n)
            for n, v in enumerate((lambda_q1, lambda_k1, lambda_q2, lambda_k2)):
                sp.dma_start(lamv[:, n], spread(v[0:1, :], DQK1)).then_inc(small_in, 16)
            sp.dma_start(sinks[:, :], spread(b_sinks_2[0:1, :], NQ)).then_inc(small_in, 16)
            with nc.allow_non_contiguous_dma(reason="columns of gains, a few KB"):
                sp.dma_start(subg[:, 0:1], subln_gain[0].rearrange("(p a) -> p a", a=1)).then_inc(small_in, 16)
                for j in range(3):
                    sp.dma_start(convc[:, j], conv_w[0, j].rearrange("(f p) -> p f", p=P)).then_inc(small_in, 16)
                for dst, src in ((lng, a_ln_g_2[0]), (lnb, a_ln_b_2[0]), (kvg, kv_norm_g_2), (bg, b_pre_g_2[0])):
                    sp.dma_start(dst[:, :], src.rearrange("(f p) -> p f", p=P)).then_inc(small_in, 16)

            def p_load():
                sp.wait_ge(base_step, 1)
                sp.dma_start(ptok[:, :].rearrange("p (t c) -> p t c", t=T),
                             p[0, 0].rearrange("(t p) c -> p t c", p=P)).then_inc(p_in, 16)

            def gain_loads():
                sp.wait_ge(pe_block, BLOCK["sc", 15, 1])
                sp.dma_start(gain[:, 1], spread(post_norm_gain[0:1, :], D)).then_inc(post_in, 16)
                sp.dma_start(gain[:, 2], spread(ple_norm_gain[0:1, :], D)).then_inc(ple_in, 16)
                sp.dma_start(gain[:, 0], spread(a_pre_g_2[0:1, :], D)).then_inc(apre_in, 16)

            def ws_load():
                sp.wait_ge(conv_out, 4)
                sp.dma_start(wsr.rearrange("t (g s) -> t g s", g=NG),
                             a_w_s_2[0].rearrange("g t s -> t g s")).then_inc(ws_in, 16)

            def bs_load():
                sp.wait_ge(pe_block, BLOCK["tr", "p", 0, 1])
                sp.dma_start(bsB[:, :], spread(a_b_s_2[0:1].rearrange("a g t -> a (g t)"), NG * P))\
                  .then_inc(bs_in, 16)

            def apost_load():
                sp.wait_ge(e_normed, T)
                sp.dma_start(gain[:, 2], spread(a_post_g_2[0:1, :], D)).then_inc(apost_in, 16)

            def bpost_load():
                sp.wait_ge(x1_ready, T)
                sp.dma_start(gain[:, 1], spread(b_post_g_2[0:1, :], D)).then_inc(bpost_in, 16)

            late = {UNIT_NO["wo", 0]: gain_loads, UNIT_NO["za", 0]: p_load, UNIT_NO["wo", 3]: ws_load,
                    UNIT_NO["ple", 0]: bs_load, UNIT_NO["v4", 2]: apost_load, UNIT_NO["v4", 4]: bpost_load}
            for n in range(4, 2 * len(UNITS)):
                if n % 2 == 0 and n // 2 in late:
                    late[n // 2]()
                load_half(n)
            for t in range(T):
                for c in range(2):
                    half = slice(c * HALF, (c + 1) * HALF)
                    sp.wait_ge(out_ready, 2 * t + c + 1)
                    sp.dma_start(out[0, t * P:(t + 1) * P, half], resid[:, t, half]).then_inc(stored, 16)
            sp.wait_ge(stored, 2 * 16 * T)

        @block.gpsimd
        def _(pool):
            pool.memset(ident[:, :], 0.0).then_inc(ident_set, 1)
            pool.memset(mhalf[:, :], -0.5).then_inc(mhalf_made, 1)
            pool.memset(ones[:, :], 1.0).then_inc(ones_made, 1)
            pool.wait_ge(ident_set, 1)
            pool.affine_select(out=ident[:, :], in_=ident[:, :], compare_op=ALU.not_equal, fill=1.0,
                               base=0, pattern=[[-1, P]], channel_multiplier=1).then_inc(ident_made, 1)
            pool.iota(iot, pattern=[[-1, HALF]], base=HALF - P, channel_multiplier=1).then_inc(iota_made, 1)
            pool.wait_ge(mhalf_made, 1)

            def root(name, t, width):
                n = NORMS[name]
                count = T + t + 1 if name in BY_HALF else t + 1 if name == "ln" else 2 * (t + 1)
                pool.wait_ge(squared[name], count)
                m = ms[:, n, t:t + 1]
                if name == "ln":
                    pool.tensor_scalar(m, ss[:, n, t, 0:1], 1.0 / width, EPS, ALU.mult, ALU.add)\
                        .then_inc(ms_ready[name], 1)
                else:
                    pool.tensor_scalar(m, ss[:, n, t, 0:1], ss[:, n, t, 1:2], EPS, ALU.add,
                                       ALU.add).then_inc(ms_ready[name], 1)
                pool.wait_ge(ms_ready[name], t + 1)
                pool.tensor_tensor(rstd[:, n, t:t + 1], m, mhalf[:, 0:1], ALU.pow).then_inc(rstd_ready[name], 1)

            def root_attn(h):
                pool.wait_ge(attn_sq, 4 * h + 4)
                pool.tensor_scalar(ms_attn[:, h, :], ss_attn[:, h, :], 1.0 / DV1, SUBLN_EPS, ALU.mult, ALU.add)\
                    .then_inc(msq_attn, 1)
                pool.wait_ge(msq_attn, h + 1)
                pool.tensor_tensor(r_attn[:, h, :], ms_attn[:, h, :], mhalf[:, 0:1].to_broadcast([P, T]), ALU.pow)\
                    .then_inc(rstd_attn, 1)

            scaled = [0]

            def split_half(n):
                u = n // 2
                s, kind = UNITS[u][0], UNITS[u][2]
                src = raw[:, n % 4, :]
                pool.wait_ge(raw_in[n % 4], 16 * (n // 4 + 1))
                by_dve = 0 <= n - 2 * UNIT_NO["v5", 0] < 8
                if by_dve:
                    pool.wait_ge(dve_scaled, 4 * (n - 2 * UNIT_NO["v5", 0] + 1))
                if s in ("q5", "z5") and not by_dve:
                    pool.wait_ge(small_in, 16 * 13)
                    for k in range(4):
                        pool.tensor_scalar(src[:, k * 256:(k + 1) * 256], src[:, k * 256:(k + 1) * 256],
                                           bg[:, 4 * (n % 2) + k:4 * (n % 2) + k + 1], 1.0, ALU.mult,
                                           ALU.mult).then_inc(w_scaled, 1)
                    scaled[0] += 4
                    pool.wait_ge(w_scaled, scaled[0])
                if u in SLOT_BEFORE:
                    pool.wait_ge(pe_block, last_block(SLOT_BEFORE[u]))
                if s == "v5":
                    pool.wait_ge(pe_block, BLOCK["s4", KA - 1])
                    pool.wait_ge(s4_bias, KA)
                    pool.wait_ge(zu_made, KA)
                for i in range(2):
                    H, _ = halves_of(u, 2 * (n % 2) + i)
                    pool.tensor_scalar(H, src[:, i * HALF:(i + 1) * HALF], 1.0, 1.0,
                                       ALU.mult, ALU.mult).then_inc(w_hi, 1)
                for f in after.get(n - 0.5, ()):
                    f()
                for i in range(2):
                    H, L = halves_of(u, 2 * (n % 2) + i)
                    pool.wait_ge(w_hi, 2 * n + i + 1)
                    ins = pool.tensor_tensor(L, src[:, i * HALF:(i + 1) * HALF], H.bitcast(f32), ALU.subtract)
                ins.then_inc(w_lo, 1)

            def mask_ws():
                pool.wait_ge(ws_in, 16)
                w = wsr.rearrange("t (g s) -> t g s", g=NG)
                pool.affine_select(out=w, in_=w, compare_op=ALU.is_ge, fill=0.0, base=0,
                                   pattern=[[0, NG], [-1, P]], channel_multiplier=1).then_inc(ws_masked, 1)

            def make_dist():
                pool.wait_ge(pe_block, BLOCK["v5", T - 1])
                pool.iota(smC[:, 256:512].bitcast(mybir.dt.int32), pattern=[[-1, 256]], base=P,
                          channel_multiplier=1).then_inc(dist_made, 1)
                pool.wait_ge(dist_made, 1)
                pool.tensor_copy(dist2, smC[:, 256:512].bitcast(mybir.dt.int32)).then_inc(dist_made, 1)
                pool.wait_ge(dist_made, 2)
                pool.affine_select(out=dist2, in_=dist2, compare_op=ALU.is_ge, fill=MASKED, base=P,
                                   pattern=[[-1, 256]], channel_multiplier=1).then_inc(dist_made, 1)
                pool.wait_ge(dist_made, 3)
                pool.affine_select(out=dist2, in_=dist2, compare_op=ALU.is_ge, fill=MASKED, base=-1,
                                   pattern=[[1, 256]], channel_multiplier=-1).then_inc(dist_made, 1)

            root("x", 0, D)
            after = {}
            at = lambda s, j, h: 2 * UNIT_NO[s, j] + h
            for h in range(NH1):
                after[2 * (UNIT_NO["za", 0] + 2 * h + 3) + 1] = [lambda h=h: root_attn(h)]
            after[0] = [lambda: root("x", 1, D), lambda: root("x", 2, D)]
            after[1] = [lambda: root("x", 3, D)]
            after[at("ple", 0, 0)] = [lambda: root("m1", 0, D)]
            after[at("ple", 0, 1)] = [lambda t=t: root("m1", t, D) for t in range(1, T)]
            after[at("gate", 1, 0)] = [lambda t=t: root("e", t, D) for t in range(T)]
            after[at("gate", 0, 1)] = [mask_ws]
            after[at("v4", 0, 1) - 0.5] = [lambda: root("x2", 0, D)]
            after[at("v4", 0, 1)] = [lambda t=t: root("x2", t, D) for t in range(1, T)]
            after[at("u4", 0, 1)] = [lambda t=t: root("ln", t, AW) for t in range(T)]
            after[at("q5", 1, 0)] = [make_dist]
            after[at("v5", 0, 0)] = [lambda: root("a", 0, D)]
            after[at("v5", 0, 1) - 0.5] = [lambda: root("h3", 0, D), lambda: root("a", 1, D)]
            after[at("v5", 0, 1)] = [lambda: root("h3", 1, D)]
            after[at("k5", 0, 0)] = [lambda: root("a", 2, D)]
            after[at("k5", 0, 1)] = [lambda: root("h3", 2, D), lambda: root("a", 3, D), lambda: root("h3", 3, D)]
            for n in range(2 * len(UNITS)):
                split_half(n)
                for f in after.get(n, ()):
                    f()
            for t in range(T):
                root("f", t, D)

        @block.scalar
        def _(act):
            A = nc.scalar.activation

            last_square = []

            def square(name, t, c, src):
                if last_square:
                    act.wait_ge(*last_square)
                value = T * c + t + 1 if name in BY_HALF else 2 * t + c + 1
                last_square[:] = squared[name], value
                A(junk[:, :], src, ACT.Square, scale=1.0 / 32, accum_out=ss[:, NORMS[name], t, c:c + 1])\
                    .then_inc(squared[name], 1)

            def turned(name, t, j):
                b = ("tr", name, t, j)
                act.wait_ge(pe_block, BLOCK[b])
                bank = psum[bank_of(b)][:, :]
                if name == "p":
                    A(actA_hi[:, j, :], bank, ACT.Copy).then_inc(hi[name], 1)
                else:
                    A(ACTS[name][0][:, 4 * j:4 * j + 4, t * P:(t + 1) * P],
                      bank.rearrange("p (k c) -> p k c", k=4), ACT.Copy).then_inc(hi[name], 1)

            def square_x(t):
                act.wait_ge(x_in[t], 16)
                for c in range(2):
                    square("x", t, c, resid[:, t, c * HALF:(c + 1) * HALF])

            square_x(0)
            square_x(1)
            for t in range(T):
                for j in range(2):
                    turned("x", t, j)
                if t == 0:
                    square_x(2)
                    square_x(3)
            act.wait_ge(lam_step, 2)
            A(lams[:, 2:4], lams[:, 0:2], ACT.Exp).then_inc(lam_exp, 1)
            for t in range(T):
                b = ("T", "v", 0, 1, t)
                act.wait_ge(pe_block, BLOCK[b])
                A(tile(vtok, t), psum[bank_of(b)][:, :], ACT.Copy).then_inc(v_copied, 1)
            for f in range(4):
                act.wait_ge(pe_block, BLOCK["F", "q", f])
                for m in range(2):
                    rows = slice(m * DQK1, (m + 1) * DQK1)
                    A(q1(f, m)[rows, :], psum[bank_of(("F", "q", f))][rows, :], ACT.Copy, scale=DQK1 ** -0.5)\
                        .then_inc(q1_hi, 1)
            for f in range(4):
                act.wait_ge(pe_block, BLOCK["F", "k", f])
                for m in range(2):
                    for half in range(2):
                        A(k1(f, m)[half * DQK1:(half + 1) * DQK1, :],
                          psum[bank_of(("F", "k", f))][m * DQK1:(m + 1) * DQK1, :], ACT.Copy).then_inc(k1_hi, 1)

            def job_out(i):
                s, f = JOBS1[i]
                act.wait_ge(pe_block, BLOCK["F", s, f])
                bank = psum[bank_of(("F", s, f))][:, :]
                if s == "za":
                    if f:
                        act.wait_ge(za_gated, f)
                    A(th[:, :], bank, ACT.Tanh, scale=0.5).then_inc(za_tanh, 1)
                if s == "c":
                    act.wait_ge(pads_made, 1)
                    if f >= 2:
                        act.wait_ge(conv_out, f - 1)
                    A(gcv[:, f % 2, 2:2 + S], bank, ACT.Copy).then_inc(c_copied, 1)
                if s == "zc":
                    act.wait_ge(za_gated, 4)
                    if f:
                        act.wait_ge(zc_gated, f)
                    A(th[:, :], bank, ACT.Tanh, scale=0.5).then_inc(zc_tanh, 1)

            def conv_hi(i):
                s, f = JOBS1[i]
                if s == "zc":
                    act.wait_ge(conv_out, f + 1)
                    A(actB_hi[:, 4 + f, :], acc[:, f % 2, :], ACT.Copy).then_inc(hi["conv"], 1)

            for i in range(SLOTS1 + 2):
                if 1 <= i <= SLOTS1:
                    job_out(i - 1)
                if 2 <= i:
                    conv_hi(i - 2)
                if 1 <= i < 17:
                    h, qt = STEPS1[i - 1]
                    b = ("tw", i - 1)
                    act.wait_ge(pe_block, BLOCK[b])
                    n = (qt + 1) * P
                    A(wgtT1[:, 0:n], psum[bank_of(b)][:, 0:n], ACT.Copy).then_inc(wt_copied, 1)
                if 2 <= i < 18:
                    h, qt = STEPS1[i - 2]
                    act.wait_ge(pe_block, BLOCK["pv", i - 2])
                    act.wait_ge(attn_sq, i - 2) if i > 2 else act.wait_ge(*last_square)
                    A(junk[:, 0:P], psum[7][:, qt * P:(qt + 1) * P], ACT.Square,
                      accum_out=ss_attn[:, h, qt:qt + 1]).then_inc(attn_sq, 1)
                    if qt == 3:
                        A(tile(qT, h), psum[7][:, :], ACT.Copy).then_inc(attn_copied, 1)
                if i < 16:
                    h, qt = STEPS1[i]
                    n = (qt + 1) * P
                    act.wait_ge(negmax, i + 1)
                    for m in range(2):
                        A(prob1(m)[:, 0:n], prob1(m)[:, 0:n], ACT.Exp, bias=nmx[:, m:m + 1],
                          accum_out=rs[:, m:m + 1]).then_inc(exped, 1)
                if i >= 7 and i % 4 == 3:
                    h = i // 4 - 1
                    act.wait_ge(attn_out, h + 1)
                    A(actB_hi[:, h, :], tile(kT, h), ACT.Copy).then_inc(hi["attn"], 1)
            last_square[:] = attn_sq, 16
            for c in range(2):
                if c == 0:
                    for k in range(2):
                        turned("p", 0, k)
                for t in range(T):
                    act.wait_ge(pe_block, BLOCK["T", "wo", c, 1, t])
                    square("m1", t, c, psum[t + 4 * c][:, :])

            def ple_out(t):
                for c in range(2):
                    b = ("ple", t, c)
                    act.wait_ge(pe_block, BLOCK[b])
                    A(e_sb(t)[:, c * HALF:(c + 1) * HALF], psum[bank_of(b)][:, :], ACT.Copy).then_inc(e_copied, 1)
                    square("e", t, c, psum[bank_of(b)][:, :])

            for t in range(T):
                ple_out(t)
                if t:
                    for j in range(2):
                        turned("x1", t - 1, j)
            for j in range(2):
                turned("x1", 3, j)
            for j in range(2):
                act.wait_ge(pe_block, BLOCK["wt", j])
                A(wcT[:, j * HALF:(j + 1) * HALF], psum[bank_of(("wt", j))][:, :], ACT.Copy).then_inc(wct_copied, 1)
            for j in range(2):
                act.wait_ge(pe_block, BLOCK["rw", j])
                A(rwB[:, j * HALF:(j + 1) * HALF], psum[bank_of(("rw", j))][:, :], ACT.Copy).then_inc(rw_copied, 1)

            def gate_out(c, t):
                n = 4 * c + t
                act.wait_ge(pe_block, BLOCK["T", "gate", c, 1, t])
                if n:
                    act.wait_ge(gate_mult, n)
                else:
                    act.wait_ge(zc_gated, 4)
                A(th[:, :], psum[t + 4 * c][:, :], ACT.Tanh, scale=0.5).then_inc(gate_tanh, 1)

            def square_x2(t, c=1):
                act.wait_ge(x2_ready, T * c + t + 1)
                square("x2", t, c, resid[:, t, c * HALF:(c + 1) * HALF])

            for t in range(T):
                gate_out(0, t)
                if t:
                    square_x2(t - 1, 0)
            square_x2(3, 0)
            def turned_h(t):
                for j in range(2):
                    turned("h", t, j)

            gate_out(1, 0)
            gate_out(1, 1)
            square_x2(0)
            gate_out(1, 2)
            square_x2(1)
            turned_h(0)
            gate_out(1, 3)
            square_x2(2)
            turned_h(1)
            square_x2(3)
            turned_h(2)
            turned_h(3)

            def ln_square(t):
                act.wait_ge(mu_step, 2 * (t + 1))
                if t:
                    act.wait_ge(squared["ln"], t)
                A(tok[:, :, :].rearrange("p a b -> p (a b)"), big[:, t, :], ACT.Square,
                  bias=nmu[:, 1, t:t + 1], accum_out=ss[:, NORMS["ln"], t, 0:1]).then_inc(squared["ln"], 1)

            for c in range(4):
                for t in range(T):
                    b = ("T", "v4", c, 1, t)
                    act.wait_ge(pe_block, BLOCK[b])
                    A(big[:, t, c * HALF:(c + 1) * HALF], psum[bank_of(b)][:, :], ACT.Gelu_apprx_tanh,
                      accum_out=vsum[:, t, c:c + 1]).then_inc(v_gelu, 1)
            for t in range(T):
                ln_square(t)

            def z4_out(f):
                act.wait_ge(pe_block, BLOCK["F", "z4", f])
                act.wait_ge(z4_gated, f) if f else act.wait_ge(gate_mult, 8)
                A(th[:, :], psum[bank_of(("F", "z4", f))][:, :], ACT.Tanh, scale=0.5).then_inc(z4_tanh, 1)

            def u4_out(f):
                act.wait_ge(pe_block, BLOCK["F", "u4", f])
                if f >= 2:
                    act.wait_ge(zu_made, f - 1)
                A(gcv[:, f % 2, 0:S], psum[bank_of(("F", "u4", f))][:, :], ACT.Gelu_apprx_tanh)\
                    .then_inc(u4_gelu, 1)

            def a_out(c, t):
                act.wait_ge(part_added, 4 * c + t + 1)
                square("a", t, c, part_(t, c))

            def h3_out(t):
                for c in range(2):
                    act.wait_ge(h3_ready, 2 * t + c + 1)
                    square("h3", t, c, resid[:, t, c * HALF:(c + 1) * HALF])

            for half in range(2):
                for j in range(4 * half, 4 * half + 4):
                    for f in range(2):
                        z4_out(2 * j + f)
                    for f in range(2):
                        u4_out(2 * j + f)
                    for f in (2 * j, 2 * j + 1):
                        act.wait_ge(y4_made, f + 1)
                        A(actA_hi[:, f % KD, :], acc[:, f % 2, :], ACT.Copy).then_inc(hi["y4"], 1)
                if half == 0:
                    for c in range(2):
                        for t in range(T):
                            act.wait_ge(pe_block, BLOCK["T", "a0", c, 1, t])
                            A(part_(t, c), psum[t + 4 * c][:, :], ACT.Copy).then_inc(part_copied, 1)

            def k5_out(j):
                act.wait_ge(pe_block, BLOCK["F", "k5", j])
                bank = psum[bank_of(("F", "k5", j))]
                for g in range(2):
                    for half in range(2):
                        A(khi(2 * j + g)[half * DH:(half + 1) * DH, :], bank[g * DH:(g + 1) * DH, :],
                          ACT.Copy).then_inc(k5_hi, 1)

            def q5_out(f):
                act.wait_ge(pe_block, BLOCK["F", "q5", f])
                if f >= 4:
                    act.wait_ge(pe_block, BLOCK["s5", 4 * (f // 2) - 5, 1])
                for m in range(2):
                    rows = slice(m * DH, (m + 1) * DH)
                    A(q5(f, m)[rows, :], psum[bank_of(("F", "q5", f))][rows, :], ACT.Copy, scale=DH ** -0.5)\
                        .then_inc(q5_hi, 1)

            def turned_n(t):
                for j in range(2):
                    turned("n", t, j)

            def v5_out(t):
                act.wait_ge(pe_block, BLOCK["v5", t])
                A(v5(t, 0), psum[bank_of(("v5", t))][:, 0:256], ACT.Copy).then_inc(v5_hi, 1)

            for t in range(T):
                a_out(0, t)
            a_out(1, 0)
            h3_out(0)
            a_out(1, 1)
            h3_out(1)
            turned_n(0)
            a_out(1, 2)
            turned_n(1)
            h3_out(2)
            a_out(1, 3)
            v5_out(0)
            h3_out(3)
            v5_out(1)
            turned_n(2)
            turned_n(3)
            v5_out(2)
            v5_out(3)
            for j in range(2):
                k5_out(j)
            A(lams[:, 6:7], lams[:, 2:3], ACT.Exp)
            for f in range(2):
                q5_out(f)
            for i in range(SLOTS2 + 2):
                for s, f in DONE2.get(i - 1, ()):
                    if s == "q5":
                        q5_out(f)
                    else:
                        act.wait_ge(pe_block, BLOCK["F", s, f])
                        act.wait_ge(z5_gated, f) if f else act.wait_ge(z4_gated, KA)
                        A(th[:, :], psum[bank_of(("F", s, f))][:, :], ACT.Tanh, scale=0.5).then_inc(z5_tanh, 1)
                for kt in ((0, 1) if STEPS2[i - 1][1] else (1,)) if 1 <= i < 17 else ():
                    b = ("t5", i - 1, kt)
                    act.wait_ge(pe_block, BLOCK[b])
                    A(pThi(kt), psum[bank_of(b)][:, :], ACT.Copy).then_inc(pt_hi[kt], 1)
                if 2 <= i < 18:
                    g, b = STEPS2[i - 2]
                    act.wait_ge(pe_block, BLOCK["o5", i - 2])
                    for m in range(2):
                        A(o5[m * DH:(m + 1) * DH, 2 * g:2 * g + 2, b * P:(b + 1) * P],
                          psum[3][0:DH, :].rearrange("p (f m s) -> p m f s", f=2, m=2)[:, m], ACT.Copy)\
                            .then_inc(o5_copied, 1)
                if i < 16:
                    g, b = STEPS2[i]
                    k0 = 0 if b else P
                    act.wait_ge(sink5, i + 1)
                    for h in range(4):
                        pr = prob2(i)[:, h, k0:256]
                        A(pr, pr, ACT.Exp, bias=nmx[:, h:h + 1], accum_out=rs[:, h:h + 1]).then_inc(exp5, 1)
                    A(esk[:, :], den[:, :], ACT.Exp).then_inc(exp5, 1)
                for f in (f for f in MEET2 if MEET2[f] == i):
                    act.wait_ge(y5_made, f + 1)
                    A(actA_hi[:, f, :], acc[:, f % 2, :], ACT.Copy).then_inc(hi["y5"], 1)
            for c in range(2):
                for t in range(T):
                    act.wait_ge(pe_block, BLOCK["T", "f", c, 1, t])
                    square("f", t, c, psum[t + 4 * c][:, :])

        @block.vector
        def _(dve):
            V = nc.vector

            def rest(name, t, j):
                b = ("tr", name, t, j)
                n = 2 * t + j if name != "p" else j
                dve.wait_ge(hi[name], n + 1)
                bank = psum[bank_of(b)][:, :]
                H, L = ACTS[name]
                if name == "p":
                    V.tensor_tensor(L[:, j, :], bank, H[:, j, :].bitcast(f32), ALU.subtract).then_inc(lo[name], 1)
                else:
                    at = (slice(None), slice(4 * j, 4 * j + 4), slice(t * P, (t + 1) * P))
                    V.tensor_tensor(L[at], bank.rearrange("p (k c) -> p k c", k=4), H[at].bitcast(f32),
                                    ALU.subtract).then_inc(lo[name], 1)

            def normed(name, norm, t, g, turn):
                dve.wait_ge(rstd_ready[norm], t + 1)
                if t >= 2:
                    dve.wait_ge(pe_block, BLOCK["tr", turn, t - 2, 1])
                r = rstd[:, NORMS[norm], t:t + 1]
                if g is None:
                    ins = V.tensor_scalar(tok[:, t % 2], resid[:, t], r, None, ALU.mult)
                else:
                    ins = V.scalar_tensor_tensor(tok[:, t % 2], resid[:, t], r, gain[:, g], ALU.mult, ALU.mult)
                ins.then_inc(tok_ready[turn], 1)

            V.memset(gcv[:, :, 0:2], 0.0).then_inc(pads_made, 1)
            dve.wait_ge(iota_made, 1)
            V.tensor_copy(base1, iot).then_inc(base_step, 1)
            dve.wait_ge(base_step, 1)
            V.scalar_tensor_tensor(base1, base1, -1.0, base1, ALU.mult, ALU.max).then_inc(base_step, 1)
            dve.wait_ge(base_step, 2)
            V.memset(base1[0:64, HALF - 64:HALF], MASKED).then_inc(base_step, 1)
            dve.wait_ge(pre_in, 16)
            normed("x", "x", 0, 0, "x")
            for j in range(2):
                rest("x", 0, j)
            normed("x", "x", 1, 0, "x")
            for t in range(1, T):
                if t + 1 < T:
                    normed("x", "x", t + 1, 0, "x")
                for j in range(2):
                    rest("x", t, j)
            dve.wait_ge(small_in, 16 * 13)
            for n in range(2):
                V.tensor_tensor_reduce(lamv[:, 2 * n], lamv[:, 2 * n], lamv[:, 2 * n + 1], 1.0, 0.0,
                                       ALU.mult, ALU.add, lams[:, n:n + 1]).then_inc(lam_step, 1)
            dve.wait_ge(lam_exp, 1)
            V.tensor_tensor(lams[:, 4:5], lams[:, 3:4], lams[:, 2:3], ALU.subtract).then_inc(lam_step, 1)
            dve.wait_ge(lam_step, 3)
            V.tensor_scalar(lams[:, 5:6], lams[:, 4:5], -LAM_INIT, None, ALU.add).then_inc(lam_step, 1)
            V.tensor_scalar(subg[:, 1:2], subg[:, 0:1], 0.5 * (1.0 - LAM_INIT), None, ALU.mult).then_inc(cols_scaled, 1)
            V.tensor_scalar(convc[:, :, :], convc[:, :, :], 0.5, None, ALU.mult).then_inc(cols_scaled, 1)
            V.tensor_scalar(lng[:, :], lng[:, :], 0.5, None, ALU.mult).then_inc(cols_scaled, 1)
            V.tensor_scalar(lnb[:, :], lnb[:, :], 0.5, None, ALU.mult).then_inc(cols_scaled, 1)
            dve.wait_ge(base_step, 3)

            dve.wait_ge(tok_ready["x"], T)
            for f in range(NH1):
                for m in range(2):
                    own = slice(m * DQK1, (m + 1) * DQK1)
                    other = slice((1 - m) * DQK1, (2 - m) * DQK1)
                    dve.wait_ge(q1_hi, 2 * f + m + 1)
                    V.scalar_tensor_tensor(q1(f, m)[other, :], psum[bank_of(("F", "q", f))][own, :], DQK1 ** -0.5,
                                           q1(f, m)[own, :].bitcast(f32), ALU.mult, ALU.subtract).then_inc(q1_lo, 1)
            for f in range(NH1):
                for m in range(2):
                    own = slice(m * DQK1, (m + 1) * DQK1)
                    dve.wait_ge(k1_hi, 4 * f + 2 * m + 2)
                    V.tensor_tensor(k1_rest(f)[own, :], psum[bank_of(("F", "k", f))][own, :],
                                    k1(f, m)[own, :].bitcast(f32), ALU.subtract).then_inc(k1_lo, 1)

            def job_in(i):
                s, f = JOBS1[i]
                bank = psum[bank_of(("F", s, f))][:, :]
                g0 = gcv[:, f % 2, :]
                if s == "za":
                    dve.wait_ge(za_tanh, f + 1)
                    V.scalar_tensor_tensor(tile(zaT, f), th[:, :], 1.0, bank, ALU.add, ALU.mult)\
                        .then_inc(za_gated, 1)
                if s == "u":
                    dve.wait_ge(c_copied, f + 1)
                    dve.wait_ge(pe_block, BLOCK["F", s, f])
                    V.tensor_tensor(g0[:, 2:2 + S], bank, g0[:, 2:2 + S], ALU.mult).then_inc(g_made, 1)
                if s == "b":
                    a = acc[:, f % 2, :]
                    dve.wait_ge(cols_scaled, 2)
                    dve.wait_ge(g_made, f + 1)
                    if f >= 2:
                        dve.wait_ge(lo["conv"], f - 1)
                    V.tensor_scalar(a, g0[:, 0:S], convc[:, 0, f:f + 1], None, ALU.mult).then_inc(taps, 1)
                    for j in (1, 2):
                        dve.wait_ge(taps, 3 * f + j)
                        V.scalar_tensor_tensor(a, g0[:, j:j + S], convc[:, j, f:f + 1], a, ALU.mult, ALU.add)\
                            .then_inc(taps, 1)
                    dve.wait_ge(taps, 3 * f + 3)
                    dve.wait_ge(pe_block, BLOCK["F", s, f])
                    V.tensor_tensor(a, bank, a, ALU.mult).then_inc(b_mult, 1)
                if s == "zc":
                    dve.wait_ge(zc_tanh, f + 1)
                    V.scalar_tensor_tensor(g0[:, 2:2 + S], th[:, :], 1.0, bank, ALU.add, ALU.mult)\
                        .then_inc(zc_gated, 1)
                    dve.wait_ge(zc_gated, f + 1)
                    dve.wait_ge(b_mult, f + 1)
                    V.tensor_tensor(acc[:, f % 2, :], acc[:, f % 2, :], g0[:, 2:2 + S], ALU.mult)\
                        .then_inc(conv_out, 1)

            def conv_lo(i):
                s, f = JOBS1[i]
                if s == "zc":
                    dve.wait_ge(hi["conv"], f + 1)
                    V.tensor_tensor(actB_lo[:, 4 + f, :], acc[:, f % 2, :], actB_hi[:, 4 + f, :].bitcast(f32),
                                    ALU.subtract).then_inc(lo["conv"], 1)

            def scores(i):
                h, qt = STEPS1[i]
                n = (qt + 1) * P
                if qt == 0:
                    V.tensor_scalar(bias1(h), base1, -SLOPE1[h], None, ALU.mult).then_inc(bias_made, 1)
                    dve.wait_ge(bias_made, h + 1)
                for m in range(2):
                    b = ("sc", i, m)
                    dve.wait_ge(pe_block, BLOCK[b])
                    V.tensor_tensor_reduce(prob1(m)[:, 0:n], psum[bank_of(b)][:, 0:n], bias1(h)[:, HALF - n:HALF],
                                           1.0, -3e38, ALU.add, ALU.max, mx[:, m:m + 1]).then_inc(scored, 1)
                dve.wait_ge(scored, 2 * i + 2)
                V.tensor_scalar(nmx[:, 0:2], mx[:, 0:2], -1.0, None, ALU.mult).then_inc(negmax, 1)

            def weights(i):
                h, qt = STEPS1[i]
                n = (qt + 1) * P
                dve.wait_ge(exped, 2 * i + 2)
                V.reciprocal(rr[:, 0:2], rs[:, 0:2]).then_inc(recip1, 1)
                dve.wait_ge(recip1, i + 1)
                dve.wait_ge(lam_step, 4)
                V.tensor_scalar(prob1(1)[:, 0:n], prob1(1)[:, 0:n], rr[:, 1:2], lams[:, 5:6], ALU.mult, ALU.mult)\
                    .then_inc(lam_scaled, 1)
                dve.wait_ge(lam_scaled, i + 1)
                if i:
                    dve.wait_ge(pe_block, BLOCK["tw", i - 1])
                V.scalar_tensor_tensor(wgt1[:, 0:n], prob1(0)[:, 0:n], rr[:, 0:1], prob1(1)[:, 0:n],
                                       ALU.mult, ALU.add).then_inc(weighed, 1)

            for i in range(SLOTS1 + 2):
                if i >= 7 and i % 4 == 3:
                    h = i // 4 - 1
                    dve.wait_ge(cols_scaled, 1)
                    dve.wait_ge(pe_block, BLOCK["ta", h])
                    V.scalar_tensor_tensor(tile(kT, h), psum[bank_of(("ta", h))][:, :], subg[:, 1:2], tile(zaT, h),
                                           ALU.mult, ALU.mult).then_inc(attn_out, 1)
                if i < 16:
                    scores(i)
                if 1 <= i <= SLOTS1:
                    job_in(i - 1)
                if 2 <= i:
                    conv_lo(i - 2)
                if i < 16:
                    weights(i)
                if i >= 6 and i % 4 == 2:
                    h = i // 4 - 1
                    a = tile(qT, h).rearrange("p (t c) -> p t c", t=T)
                    dve.wait_ge(rstd_attn, h + 1)
                    dve.wait_ge(attn_copied, h + 1)
                    V.tensor_tensor(a, a, r_attn[:, h, :].unsqueeze(2).to_broadcast([P, T, P]), ALU.mult)\
                        .then_inc(attn_normed, 1)
                if i >= 7 and i % 4 == 3:
                    h = i // 4 - 1
                    dve.wait_ge(hi["attn"], h + 1)
                    V.tensor_tensor(actB_lo[:, h, :], tile(kT, h), actB_hi[:, h, :].bitcast(f32),
                                    ALU.subtract).then_inc(lo["attn"], 1)

            def post(name, done, t, g, ready):
                dve.wait_ge(rstd_ready[name], t + 1)
                if t:
                    dve.wait_ge(ready, t)
                for c in range(2):
                    V.scalar_tensor_tensor(acc[:, c, :], psum[t + 4 * c][:, :], rstd[:, NORMS[name], t:t + 1],
                                           gain[:, g, c * HALF:(c + 1) * HALF], ALU.mult, ALU.mult)\
                        .then_inc(done, 1)
                dve.wait_ge(done, 2 * t + 2)
                V.tensor_tensor(resid[:, t], resid[:, t], acc[:, :, :].rearrange("p a b -> p (a b)"), ALU.add)\
                    .then_inc(ready, 1)

            for k in range(2):
                rest("p", 0, k)
            dve.wait_ge(post_in, 16)
            for t in range(T):
                post("m1", post_scaled, t, 1, x1_ready)
                if t == 2:
                    for j in range(2):
                        rest("x1", 0, j)
            for t in range(1, T):
                for j in range(2):
                    rest("x1", t, j)
            dve.wait_ge(ple_in, 16)
            for t in range(T):
                dve.wait_ge(rstd_ready["e"], t + 1)
                dve.wait_ge(e_copied, 2 * t + 2)
                V.scalar_tensor_tensor(e_sb(t), e_sb(t), rstd[:, NORMS["e"], t:t + 1], gain[:, 2], ALU.mult,
                                       ALU.mult).then_inc(e_normed, 1)

            def gate_in(c, t):
                n = 4 * c + t
                half = slice(c * HALF, (c + 1) * HALF)
                dve.wait_ge(gate_tanh, n + 1)
                dve.wait_ge(e_normed, t + 1)
                if n:
                    dve.wait_ge(x2_ready, n)
                V.scalar_tensor_tensor(acc[:, 0, :], th[:, :], 1.0, e_sb(t)[:, half], ALU.add, ALU.mult)\
                    .then_inc(gate_mult, 1)
                dve.wait_ge(gate_mult, n + 1)
                V.scalar_tensor_tensor(resid[:, t, half], acc[:, 0, :], 0.5, resid[:, t, half], ALU.mult,
                                       ALU.add).then_inc(x2_ready, 1)

            for t in range(T):
                gate_in(0, t)

            def rest_h(t):
                for j in range(2):
                    rest("h", t, j)

            gate_in(1, 0)
            gate_in(1, 1)
            dve.wait_ge(apre_in, 16)
            normed("h", "x2", 0, 0, "h")
            gate_in(1, 2)
            normed("h", "x2", 1, 0, "h")
            rest_h(0)
            gate_in(1, 3)
            rest_h(1)
            normed("h", "x2", 2, 0, "h")
            rest_h(2)
            normed("h", "x2", 3, 0, "h")
            rest_h(3)
            dve.wait_ge(bs_in, 16)
            V.tensor_scalar(bsB[:, :], bsB[:, :], 0.5, None, ALU.mult).then_inc(cols_scaled, 1)
            for t in range(T):
                dve.wait_ge(v_gelu, 12 + t + 1)
                V.tensor_reduce(nmu[:, 0, t:t + 1], vsum[:, t, :], AX.X, ALU.add).then_inc(mu_step, 1)
                dve.wait_ge(mu_step, 2 * t + 1)
                V.tensor_scalar(nmu[:, 1, t:t + 1], nmu[:, 0, t:t + 1], -1.0 / AW, None, ALU.mult).then_inc(mu_step, 1)

            def z4_in(f):
                dve.wait_ge(z4_tanh, f + 1)
                if f >= 2:
                    dve.wait_ge(lo["y4"], f - 1)
                V.scalar_tensor_tensor(acc[:, f % 2, :], th[:, :], 1.0, psum[bank_of(("F", "z4", f))][:, :],
                                       ALU.add, ALU.mult).then_inc(z4_gated, 1)

            def u4_in(f):
                dve.wait_ge(u4_gelu, f + 1)
                dve.wait_ge(z4_gated, f + 1)
                V.tensor_tensor(acc[:, f % 2, :], acc[:, f % 2, :], gcv[:, f % 2, 0:S], ALU.mult).then_inc(zu_made, 1)

            def s4_in(f):
                g = f // 2
                bias = tok[:, f % 2, HALF:HALF + P]
                s = tok[:, f % 2, 0:HALF]
                dve.wait_ge(cols_scaled, 5)
                dve.wait_ge(rw_copied, 2)
                if f >= 2:
                    dve.wait_ge(s4_scaled, f - 1)
                V.scalar_tensor_tensor(bias, rwB[:, g * P:(g + 1) * P], lnb[:, f:f + 1], bsB[:, g * P:(g + 1) * P],
                                       ALU.mult, ALU.add).then_inc(s4_bias, 1)
                dve.wait_ge(s4_bias, f + 1)
                b = ("s4", f)
                dve.wait_ge(pe_block, BLOCK[b])
                if f >= 2:
                    dve.wait_ge(y4_made, f - 1)
                V.scalar_tensor_tensor(s.rearrange("p (t c) -> p t c", t=T),
                                       psum[bank_of(b)][:, :].rearrange("p (t c) -> p t c", t=T), lng[:, f:f + 1],
                                       bias.unsqueeze(1).to_broadcast([P, T, P]), ALU.mult, ALU.add)\
                    .then_inc(s4_scaled, 1)
                dve.wait_ge(s4_scaled, f + 1)
                dve.wait_ge(zu_made, f + 1)
                V.tensor_tensor(acc[:, f % 2, :], acc[:, f % 2, :], s, ALU.mult).then_inc(y4_made, 1)

            for half in range(2):
                for j in range(4 * half, 4 * half + 4):
                    for f in range(2):
                        z4_in(2 * j + f)
                        if j == 0:
                            for t in (2 * f, 2 * f + 1):
                                dve.wait_ge(rstd_ready["ln"], t + 1)
                                V.tensor_scalar(big[:, t, :], big[:, t, :], nmu[:, 1, t:t + 1],
                                                rstd[:, NORMS["ln"], t:t + 1], ALU.add, ALU.mult)\
                                    .then_inc(v_normed, 1)
                    for f in range(2):
                        u4_in(2 * j + f)
                    for f in (2 * j, 2 * j + 1):
                        s4_in(f)
                    for f in (2 * j, 2 * j + 1):
                        dve.wait_ge(hi["y4"], f + 1)
                        V.tensor_tensor(actA_lo[:, f % KD, :], acc[:, f % 2, :], actA_hi[:, f % KD, :].bitcast(f32),
                                        ALU.subtract).then_inc(lo["y4"], 1)

            def part_in(c, t):
                dve.wait_ge(pe_block, BLOCK["T", "a1", c, 1, t])
                dve.wait_ge(part_copied, 4 * c + t + 1)
                V.tensor_tensor(part_(t, c), psum[t + 4 * c][:, :], part_(t, c), ALU.add).then_inc(part_added, 1)

            def gained(c, t):
                return big[:, t, 0:HALF] if c == 0 else big[:, t, D:D + HALF]

            def part_gain(c, t):
                if c == 0:
                    dve.wait_ge(squared["a"], t + 1)
                dve.wait_ge(part_added, 4 * c + t + 1)
                V.tensor_tensor(gained(c, t), part_(t, c), gain[:, 2, c * HALF:(c + 1) * HALF], ALU.mult)\
                    .then_inc(a_gained, 1)

            def h3_in(t):
                dve.wait_ge(rstd_ready["a"], t + 1)
                dve.wait_ge(a_gained, 4 + t + 1)
                for c in range(2):
                    half = slice(c * HALF, (c + 1) * HALF)
                    V.scalar_tensor_tensor(resid[:, t, half], gained(c, t), rstd[:, NORMS["a"], t:t + 1],
                                           resid[:, t, half], ALU.mult, ALU.add).then_inc(h3_ready, 1)

            def rest_n(t):
                for j in range(2):
                    rest("n", t, j)

            def v5_rest(t):
                dve.wait_ge(v5_hi, t + 1)
                V.tensor_tensor(v5(t, 1), psum[bank_of(("v5", t))][:, 0:256], v5(t, 0).bitcast(f32), ALU.subtract)\
                    .then_inc(v5_lo, 1)

            def scale_rows(j):
                n = 2 * UNIT_NO["v5", 0] + j
                g = kvg if j < 4 else bg
                dve.wait_ge(raw_in[n % 4], 16 * (n // 4 + 1))
                for k in range(4):
                    w = raw[:, n % 4, k * 256:(k + 1) * 256]
                    V.tensor_scalar(w, w, g[:, 4 * (n % 2) + k:4 * (n % 2) + k + 1], None, ALU.mult)\
                        .then_inc(dve_scaled, 1)

            dve.wait_ge(apost_in, 16)
            for t in range(T):
                part_in(0, t)
                if t:
                    part_gain(0, t - 1)
            part_gain(0, 3)
            scale_rows(0)
            scale_rows(1)
            part_in(1, 0)
            part_gain(1, 0)
            h3_in(0)
            part_in(1, 1)
            normed("n", "h3", 0, None, "n")
            part_gain(1, 1)
            h3_in(1)
            scale_rows(2)
            normed("n", "h3", 1, None, "n")
            rest_n(0)
            scale_rows(3)
            part_in(1, 2)
            part_gain(1, 2)
            rest_n(1)
            h3_in(2)
            part_in(1, 3)
            part_gain(1, 3)
            normed("n", "h3", 2, None, "n")
            h3_in(3)
            v5_rest(0)
            v5_rest(1)
            rest_n(2)
            normed("n", "h3", 3, None, "n")
            scale_rows(4)
            scale_rows(5)
            rest_n(3)
            scale_rows(6)
            scale_rows(7)
            v5_rest(2)
            v5_rest(3)

            def scores2(i):
                g, b = STEPS2[i]
                k0 = 0 if b else P
                if b == 0:
                    dve.wait_ge(pe_block, BLOCK["v5", T - 1])
                    for h in range(4):
                        V.tensor_scalar(bias2(g)[:, h, :], dist2, -SLOPE2[4 * g + h], None, ALU.mult)\
                            .then_inc(bias2_made, 1)
                    dve.wait_ge(bias2_made, 4 * g + 4)
                if i >= 2:
                    dve.wait_ge(pe_block, BLOCK["t5", i - 2, 1])
                for h in (0, 2, 1, 3):
                    blk = ("s5", i, h % 2)
                    dve.wait_ge(pe_block, BLOCK[blk])
                    src = psum[bank_of(blk)][:, (h // 2) * 256 + k0:(h // 2) * 256 + 256]
                    V.tensor_tensor_reduce(prob2(i)[:, h, k0:256], src, bias2(g)[:, h, k0:256], 1.0,
                                           sinks[:, 4 * g + h:4 * g + h + 1], ALU.add, ALU.max, mx[:, h:h + 1])\
                        .then_inc(s5_scored, 1)
                dve.wait_ge(s5_scored, 4 * i + 4)
                V.tensor_scalar(nmx[:, :], mx[:, :], -1.0, None, ALU.mult).then_inc(neg5, 1)
                dve.wait_ge(neg5, i + 1)
                V.tensor_tensor(den[:, :], sinks[:, 4 * g:4 * g + 4], nmx[:, :], ALU.add).then_inc(sink5, 1)

            def probs2(i):
                g, b = STEPS2[i]
                k0 = 0 if b else P
                dve.wait_ge(exp5, 5 * i + 5)
                V.tensor_tensor(den[:, :], rs[:, :], esk[:, :], ALU.add).then_inc(den5, 1)
                dve.wait_ge(den5, i + 1)
                V.reciprocal(rr[:, :], den[:, :]).then_inc(rec5, 1)
                dve.wait_ge(rec5, i + 1)
                for h in range(4):
                    pr = prob2(i)[:, h, k0:256]
                    V.tensor_scalar(pr, pr, rr[:, h:h + 1], None, ALU.mult).then_inc(prob5, 1)

            dve.wait_ge(a_gained, 8)
            dve.wait_ge(tok_ready["h"], T)
            for j in range(2):
                bank = psum[bank_of(("F", "k5", j))]
                for g in range(2):
                    dve.wait_ge(k5_hi, 4 * j + 2 * g + 2)
                    own = slice(g * DH, (g + 1) * DH)
                    for half in range(2):
                        V.tensor_tensor(klo(2 * j + g)[half * DH:(half + 1) * DH, :], bank[own, :],
                                        khi(2 * j + g)[own, :].bitcast(f32), ALU.subtract).then_inc(k5_lo, 1)

            def q5_rest(f):
                for m in range(2):
                    own, other = slice(m * DH, (m + 1) * DH), slice((1 - m) * DH, (2 - m) * DH)
                    dve.wait_ge(q5_hi, 2 * f + m + 1)
                    V.scalar_tensor_tensor(q5(f, m)[other, :], psum[bank_of(("F", "q5", f))][own, :], DH ** -0.5,
                                           q5(f, m)[own, :].bitcast(f32), ALU.mult, ALU.subtract).then_inc(q5_lo, 1)

            q5_rest(0)
            q5_rest(1)
            dve.wait_ge(dist_made, 4)
            for i in range(SLOTS2 + 2):
                if i < 16:
                    scores2(i)
                for kt in ((0, 1) if STEPS2[i - 1][1] else (1,)) if 1 <= i < 17 else ():
                    dve.wait_ge(pt_hi[kt], i if kt else kt0_steps(i - 1))
                    V.tensor_tensor(pTlo(kt), psum[bank_of(("t5", i - 1, kt))][:, :], pThi(kt).bitcast(f32),
                                    ALU.subtract).then_inc(pt_lo[kt], 1)
                if i < 16:
                    probs2(i)
                for f in (f for s, f in DONE2.get(i - 1, ()) if s == "q5"):
                    q5_rest(f)
                for f in (f for s, f in DONE2.get(i - 1, ()) if s == "z5"):
                    dve.wait_ge(z5_tanh, f + 1)
                    V.scalar_tensor_tensor(zg[:, f, :], th[:, :], 1.0, psum[bank_of(("F", "z5", f))][:, :], ALU.add,
                                           ALU.mult).then_inc(z5_gated, 1)
                for f in (f for f in MEET2 if MEET2[f] == i - 1):
                    dve.wait_ge(hi["y5"], f + 1)
                    V.tensor_tensor(actA_lo[:, f, :], acc[:, f % 2, :], actA_hi[:, f, :].bitcast(f32),
                                    ALU.subtract).then_inc(lo["y5"], 1)
                for f in (f for f in MEET2 if MEET2[f] == i):
                    if f >= 2:
                        dve.wait_ge(lo["y5"], f - 1)
                    dve.wait_ge(z5_gated, f + 1)
                    dve.wait_ge(o5_copied, 8 * (f // 2 + 1))
                    V.scalar_tensor_tensor(acc[:, f % 2, :], zg[:, f, :], 0.5, o5[:, f, :], ALU.mult, ALU.mult)\
                        .then_inc(y5_made, 1)
            dve.wait_ge(bpost_in, 16)

            def f_gain(c, t):
                dve.wait_ge(squared["f"], T * c + t + 1)
                V.tensor_tensor(part_(t, c), psum[t + 4 * c][:, :], gain[:, 1, c * HALF:(c + 1) * HALF], ALU.mult)\
                    .then_inc(f_gained, 1)

            for t in range(T):
                f_gain(0, t)
            for t in range(T):
                f_gain(1, t)
                dve.wait_ge(rstd_ready["f"], t + 1)
                dve.wait_ge(f_gained, T + t + 1)
                for c in range(2):
                    half = slice(c * HALF, (c + 1) * HALF)
                    V.scalar_tensor_tensor(resid[:, t, half], part_(t, c), rstd[:, NORMS["f"], t:t + 1],
                                           resid[:, t, half], ALU.mult, ALU.add).then_inc(out_ready, 1)

        @block.tensor
        def _(pe):
            M = nc.tensor.matmul

            def exact(out_, whi_, wlo_, xhi_, xlo_, start, stop):
                M(out_, whi_, xhi_, start=start, stop=False)
                M(out_, whi_, xlo_, start=False, stop=False)
                return M(out_, wlo_, xhi_, start=False, stop=stop)

            def weights_of(stage, j, first_half=False):
                n = UNIT_NO[stage, j]
                pe.wait_ge(w_lo, 2 * n + (1 if first_half else 2))
                return whi[:, SLOT[n], :], wlo[:, SLOT[n], :]

            def feature_major(kind, stage, f):
                H, L = weights_of(stage, f // 2)
                aH, aL = READS[stage]
                tokens = slice(0, S)
                if stage == "k5":
                    tokens = slice(0, S // 2) if kind == "Fa" else slice(S // 2, S)
                aH, aL = aH[:, :, tokens], aL[:, :, tokens]
                out_ = psum[bank_of(("F", stage, f))][:, tokens]
                first, last = (0, KD // 2) if kind == "Fk" else (KD // 2 * ((stage, f) in JOBS2), KD)
                for k in range(first, last):
                    c = slice(k * 256 + (f % 2) * P, k * 256 + (f % 2) * P + P)
                    ins = exact(out_, H[:, c], L[:, c], aH[:, k, :], aL[:, k, :], k == 0, k == KD - 1)
                return ins

            def token_major(stage, c, kh, t, head=False):
                first = HEADS.get((stage, c, kh, t), 0)
                H, L = weights_of(stage, 2 * c + kh, head and first <= 2)
                aH, aL = READS[stage]
                bank = bank_of(("T", stage, c, kh, t))
                rows = slice(t * P, (t + 1) * P)
                for k in range(first) if head else range(first, 4):
                    w = slice(k * HALF, (k + 1) * HALF)
                    a = 4 * kh + k
                    ins = exact(psum[bank][:, :], aH[:, a, rows], aL[:, a, rows], H[:, w], L[:, w],
                                kh == 0 and k == 0, kh == 1 and k == 3)
                return ins

            def turn(name, t, j):
                bank = psum[bank_of(("tr", name, t, j))]
                for k in range(4):
                    if name == "p":
                        src = ptok[:, k * PLE + j * P:k * PLE + (j + 1) * P]
                    elif name == "x1":
                        src = resid[:, t, (4 * j + k) * P:(4 * j + k + 1) * P]
                    else:
                        src = tok[:, t % 2, (4 * j + k) * P:(4 * j + k + 1) * P]
                    ins = nc.tensor.transpose(bank[:, k * P:(k + 1) * P], src, ident[:, :])
                return ins

            def ready(b):
                kind = b[0]
                if kind == "tr":
                    name, t, j = b[1:]
                    if name == "p":
                        pe.wait_ge(p_in, 16)
                    elif name == "x1":
                        pe.wait_ge(x1_ready, t + 1)
                    else:
                        pe.wait_ge(tok_ready[name], t + 1)
                    return
                s = b[1]
                if kind in ("F", "Fa"):
                    if s == "q":
                        pe.wait_ge(lo["x"], 2 * T)
                    if s == "k5":
                        pe.wait_ge(lo["n"], T if kind == "Fa" else 2 * T)
                if kind in ("T", "Th"):
                    c, kh, t = b[2:]
                    if s == "v":
                        pe.wait_ge(lo["x"], 2 * t + 1 + kh)
                    if s == "wo":
                        pe.wait_ge(*((lo["attn"], NH1 - (kind == "Th")) if kh == 0 else (lo["conv"], 4)))
                    if s in ("gate", "v4"):
                        pe.wait_ge(lo["x1" if s == "gate" else "h"], 2 * t + 1 + kh)
                    if s in ("a0", "a1"):
                        pe.wait_ge(lo["y4"], KD * int(s[1]) + 4 * (kh + 1))
                    if s == "f":
                        pe.wait_ge(lo["y5"], 4 * (kh + 1))
                if kind == "ple":
                    pe.wait_ge(lo["p"], 2)
                if kind == "v5":
                    pe.wait_ge(lo["n"], 2 * (s + 1))
                if kind == "sc":
                    pe.wait_ge(q1_lo, 2 * (s // 4) + 2)
                    pe.wait_ge(k1_lo, 2 * (s // 4) + 2)
                if kind == "tw":
                    pe.wait_ge(weighed, s + 1)
                if kind == "pv":
                    pe.wait_ge(wt_copied, s + 1)
                    if s:
                        pe.wait_ge(attn_sq, s)
                    pe.wait_ge(v_copied, T)
                if kind == "ta":
                    pe.wait_ge(attn_normed, s + 1)
                if kind == "wt":
                    pe.wait_ge(ws_masked, 1)
                if kind == "rw":
                    pe.wait_ge(wct_copied, 2)
                if kind == "s4":
                    pe.wait_ge(v_normed, T)
                if kind == "s5":
                    pe.wait_ge(q5_lo, 4 * (s // 4) + 4)
                    pe.wait_ge(k5_lo, 8)
                if kind == "t5":
                    pe.wait_ge(prob5, 4 * (s + 1))
                if kind == "o5":
                    pe.wait_ge(v5_lo, T)
                    pe.wait_ge(pt_lo[1], s + 1)
                    if STEPS2[s][1]:
                        pe.wait_ge(pt_lo[0], kt0_steps(s))

            def work(b):
                kind = b[0]
                bank = psum[bank_of(b)]
                if kind == "tr":
                    return turn(*b[1:])
                if kind in ("F", "Fa", "Fk"):
                    return feature_major(*b)
                if kind in ("T", "Th"):
                    return token_major(*b[1:], head=kind == "Th")
                if kind == "sc":
                    i, m = b[1:]
                    h, qt = STEPS1[i]
                    rows = slice(m * DQK1, (m + 1) * DQK1)
                    n = (qt + 1) * P
                    q = q1(h, m)[:, qt * P:(qt + 1) * P]
                    M(bank[:, 0:n], q, k1(h, m)[:, 0:n], start=True, stop=False)
                    return M(bank[:, 0:n], q[rows], k1_rest(h)[rows, 0:n], start=False, stop=True)
                if kind == "tw":
                    for k in range(STEPS1[b[1]][1] + 1):
                        c = slice(k * P, (k + 1) * P)
                        ins = nc.tensor.transpose(bank[:, c], wgt1[:, c], ident[:, :])
                    return ins
                if kind == "pv":
                    h, qt = STEPS1[b[1]]
                    for k in range(qt + 1):
                        ins = M(bank[:, qt * P:(qt + 1) * P], wgtT1[:, k * P:(k + 1) * P],
                                tile(vtok, k)[:, h * P:(h + 1) * P], start=k == 0, stop=k == qt)
                    return ins
                if kind == "ta":
                    for k in range(T):
                        c = slice(k * P, (k + 1) * P)
                        ins = nc.tensor.transpose(bank[:, c], tile(qT, b[1])[:, c], ident[:, :])
                    return ins
                if kind == "ple":
                    t, c = b[1:]
                    H, L = weights_of("ple", 0)
                    rows = slice(t * P, (t + 1) * P)
                    for k in range(2):
                        w = slice(k * D + c * HALF, k * D + (c + 1) * HALF)
                        ins = exact(bank[:, :], actA_hi[:, k, rows], actA_lo[:, k, rows], H[:, w], L[:, w],
                                    k == 0, k == 1)
                    return ins
                if kind == "wt":
                    for k in range(4):
                        g = 4 * b[1] + k
                        ins = nc.tensor.transpose(bank[:, k * P:(k + 1) * P], wsr[:, g * P:(g + 1) * P], ident[:, :])
                    return ins
                if kind == "rw":
                    return M(bank[:, :], ones[:, :], wcT[:, b[1] * HALF:(b[1] + 1) * HALF], start=True, stop=True)
                if kind == "s4":
                    f = b[1]
                    for n in range(T):
                        ins = M(bank[:, n * P:(n + 1) * P], big[:, n, f * P:(f + 1) * P],
                                wcT[:, (f // 2) * P:(f // 2 + 1) * P], start=True, stop=True)
                    return ins
                if kind == "v5":
                    t = b[1]
                    n = UNIT_NO["v5", 0]
                    pe.wait_ge(w_lo, 2 * n + 2)
                    rows = slice(t * P, (t + 1) * P)
                    for k in range(KD):
                        H, L = halves_of(n, k // 2)
                        w = slice((k % 2) * 256, (k % 2 + 1) * 256)
                        ins = exact(bank[:, 0:256], actB_hi[:, k, rows], actB_lo[:, k, rows], H[:, w], L[:, w],
                                    k == 0, k == KD - 1)
                    return ins
                if kind == "s5":
                    i, m = b[1:]
                    g, blk = STEPS2[i]
                    k0 = 0 if blk else P
                    keys = slice((blk - 1) * P + k0, (blk + 1) * P)
                    rows = slice(m * DH, (m + 1) * DH)
                    for j in range(2):
                        out_ = bank[:, j * 256 + k0:(j + 1) * 256]
                        q = q5(2 * g + j, m)[:, blk * P:(blk + 1) * P]
                        M(out_, q, khi(g)[:, keys], start=True, stop=False)
                        ins = M(out_, q[rows], klo(g)[rows, keys], start=False, stop=True)
                    return ins
                if kind == "t5":
                    i, kt = b[1:]
                    for h in range(4):
                        ins = nc.tensor.transpose(bank[:, h * P:(h + 1) * P],
                                                  prob2(i)[:, h, kt * P:(kt + 1) * P], ident[:, :])
                    return ins
                if kind == "o5":
                    g, blk = STEPS2[b[1]]
                    kts = (0, 1) if blk else (1,)
                    for kt in kts:
                        vH, vL = (v5(blk - 1 + kt, part)[:, g * DH:(g + 1) * DH] for part in range(2))
                        ins = exact(bank[0:DH, :], vH, vL, pThi(kt), pTlo(kt), kt == kts[0], kt == 1)
                    return ins

            pe.wait_ge(ident_made, 1)
            pe.wait_ge(ones_made, 1)
            for b in ORDER:
                if BEFORE.get(b) is not None:
                    pe.wait_ge(*emptied(BEFORE[b]))
                ready(b)
                work(b).then_inc(pe_block, 1)


_INS = ["x", "p", "pre_norm_gain", "w_in", "lambda_q1", "lambda_k1", "lambda_q2", "lambda_k2",
        "subln_gain", "conv_w", "w_out", "post_norm_gain", "w_ple_proj", "ple_norm_gain", "w_ple_gate",
        "a_w_in_2", "a_ln_g_2", "a_ln_b_2", "a_w_s_2", "a_b_s_2", "a_w_out_2", "a_pre_g_2",
        "a_post_g_2", "kv_norm_g_2", "w_k_2", "w_v_2", "b_w_in_2", "b_sinks_2", "b_w_out_2",
        "b_pre_g_2", "b_post_g_2"]


def kernel(**inputs):
    import numpy as np
    import concourse.bacc as bacc
    from concourse.bass_utils import run_bass_kernel_spmd

    nc = bacc.Bacc("TRN2", target_bir_lowering=False, num_devices=1)
    arrays, args = {}, []
    for name in _INS:
        a = np.ascontiguousarray(inputs[name])
        arrays[f"in_{name}"] = a
        args.append(nc.dram_tensor(f"in_{name}", a.shape, mybir.dt.from_np(a.dtype), kind="ExternalInput").ap())
    args.append(nc.dram_tensor("out_dram", (1, S, D), mybir.dt.float32, kind="ExternalOutput").ap())
    program(nc, *args)
    r = run_bass_kernel_spmd(nc, [arrays], core_ids=[0])
    return r.results[0]["out_dram"]
```
